# Optimizing a Trainium2 kernel written in Bass

```python
import math
import jax, jax.numpy as jnp
from jax import lax
import numpy as np

D_MODEL = 1024
BATCH = 1
SEQ = 512
DEPTH = 1
DEC_BATCH = 8
DEC_SEQ = 16
PAST_LEN = 256

CHUNK = 64
WINDOW = 128
N_BACK = WINDOW // CHUNK
ATTN_WIDTH = D_MODEL // 2
HEAD_DIM = 64
N_HEADS = ATTN_WIDTH // HEAD_DIM
N_KV_HEADS = 2
Q_PER_KV = N_HEADS // N_KV_HEADS
KV_WIDTH = N_KV_HEADS * HEAD_DIM
SSM_WIDTH = D_MODEL - ATTN_WIDTH
SSM_GROUP = 16
SSM_GROUPS = SSM_WIDTH // SSM_GROUP
SSM_STATE = 64
PROJ_WIDTH = ATTN_WIDTH + 2 * KV_WIDTH + SSM_WIDTH
N_EXPERT_GROUPS = 4
EXPERTS_PER_GROUP = 8
N_EXPERTS = N_EXPERT_GROUPS * EXPERTS_PER_GROUP
TOP_K = 2
D_EXPERT = D_MODEL // 2
EPS = 1e-6
NEG = -1e30

kernel_name = 'hymba_swa_sink_s5_hmoe_stream_step'

def _rmsnorm(x, g):
    xf = x.astype(jnp.float32)
    y = xf * lax.rsqrt(jnp.mean(xf * xf, axis=-1, keepdims=True) + EPS)
    return (y * g.astype(jnp.float32)).astype(x.dtype)

def _project(h, w_in):
    b, L = h.shape[:2]
    z = h @ w_in
    q = z[..., :ATTN_WIDTH].reshape(b, L, N_HEADS, HEAD_DIM)
    k = z[..., ATTN_WIDTH:ATTN_WIDTH + KV_WIDTH].reshape(b, L, N_KV_HEADS, HEAD_DIM)
    v = z[..., ATTN_WIDTH + KV_WIDTH:ATTN_WIDTH + 2 * KV_WIDTH].reshape(b, L, N_KV_HEADS, HEAD_DIM)
    u = z[..., ATTN_WIDTH + 2 * KV_WIDTH:]
    return q, k, v, u

def _sink_attention(q, k, v, valid, sinks):
    s = jnp.einsum('bnqhgd,bnkhd->bnhgqk', q.astype(jnp.float32), k.astype(jnp.float32)) * (HEAD_DIM ** -0.5)
    s = jnp.where(valid[None, :, None, None, None, :], s, NEG)
    sink = sinks.astype(jnp.float32).reshape(1, 1, N_KV_HEADS, Q_PER_KV, 1, 1)
    m = jnp.maximum(jnp.max(s, axis=-1, keepdims=True), sink)
    p = jnp.exp(s - m)
    denom = jnp.sum(p, axis=-1, keepdims=True) + jnp.exp(sink - m)
    return jnp.einsum('bnhgqk,bnkhd->bnqhgd', p / denom, v.astype(jnp.float32))

def _attn_prompt(q, k, v, sinks):
    b, L = q.shape[:2]
    nc = L // CHUNK
    qb = q.reshape(b, nc, CHUNK, N_KV_HEADS, Q_PER_KV, HEAD_DIM)
    pad = ((0, 0), (N_BACK * CHUNK, 0), (0, 0), (0, 0))
    kp = jnp.pad(k, pad).reshape(b, nc + N_BACK, CHUNK, N_KV_HEADS, HEAD_DIM)
    vp = jnp.pad(v, pad).reshape(b, nc + N_BACK, CHUNK, N_KV_HEADS, HEAD_DIM)
    kb = jnp.concatenate([kp[:, j:j + nc] for j in range(N_BACK + 1)], axis=2)
    vb = jnp.concatenate([vp[:, j:j + nc] for j in range(N_BACK + 1)], axis=2)
    key_chunk = jnp.arange(nc)[:, None] - N_BACK + jnp.arange((N_BACK + 1) * CHUNK)[None, :] // CHUNK
    o = _sink_attention(qb, kb, vb, key_chunk >= 0, sinks)
    return o.reshape(b, L, ATTN_WIDTH)

def _attn_sample(q, k_new, v_new, cache_k, cache_v, sinks):
    b, L = q.shape[:2]
    wc = cache_k.shape[1]
    qb = q.reshape(b, 1, L, N_KV_HEADS, Q_PER_KV, HEAD_DIM)
    k_all = jnp.concatenate([cache_k.astype(k_new.dtype), k_new], axis=1)
    v_all = jnp.concatenate([cache_v.astype(v_new.dtype), v_new], axis=1)
    valid = jnp.ones((1, wc + L), dtype=bool)
    o = _sink_attention(qb, k_all[:, None], v_all[:, None], valid, sinks)
    return o.reshape(b, L, ATTN_WIDTH), k_all[:, L:], v_all[:, L:]

def _ssm_discretise(a_re, a_im, log_dt, b_re, b_im):
    dt = jnp.exp(log_dt.astype(jnp.float32))[:, None]
    lr = a_re.astype(jnp.float32)
    li = a_im.astype(jnp.float32)
    mag = jnp.exp(lr * dt)
    ang = li * dt
    abar_re = mag * jnp.cos(ang)
    abar_im = mag * jnp.sin(ang)
    den = lr * lr + li * li
    nr = abar_re - 1.0
    ni = abar_im
    f_re = ((nr * lr + ni * li) / den)[..., None]
    f_im = ((ni * lr - nr * li) / den)[..., None]
    br = b_re.astype(jnp.float32)
    bi = b_im.astype(jnp.float32)
    bbar_re = f_re * br - f_im * bi
    bbar_im = f_re * bi + f_im * br
    return abar_re, abar_im, bbar_re, bbar_im

def _cplx_combine(e1, e2):
    a1r, a1i, b1r, b1i = e1
    a2r, a2i, b2r, b2i = e2
    return (a2r * a1r - a2i * a1i,
            a2r * a1i + a2i * a1r,
            a2r * b1r - a2i * b1i + b2r,
            a2r * b1i + a2i * b1r + b2i)

def _ssm(u, h0_re, h0_im, disc, c_re, c_im, d_skip, w_glu, b_glu):
    abar_re, abar_im, bbar_re, bbar_im = disc
    b, L = u.shape[:2]
    ug = u.astype(jnp.float32).reshape(b, L, SSM_GROUPS, SSM_GROUP)
    bu_re = jnp.einsum('blgc,gpc->blgp', ug, bbar_re)
    bu_im = jnp.einsum('blgc,gpc->blgp', ug, bbar_im)
    h0r = h0_re.astype(jnp.float32)
    h0i = h0_im.astype(jnp.float32)
    bu_re = bu_re.at[:, 0].add(abar_re * h0r - abar_im * h0i)
    bu_im = bu_im.at[:, 0].add(abar_re * h0i + abar_im * h0r)
    a_r = jnp.broadcast_to(abar_re, bu_re.shape)
    a_i = jnp.broadcast_to(abar_im, bu_re.shape)
    _, _, h_re, h_im = lax.associative_scan(_cplx_combine, (a_r, a_i, bu_re, bu_im), axis=1)
    y = (jnp.einsum('blgp,gcp->blgc', h_re, c_re.astype(jnp.float32))
         - jnp.einsum('blgp,gcp->blgc', h_im, c_im.astype(jnp.float32))
         + d_skip.astype(jnp.float32).reshape(SSM_GROUPS, SSM_GROUP) * ug)
    y = jax.nn.gelu(y.reshape(b, L, SSM_WIDTH))
    y = y * jax.nn.sigmoid(y @ w_glu.astype(jnp.float32) + b_glu.astype(jnp.float32))
    return y.astype(u.dtype), h_re[:, -1], h_im[:, -1]

def _hier_moe(x, w_rg, b_rg, w_re, b_re, w_g, w_u, w_d):
    t = x.shape[0]
    lg = (x @ w_rg).astype(jnp.float32) + b_rg.astype(jnp.float32)
    pg = jax.nn.softmax(lg, axis=-1)
    _, gsel = lax.top_k(lg, 1)
    g_onehot = jax.nn.one_hot(gsel[:, 0], N_EXPERT_GROUPS, dtype=jnp.float32)
    le = ((x @ w_re).astype(jnp.float32) + b_re.astype(jnp.float32)).reshape(t, N_EXPERT_GROUPS, EXPERTS_PER_GROUP)
    le_g = jnp.einsum('tge,tg->te', le, g_onehot)
    tv, ti = lax.top_k(le_g, TOP_K)
    w = jax.nn.softmax(tv, axis=-1) * jnp.sum(pg * g_onehot, axis=-1, keepdims=True)
    eid = gsel * EXPERTS_PER_GROUP + ti
    gates = jnp.sum(jax.nn.one_hot(eid, N_EXPERTS, dtype=jnp.float32) * w[..., None], axis=1)
    y = jnp.zeros((t, D_MODEL), jnp.float32)
    for e in range(N_EXPERTS):
        h = jax.nn.silu(x @ w_g[e]) * (x @ w_u[e])
        y = y + gates[:, e:e + 1] * (h @ w_d[e]).astype(jnp.float32)
    return y.astype(x.dtype)

def setup_inputs(seed: int = 0) -> dict:
    key = jax.random.key(seed)
    ks = jax.random.split(key, 32)
    f32 = jnp.float32
    nrm = lambda k, shape, s: jax.random.normal(k, shape, f32) * s
    wc = min(WINDOW, PAST_LEN)
    n_idx = jnp.arange(SSM_STATE, dtype=f32)
    log_dt = jax.random.uniform(ks[8], (DEPTH, SSM_GROUPS), f32, math.log(1e-3), math.log(1e-1))
    return {
        'x_prompt': nrm(ks[0], (BATCH, SEQ, D_MODEL), 1.0),
        'x_sample': nrm(ks[1], (DEC_BATCH, DEC_SEQ, D_MODEL), 1.0),
        'cache_k': nrm(ks[2], (DEPTH, DEC_BATCH, wc, N_KV_HEADS, HEAD_DIM), 1.0),
        'cache_v': nrm(ks[3], (DEPTH, DEC_BATCH, wc, N_KV_HEADS, HEAD_DIM), 1.0),
        'state_ssm_re': nrm(ks[4], (DEPTH, DEC_BATCH, SSM_GROUPS, SSM_STATE), 0.5),
        'state_ssm_im': nrm(ks[5], (DEPTH, DEC_BATCH, SSM_GROUPS, SSM_STATE), 0.5),
        'g_norm_mix': 1.0 + nrm(ks[6], (DEPTH, D_MODEL), 0.02),
        'w_in': nrm(ks[7], (DEPTH, D_MODEL, PROJ_WIDTH), D_MODEL ** -0.5),
        'attn_sinks': nrm(ks[9], (DEPTH, N_HEADS), 0.5),
        'ssm_a_re': -0.5 + nrm(ks[10], (DEPTH, SSM_GROUPS, SSM_STATE), 0.01),
        'ssm_a_im': math.pi * n_idx + nrm(ks[11], (DEPTH, SSM_GROUPS, SSM_STATE), 0.01),
        'ssm_log_dt': log_dt,
        'ssm_b_re': nrm(ks[12], (DEPTH, SSM_GROUPS, SSM_STATE, SSM_GROUP), (2 * SSM_GROUP) ** -0.5),
        'ssm_b_im': nrm(ks[13], (DEPTH, SSM_GROUPS, SSM_STATE, SSM_GROUP), (2 * SSM_GROUP) ** -0.5),
        'ssm_c_re': nrm(ks[14], (DEPTH, SSM_GROUPS, SSM_GROUP, SSM_STATE), (2 * SSM_STATE) ** -0.5),
        'ssm_c_im': nrm(ks[15], (DEPTH, SSM_GROUPS, SSM_GROUP, SSM_STATE), (2 * SSM_STATE) ** -0.5),
        'ssm_d': 1.0 + nrm(ks[16], (DEPTH, SSM_WIDTH), 0.1),
        'w_glu': nrm(ks[17], (DEPTH, SSM_WIDTH, SSM_WIDTH), SSM_WIDTH ** -0.5),
        'b_glu': nrm(ks[18], (DEPTH, SSM_WIDTH), 0.02),
        'g_attn_out': 1.0 + nrm(ks[19], (DEPTH, ATTN_WIDTH), 0.02),
        'g_ssm_out': 1.0 + nrm(ks[20], (DEPTH, SSM_WIDTH), 0.02),
        'w_out': nrm(ks[21], (DEPTH, D_MODEL, D_MODEL), D_MODEL ** -0.5),
        'g_norm_ffn': 1.0 + nrm(ks[22], (DEPTH, D_MODEL), 0.02),
        'w_router_group': nrm(ks[23], (DEPTH, D_MODEL, N_EXPERT_GROUPS), D_MODEL ** -0.5),
        'b_router_group': nrm(ks[24], (DEPTH, N_EXPERT_GROUPS), 0.01),
        'w_router_expert': nrm(ks[25], (DEPTH, D_MODEL, N_EXPERTS), D_MODEL ** -0.5),
        'b_router_expert': nrm(ks[26], (DEPTH, N_EXPERTS), 0.01),
        'w_exp_gate': nrm(ks[27], (DEPTH, N_EXPERTS, D_MODEL, D_EXPERT), D_MODEL ** -0.5),
        'w_exp_up': nrm(ks[28], (DEPTH, N_EXPERTS, D_MODEL, D_EXPERT), D_MODEL ** -0.5),
        'w_exp_down': nrm(ks[29], (DEPTH, N_EXPERTS, D_EXPERT, D_MODEL), D_EXPERT ** -0.5),
        'g_final': 1.0 + nrm(ks[30], (D_MODEL,), 0.02),
    }

def reference(x_prompt, x_sample, cache_k, cache_v, state_ssm_re, state_ssm_im,
              g_norm_mix, w_in, attn_sinks, ssm_a_re, ssm_a_im, ssm_log_dt,
              ssm_b_re, ssm_b_im, ssm_c_re, ssm_c_im, ssm_d, w_glu, b_glu,
              g_attn_out, g_ssm_out, w_out, g_norm_ffn,
              w_router_group, b_router_group, w_router_expert, b_router_expert,
              w_exp_gate, w_exp_up, w_exp_down, g_final):
    xp, xs = x_prompt, x_sample
    bp, lp = xp.shape[:2]
    bs, ls = xs.shape[:2]
    wc_prompt = min(WINDOW, lp)
    kp_l, vp_l, srp_l, sip_l, ks_l, vs_l, srs_l, sis_l = [], [], [], [], [], [], [], []
    for l in range(DEPTH):
        hp = _rmsnorm(xp, g_norm_mix[l])
        hs = _rmsnorm(xs, g_norm_mix[l])
        qp, kp, vp, up = _project(hp, w_in[l])
        qs, kq, vq, us = _project(hs, w_in[l])
        ap = _attn_prompt(qp, kp, vp, attn_sinks[l]).astype(xp.dtype)
        a_s, k_roll, v_roll = _attn_sample(qs, kq, vq, cache_k[l], cache_v[l], attn_sinks[l])
        a_s = a_s.astype(xs.dtype)
        disc = _ssm_discretise(ssm_a_re[l], ssm_a_im[l], ssm_log_dt[l], ssm_b_re[l], ssm_b_im[l])
        h0 = jnp.zeros((bp, SSM_GROUPS, SSM_STATE), jnp.float32)
        sp, hr_p, hi_p = _ssm(up, h0, h0, disc, ssm_c_re[l], ssm_c_im[l], ssm_d[l], w_glu[l], b_glu[l])
        ss, hr_s, hi_s = _ssm(us, state_ssm_re[l], state_ssm_im[l], disc, ssm_c_re[l], ssm_c_im[l],
                              ssm_d[l], w_glu[l], b_glu[l])
        mix_p = jnp.concatenate([_rmsnorm(ap, g_attn_out[l]), _rmsnorm(sp, g_ssm_out[l])], axis=-1) @ w_out[l]
        mix_s = jnp.concatenate([_rmsnorm(a_s, g_attn_out[l]), _rmsnorm(ss, g_ssm_out[l])], axis=-1) @ w_out[l]
        xp = xp + mix_p
        xs = xs + mix_s
        tp = bp * lp
        hf = jnp.concatenate([_rmsnorm(xp, g_norm_ffn[l]).reshape(tp, D_MODEL),
                              _rmsnorm(xs, g_norm_ffn[l]).reshape(bs * ls, D_MODEL)], axis=0)
        f = _hier_moe(hf, w_router_group[l], b_router_group[l], w_router_expert[l], b_router_expert[l],
                      w_exp_gate[l], w_exp_up[l], w_exp_down[l])
        xp = xp + f[:tp].reshape(bp, lp, D_MODEL)
        xs = xs + f[tp:].reshape(bs, ls, D_MODEL)
        kp_l.append(kp[:, lp - wc_prompt:].astype(cache_k.dtype))
        vp_l.append(vp[:, lp - wc_prompt:].astype(cache_v.dtype))
        srp_l.append(hr_p.astype(state_ssm_re.dtype))
        sip_l.append(hi_p.astype(state_ssm_im.dtype))
        ks_l.append(k_roll.astype(cache_k.dtype))
        vs_l.append(v_roll.astype(cache_v.dtype))
        srs_l.append(hr_s.astype(state_ssm_re.dtype))
        sis_l.append(hi_s.astype(state_ssm_im.dtype))
    y_prompt = _rmsnorm(xp, g_final)
    y_sample = _rmsnorm(xs, g_final)
    new_k_prompt = jnp.stack(kp_l, 0)
    new_v_prompt = jnp.stack(vp_l, 0)
    new_ssm_re_prompt = jnp.stack(srp_l, 0)
    new_ssm_im_prompt = jnp.stack(sip_l, 0)
    new_k_sample = jnp.stack(ks_l, 0)
    new_v_sample = jnp.stack(vs_l, 0)
    new_ssm_re_sample = jnp.stack(srs_l, 0)
    new_ssm_im_sample = jnp.stack(sis_l, 0)
    return (y_prompt, y_sample, new_k_prompt, new_v_prompt, new_ssm_re_prompt, new_ssm_im_prompt,
            new_k_sample, new_v_sample, new_ssm_re_sample, new_ssm_im_sample)


_drawn_inputs = setup_inputs


def setup_inputs(seed=0):
    import zlib

    import numpy as np

    out = dict(_drawn_inputs(seed))
    spreads = {}
    factors = {'attn_sinks': 3.877,
     'ssm_a_re': 55.348,
     'b_glu': 16.39,
     'g_attn_out': 8.849,
     'b_router_group': 17.876,
     'b_router_expert': 20.35,
     'g_final': 21.247,
     'g_ssm_out': 5.913,
     'g_norm_ffn': 4.19}
    for name, (base, spread) in spreads.items():
        noise = np.random.default_rng([zlib.crc32(name.encode()), seed]).standard_normal(out[name].shape)
        drawn = base * np.exp(spread * noise) if base else spread * noise
        out[name] = __import__('jax').numpy.asarray(drawn.astype(out[name].dtype))
    for name, factor in factors.items():
        out[name] = (out[name] * factor).astype(out[name].dtype)
    return out
```

```python
from contextlib import ExitStack

import numpy as np

import concourse.bass as bass
from concourse import mybir

F32 = mybir.dt.float32
I32 = mybir.dt.int32
U32 = mybir.dt.uint32
ALU = mybir.AluOpType
ACT = mybir.ActivationFunctionType
AX = mybir.AxisListType

P = 128
D = 1024
SEQ = 512
NB, LS = 8, 16
TOK = SEQ + NB * LS
NT = TOK // P
KD = D // P
HD = 64
NKV, QPK = 2, 4
WIN = 128
NK = WIN + LS
G, GC, NS = 32, 16, 64
R = G // 2
T = 8
NC = TOK // T
NCP = SEQ // T
W = 512
GB = W // P
PROJ = 1280
NE, NEG_G, EPG, DE = 32, 4, 8, 512
NR = NEG_G + NE
TT = 64
KH = DE // P
TILES_MAX = 2 * TOK // TT + NE
SLOTS = TILES_MAX * TT
EPS = 1e-6
SCALE = HD ** -0.5
MASKED = -1e30
MAGIC = 1.5 * 2.0 ** 23
TWO_PI = (6.28125, 0.0019350051879882812, 3.019916050561733e-07)


def build(nc, a, o):
    with ExitStack() as ctx:
        def sb(name, shape, dt=F32):
            return ctx.enter_context(nc.sbuf_tensor(name, shape, dt))

        def sem(name):
            return ctx.enter_context(nc.semaphore(name))

        slot = [sb(f"slot{i}", [P, 12288]) for i in range(2)]
        reg_x = sb("reg_x", [P, 5120])
        reg_f = sb("reg_f", [P, 5120])
        reg_h = sb("reg_h", [P, 5120])

        gate_w = [s[:, 0:4096].rearrange("p (h c n) -> p h c n", h=2, c=4) for s in slot]
        up_w = [s[:, 4096:8192].rearrange("p (h c n) -> p h c n", h=2, c=4) for s in slot]
        down_w = [s[:, 8192:12288].rearrange("p (k n) -> p k n", k=KH) for s in slot]

        sum_w = slot[0][:, 0:4096].rearrange("p (r i m) -> p r i m", r=R, i=2)
        conv_w = slot[0][:, 4096:8192].rearrange("p (g m) -> p g m", g=G)
        out_tab = slot[0][:, 8192:12288].rearrange("p (r i t c) -> p r i t c", r=R, i=2, t=T)
        u_stage = slot[0][:, 0:2560].rearrange("p (b s n) -> p b s n", b=GB, s=T)
        rot_tmp = [slot[0][:, 1024 * i:1024 * i + 1024].rearrange("p (r n) -> p r n", r=R)
                   for i in range(4)]
        w_in = slot[1][:, 0:10240].rearrange("p (k n) -> p k n", k=KD)
        w_out = slot[1][:, 0:8192].rearrange("p (k n) -> p k n", k=KD)
        w_glu = slot[1][:, 8192:10240].rearrange("p (k n) -> p k n", k=GB)
        rot = [slot[1][:, 10240 + 1024 * i:11264 + 1024 * i].rearrange("p (r n) -> p r n", r=R)
               for i in range(2)]
        x_t = reg_h[:].rearrange("p (k t) -> p k t", k=KD)
        kern = reg_h[:, 0:4096].rearrange("p (g m) -> p g m", g=G)
        attn_t = reg_h[:, 0:2560].rearrange("p (h t) -> p h t", h=QPK)
        y_t = reg_h[:, 2560:5120].rearrange("p (b t) -> p b t", b=GB)
        mix_t = y_t
        roll = [reg_h[:, 2560 + 1024 * i:3584 + 1024 * i].rearrange("p (r n) -> p r n", r=R) for i in range(2)]
        x_sq = reg_x[:].rearrange("p (k t) -> p k t", k=KD)
        u_c = reg_x[:, 0:2560].rearrange("p (g n) -> p g n", g=G)
        y_g = reg_x[:, 0:2560].rearrange("p (b t) -> p b t", b=GB)
        states = reg_x[:, 2560:5120].rearrange("p (r i n) -> p r i n", r=R, i=2)
        mix_sq = reg_x[:, 2560:5120].rearrange("p (b t) -> p b t", b=GB)
        ffn_in = reg_x[:].rearrange("p (i n) -> p i n", i=NT)
        q_t = reg_f[:, 0:2560].rearrange("p (h t) -> p h t", h=QPK)
        kd_t = reg_f[:, 2560:3712].rearrange("p (b n) -> p b n", b=NB)
        v_old = reg_f[:, 3712:4736].rearrange("p (b n) -> p b n", b=NB)
        resid = reg_f[:].rearrange("p (i n) -> p i n", i=NT)

        k_t = sb("k_t", [P, TOK])
        kv_row = sb("kv_row", [P, NT, 256])
        sums = sb("sums", [P, 2, R, NC])
        v_new = sums[0:LS, 0].rearrange("p r n -> p (r n)")[:, 0:NB * P].rearrange("p (b n) -> p b n", b=NB)
        rstd_row = sb("rstd_row", [P, TOK])
        probs = sb("probs", [P, 2, 1024])
        probs_t = sb("probs_t", [P, 1024])
        bp_buf = sb("bp_buf", [P, 1024])
        bp = bp_buf[:].rearrange("p (r i s c) -> p r i s c", r=4, i=2, s=T)
        q_z = bp_buf[:].rearrange("p (b v h t) -> p b v h t", b=NB, v=NKV, h=QPK)
        ssm_b = sb("ssm_b", [P, 2, R, GC])
        bbar = sb("bbar", [P, 2, R, GC])
        ssm_c = sb("ssm_c", [P, 2, R, GC])
        pw = sb("pw", [P, 2, T, R])
        prep = sb("prep", [P, 32, R])
        h0 = sb("h0", [P, 2, R, NB])
        h_last = sb("h_last", [P, 2, R])
        h_dec = sb("h_dec", [P, 2, R, NB])
        dec_tmp = probs_t[:, 512:1024].rearrange("p (i r b) -> p i r b", i=4, r=R)
        mask = reg_f[:, 4736:4992]
        ident = sb("ident", [P, P])
        ones = sb("ones", [P, P])
        before = sb("before", [P, P])
        cols = sb("cols", [P, 32])
        g_mix = cols[:, 0:8]
        g_attn = cols[:, 8:12]
        g_ssm = cols[:, 12:16]
        b_glu = cols[:, 16:20]
        sink_d = cols[:, 20:21]
        sink_row = sb("sink_row", [P, 8])
        skip = sb("skip", [GC, G])
        skip_tmp = probs_t[0:GC, 0:512].rearrange("p (g c) -> p g c", g=G)
        w_r = ssm_b[:].rearrange("p i r c -> p (i r c)")[:, 0:KD * NR].rearrange("p (k n) -> p k n", k=KD)
        b_r = sb("b_r", [P, NR])
        sm = sb("sm", [P, 2, 6, 4])
        stat = sb("stat", [P, 8, NT])
        g_ffn = probs_t
        g_fin = bp_buf
        kv_f = kv_row[:].rearrange("p i n -> p (i n)")
        pair = kv_f[:, 0:320].rearrange("p (k i e) -> p k i e", k=2, i=NT)
        ptmp = kv_f[:, 320:640].rearrange("p (k i e) -> p k i e", k=2, i=NT)
        both, place, le_m = [kv_f[:, 640 + 160 * n:800 + 160 * n].rearrange("p (i e) -> p i e", i=NT)
                             for n in range(3)]
        le_g, top_g, top_e = [kv_f[:, 1120 + 40 * n:1160 + 40 * n].rearrange("p (i e) -> p i e", i=NT)
                              for n in range(3)]
        one_g = kv_f[:, 1240:1260].rearrange("p (i e) -> p i e", i=NT)
        place_e = rstd_row[:, 0:160].rearrange("p (e i) -> p e i", e=NE)
        logit = rstd_row[:, 160:340].rearrange("p (i n) -> p i n", i=NT)
        pad8 = sb("pad8", [P, NT, 8])
        ig = sb("ig", [P, NT, 8], U32)
        ie = sb("ie", [P, NT, 8], U32)
        iota_e = sb("iota_e", [P, NE])
        iota_t = sb("iota_t", [P, TT])
        tile_tt = sb("tile_tt", [P, NT])
        zero_nt = sb("zero_nt", [P, NT])
        rt = sb("rt", [P, 12, NT])
        pos_u = sb("pos_u", [P, 2, NT], U32)
        ntile = sb("ntile", [P, 3, NE])
        first_f = sb("first_f", [P, NE + 1])
        first_i = sb("first_i", [1, NE + 1], I32)

        xrow = probs[:, 0, 0:512]
        xt_e = probs[:, 0, 512:1024].rearrange("p (c n) -> p c n", c=4)
        act_g = probs[0:TT, 1, 0:512]
        hid = probs[0:TT, 1, 512:1024]
        sums_f = sums[:].rearrange("p i r n -> p (i r n)")
        hid_t = sums_f[:, 0:256].rearrange("p (k t) -> p k t", k=KH)
        y_out = [sums_f[:, 256 + 512 * i:768 + 512 * i] for i in range(2)]
        sel = sums_f[:, 1280:1600].rearrange("p (i s) -> p i s", i=NT)
        place_b = sums_f[:, 1600:1605]
        place_c = sums_f[:, 1608:1613]
        got = [[slot[i][:, 1024 * k:1024 * k + 1024] for k in range(2)] for i in range(2)]
        fin = [slot[i][:, 2048:3072] for i in range(2)]
        junk = slot[0][:, 4096:5120]

        pp = [ctx.enter_context(nc.psum_tensor(f"pair{i}", [P, 2, 512], F32)) for i in range(4)]

        u_scr = nc.dram_tensor("u_scr", [W, T, NC], F32).ap()
        y_scr = nc.dram_tensor("y_scr", [W, T, NC], F32).ap()
        y_slots = nc.dram_tensor("y_slots", [SLOTS, D], F32).ap()

        names = """in_small in_x0 in_x1 in_w0 in_w1 in_attn in_kv out_w in_resid in_rows
            const_done dve_step pool_step act_step sq_done rstd_ps rstd_act rstd_done xg_done proj_ps proj_out
            kv_ps kv_out tr_ps stat_cols u_out u_stored u_in prep_act prep_dve bbar_done bp_ready bp_tr bp_out
            out_tab_done kern_ps kern_out conv_zero kern_done conv_in sum_ps sum_out rot_done states_done
            y_ps y_out_done y_stored y_in gelu_done glu_ps sig_done mix_done mixsq_done
            sc_ps neg_done exp_done norm_done pt_ps pt_out av_ps av_sq attn_done attn_z
            vnew_in states_out cache_out ssq_ps ssq_out rs_act rs_done op_ps op_out rsf_act ffn_sq ffn_done
            xf_tr xf_out lg_ps lg_out route_act pair_done place_ps pos_done
            gate_in0 gate_in1 up_in0 up_in1 down_in0 down_in1 sel_ready gx_ready gx_copied xt_ready xt_copied
            gu_ready sg_ready h_ready ht_ready ht_copied y_ready y_copied y_kept0 y_kept1
            got0 got1 zero_ready zeroed fin_sq fin_ms fin_sqrt fin_done sc_read base_step place_ready rows_done stat_ready skip_ready ssq_read rot_ready ffn_ms ffn_sqrt rsf_ms op_read fin_out0 fin_out1""".split()
        s = {n: sem(n) for n in names}
        gate_in = [s["gate_in0"], s["gate_in1"]]
        up_in = [s["up_in0"], s["up_in1"]]
        down_in = [s["down_in0"], s["down_in1"]]
        y_kept = [s["y_kept0"], s["y_kept1"]]
        got_in = [s["got0"], s["got1"]]
        fin_out = [s["fin_out0"], s["fin_out1"]]

        N_SMALL = 19

        block = ctx.enter_context(nc.Block())

        def tiles_of(eng, e):
            first = eng.value_load(first_i[0:1, bass.ds(e, 1)], min_val=0, max_val=TILES_MAX - 1)
            end = eng.value_load(first_i[0:1, bass.ds(e + 1, 1)], min_val=1, max_val=TILES_MAX)
            return first, end

        gate_v = a["w_exp_gate"].rearrange("e (h p c) n -> e p h c n", h=2, c=4)
        up_v = a["w_exp_up"].rearrange("e (h p c) n -> e p h c n", h=2, c=4)
        down_v = a["w_exp_down"].rearrange("e (p k) n -> e p k n", k=KH)

        @block.sync
        def _(sp):
            w_in_v = a["w_in"].rearrange("(p k) n -> p k n", k=KD)
            for h in range(2):
                kk = slice(4 * h, 4 * h + 4)
                sp.dma_start(x_t[:, kk, :], a["x_t"][:, kk, :]).then_inc(s[f"in_x{h}"], 16)
            for h in range(2):
                kk = slice(4 * h, 4 * h + 4)
                sp.dma_start(w_in[:, kk, :], w_in_v[:, kk, :]).then_inc(s[f"in_w{h}"], 16)
            sp.wait_ge(s["zero_ready"], 1)
            sp.dma_start(y_slots.rearrange("(i p) n -> p i n", p=P),
                         probs_t[:].unsqueeze(1).to_broadcast([P, SLOTS // P, D])).then_inc(s["zeroed"], 16)
            sp.dma_start(kd_t[:, :, 0:WIN], a["cache_k_t"]).then_inc(s["in_attn"], 16)
            sp.dma_start(v_old, a["cache_v"].rearrange("b k n -> k b n")).then_inc(s["in_attn"], 16)

            for b in range(GB):
                sp.wait_ge(s["u_out"], b + 1)
                sp.dma_start(u_scr[b * P:(b + 1) * P], u_stage[:, b]).then_inc(s["u_stored"], 16)
            sp.wait_ge(s["u_stored"], 16 * GB)
            sp.wait_ge(s["rstd_ps"], 1)
            us = u_scr.rearrange("(g c) s n -> s c g n", c=GC)
            for t in range(T):
                sp.dma_start(u_c[GC * t:GC * t + GC], us[t]).then_inc(s["u_in"], 16)
            sp.wait_ge(s["conv_zero"], 1)
            sp.wait_ge(s["kern_done"], 1)
            for t in range(T):
                sp.dma_start(conv_w[GC * t:GC * t + GC, :, GC * t:P], kern[0:GC, :, 0:P - GC * t])\
                    .then_inc(s["conv_in"], 16)
            sp.wait_ge(s["kv_out"], NT)
            for n, name in enumerate(("k", "v")):
                sp.dma_start(o[f"new_{name}_prompt"], kv_row[:, NT - 2, P * n:P * n + P])\
                    .then_inc(s["cache_out"], 16)
                for b in range(NB):
                    sp.dma_start(o[f"new_{name}_sample"][b, WIN - LS:WIN, :],
                                 kv_row[LS * b:LS * b + LS, NT - 1, P * n:P * n + P]).then_inc(s["cache_out"], 16)
                sp.dma_start(o[f"new_{name}_sample"][:, 0:WIN - LS, :], a[f"cache_{name}"][:, LS:WIN, :])\
                    .then_inc(s["cache_out"], 16)
            sp.wait_ge(s["kv_ps"], NT)
            sp.dma_start(w_out, a["w_out"]).then_inc(s["out_w"], 16)
            sp.dma_start(w_glu, a["w_glu"].rearrange("(k p) n -> p k n", p=P)).then_inc(s["out_w"], 16)
            sp.wait_ge(s["y_out_done"], 8)
            ys = y_scr.rearrange("(g c) t n -> t c g n", c=GC)
            for t in range(T):
                sp.dma_start(ys[t], u_c[GC * t:GC * t + GC]).then_inc(s["y_stored"], 16)
            sp.wait_ge(s["y_stored"], 16 * T)
            sp.dma_start(y_t, y_scr.rearrange("(b p) t n -> p b (t n)", p=P)).then_inc(s["y_in"], 16)
            sp.wait_ge(s["states_done"], 3)
            for b in range(NB):
                sp.dma_start(v_new[:, b, :], kv_row[LS * b:LS * b + LS, NT - 1, P:256]).then_inc(s["vnew_in"], 16)
            sp.dma_start(o["state_prompt"], h_last[:]).then_inc(s["states_out"], 16)
            sp.dma_start(o["state_sample"], h_dec[:]).then_inc(s["states_out"], 16)
            sp.wait_ge(s["y_ps"], 4)
            sp.dma_start(gate_w[0], gate_v[0]).then_inc(gate_in[0], 16)
            sp.dma_start(up_w[0], up_v[0]).then_inc(up_in[0], 16)
            sp.dma_start(down_w[0], down_v[0]).then_inc(down_in[0], 16)
            sp.wait_ge(s["av_ps"], NT)
            sp.dma_start(resid, a["x_rows"].rearrange("(i p) n -> p i n", p=P)).then_inc(s["in_resid"], 16)
            sp.dma_start(w_r, a["w_router"].rearrange("(p k) n -> p k n", k=KD)).then_inc(s["in_rows"], 16)
            sp.dma_start(g_ffn[:], a["g_norm_ffn"].to_broadcast((P, D))).then_inc(s["in_rows"], 16)
            sp.dma_start(g_fin[:], a["g_final"].to_broadcast((P, D))).then_inc(s["in_rows"], 16)
            sp.wait_ge(s["op_ps"], 2 * NT)
            sp.dma_start(gate_w[1], gate_v[1]).then_inc(gate_in[1], 16)
            sp.dma_start(up_w[1], up_v[1]).then_inc(up_in[1], 16)
            sp.dma_start(down_w[1], down_v[1]).then_inc(down_in[1], 16)
            sp.wait_ge(s["pos_done"], 1)
            with sp.Fori(1, NE // 2) as it:
                for q in range(2):
                    e = it * 2 + q
                    done = sp.value_load(first_i[0:1, bass.ds(e - 1, 1)], min_val=1, max_val=TILES_MAX)
                    sp.wait_ge(s["gu_ready"], done)
                    sp.dma_start(gate_w[q], gate_v[e]).then_inc(gate_in[q], 16)
                    sp.dma_start(up_w[q], up_v[e]).then_inc(up_in[q], 16)
                    sp.wait_ge(s["y_ready"], done)
                    sp.dma_start(down_w[q], down_v[e]).then_inc(down_in[q], 16)
            for i in range(NT):
                sp.wait_ge(s["fin_done"], i + 1)
                sp.dma_start(o["y"][P * i:P * i + P, :], fin[i % 2]).then_inc(fin_out[i % 2], 16)
            sp.wait_ge(fin_out[0], 16 * 3)
            sp.wait_ge(fin_out[1], 16 * 2)
            sp.wait_ge(s["states_out"], 32)
            sp.wait_ge(s["cache_out"], 16 * 2 * (NB + 2))

        @block.gpsimd
        def _(pool):
            steps = [0]

            def step(ins):
                steps[0] += 1
                ins.then_inc(s["pool_step"], 1)
                pool.wait_ge(s["pool_step"], steps[0])

            pool.memset(probs_t[:], 0.0).then_inc(s["zero_ready"], 1)
            loads = [(g_mix, a["g_norm_mix"]), (g_attn, a["g_attn"]), (g_ssm, a["g_ssm"]), (b_glu, a["b_glu"]),
                     (sink_d, a["sink_rows"]), (sink_row[:], a["sinks"].to_broadcast((P, 8))),
                     (skip[:], a["ssm_d"]), (b_r[:], a["b_router"].to_broadcast((P, NR)))]
            loads += [(ssm_b[:, i], a["ssm_b"][:, i]) for i in range(2)]
            loads += [(ssm_c[:, i], a["ssm_c"][:, i]) for i in range(2)]
            loads += [(h0[:, i], a["h0"][:, i]) for i in range(2)]
            loads += [(prep[:, 0, :], a["a_re"]), (prep[:, 1, :], a["a_im"])]
            loads += [(prep[HD * m:HD * m + HD, 2, :], a["log_dt"][m:m + 1, :].to_broadcast((HD, R))) for m in range(2)]
            for dst, src in loads[-4:] + loads[:-4]:
                pool.dma_start(dst, src).then_inc(s["in_small"], 16)
            assert len(loads) + 1 == N_SMALL

            step(pool.memset(ident[:], 0.0))
            step(pool.affine_select(out=ident[:], in_=ident[:], compare_op=ALU.not_equal, fill=1.0, base=0,
                                    pattern=[[-1, P]], channel_multiplier=1))
            step(pool.memset(ones[:], 1.0))
            step(pool.affine_select(out=before[:], in_=ones[:], compare_op=ALU.is_gt, fill=0.0, base=0,
                                    pattern=[[1, P]], channel_multiplier=-1))
            step(pool.memset(tile_tt[:], float(TT)))
            step(pool.memset(zero_nt[:], 0.0))
            step(pool.memset(mask, 0.0))
            step(pool.memset(mask[0:HD, 192:256], MASKED))
            step(pool.memset(mask[HD:P, 0:HD], MASKED))
            step(pool.iota(iota_e[:], [[1, NE]], base=0, channel_multiplier=0, allow_small_or_imprecise_dtypes=True))
            step(pool.iota(iota_t[:], [[1, TT]], base=0, channel_multiplier=0,
                           allow_small_or_imprecise_dtypes=True))
            pool.memset(pad8[:], -3.0e38).then_inc(s["const_done"], 1)

            pool.wait_ge(s["bbar_done"], 1)
            t1 = probs[:, 0, 0:448].rearrange("p (r s c) -> p r s c", r=4, s=7)
            t2 = probs[:, 0, 512:960].rearrange("p (r s c) -> p r s c", r=4, s=7)
            for q in range(4):
                rr = slice(4 * q, 4 * q + 4)
                pr, pi = [pw[:, i, 1:T, rr].rearrange("p s r -> p r s").unsqueeze(3).to_broadcast([P, 4, T - 1, GC])
                          for i in range(2)]
                br, bi = [bbar[:, i, rr, :].unsqueeze(2).to_broadcast([P, 4, T - 1, GC]) for i in range(2)]
                if q >= 1:
                    pool.wait_ge(s["bp_tr"], q)
                for i in range(2):
                    pool.tensor_copy(bp[:, :, i, T - 1, :], bbar[:, i, rr, :])
                pool.tensor_tensor(t1, br, pr, ALU.mult)
                step(pool.tensor_tensor(t2, bi, pi, ALU.mult))
                step(pool.tensor_tensor(bp[:, :, 0, 0:T - 1, :], t1, t2, ALU.subtract))
                pool.tensor_tensor(t1, br, pi, ALU.mult)
                step(pool.tensor_tensor(t2, bi, pr, ALU.mult))
                pool.tensor_tensor(bp[:, :, 1, 0:T - 1, :], t1, t2, ALU.add).then_inc(s["bp_ready"], 1)

            re, im = rot
            wl = [prep[:, 20 + i, :] for i in range(4)]
            step(pool.memset(re[:, :, 0:1], 1.0))
            step(pool.memset(im[:, :, 0:1], 0.0))
            n = 1
            cur, nxt = (prep[:, 18, :], prep[:, 19, :]), wl[0:2]
            while n < NCP:
                cr, ci = [c.unsqueeze(2).to_broadcast([P, R, n]) for c in cur]
                m1 = probs[:, 0, 0:R * n].rearrange("p (r n) -> p r n", n=n)
                m2 = probs[:, 0, 512:512 + R * n].rearrange("p (r n) -> p r n", n=n)
                pool.tensor_tensor(m1, re[:, :, 0:n], cr, ALU.mult)
                step(pool.tensor_tensor(m2, im[:, :, 0:n], ci, ALU.mult))
                step(pool.tensor_tensor(re[:, :, n:2 * n], m1, m2, ALU.subtract))
                pool.tensor_tensor(m1, re[:, :, 0:n], ci, ALU.mult)
                step(pool.tensor_tensor(m2, im[:, :, 0:n], cr, ALU.mult))
                step(pool.tensor_tensor(im[:, :, n:2 * n], m1, m2, ALU.add))
                q1, q2 = prep[:, 24, :], prep[:, 25, :]
                pool.tensor_tensor(q1, cur[0], cur[0], ALU.mult)
                step(pool.tensor_tensor(q2, cur[1], cur[1], ALU.mult))
                step(pool.tensor_tensor(nxt[0], q1, q2, ALU.subtract))
                step(pool.tensor_tensor(q1, cur[0], cur[1], ALU.mult))
                step(pool.tensor_tensor(nxt[1], q1, q1, ALU.add))
                cur, nxt = nxt, (wl[2:4] if nxt is wl or nxt[0] is wl[0] else wl[0:2])
                n *= 2
            pool.sem_inc(s["rot_ready"], 1)

            pool.wait_ge(s["bp_tr"], 4)
            pool.memset(bp_buf[:], 0.0).then_inc(s["attn_z"], 1)

            pool.wait_ge(s["sum_out"], 8)
            ar, ai = [pw[:, i, 0, :].unsqueeze(2).to_broadcast([P, R, NB]) for i in range(2)]
            dec = states[:, :, :, NCP:NC].rearrange("p r i (b j) -> p r i b j", j=2)
            new = sums[:, :, :, NCP:NC].rearrange("p i r (b j) -> p i r b j", j=2)
            d0, d1 = dec_tmp[:, 0], dec_tmp[:, 1]
            for i in range(2):
                step(pool.tensor_copy(dec[:, :, i, :, 0], h0[:, i]))
            for j in range(2):
                hr, hi = (h0[:, 0], h0[:, 1]) if j == 0 else (dec_tmp[:, 2], dec_tmp[:, 3])
                tr, ti = (dec_tmp[:, 2], dec_tmp[:, 3]) if j == 0 else (h_dec[:, 0], h_dec[:, 1])
                for x, y, op, dst, i in ((ar, ai, ALU.subtract, tr, 0), (ai, ar, ALU.add, ti, 1)):
                    step(pool.tensor_tensor(d0, hr, x, ALU.mult))
                    step(pool.tensor_tensor(d1, hi, y, ALU.mult))
                    step(pool.tensor_tensor(d0, d0, d1, op))
                    step(pool.tensor_tensor(dst, d0, new[:, i, :, :, j], ALU.add))
                if j == 0:
                    for i in range(2):
                        step(pool.tensor_copy(dec[:, :, i, :, 1], dec_tmp[:, 2 + i]))
            pool.sem_inc(s["states_done"], 2)

            pool.wait_ge(s["pos_done"], 1)
            pool.sem_inc(s["base_step"], 1)
            pool.sem_inc(s["sel_ready"], 1)
            with pool.Fori(0, NE) as e:
                first, end = tiles_of(pool, e)
                pool.wait_ge(s["base_step"], e + first + 1)
                pool.tensor_copy(place_b, place_e[:, bass.ds(e, 1), :].rearrange("p e i -> p (e i)"))\
                    .then_inc(s["base_step"], 1)
                with pool.Fori(first, end) as w:
                    pool.wait_ge(s["base_step"], e + w + 2)
                    pool.wait_ge(s["sel_ready"], w + 1)
                    pool.tensor_tensor(place_c, place_b, zero_nt[:], ALU.add).then_inc(s["place_ready"], 1)
                    pool.wait_ge(s["place_ready"], w + 1)
                    pool.tensor_tensor(place_b, place_b, tile_tt[:], ALU.subtract).then_inc(s["base_step"], 1)
            pool.sem_inc(s["place_ready"], 1)

            pool.wait_ge(s["rows_done"], 1)
            for i in range(NT):
                if i >= 2:
                    pool.wait_ge(s["fin_done"], i - 1)
                for k in range(2):
                    pool.indirect_dma_start(got[i % 2][k], None, y_slots,
                                            bass.IndirectOffsetOnAxis(pos_u[:, k, i:i + 1], 0))\
                        .then_inc(got_in[i % 2], 16)

        @block.tensor
        def _(pe):
            pe.wait_ge(s["const_done"], 1)
            for h in range(2):
                pe.wait_ge(s["sq_done"], h + 1)
                for k in range(4 * h, 4 * h + 4):
                    pe.matmul(pp[2][:, 0, :], ones[:], x_sq[:, k, 0:SEQ], start=k == 0, stop=k == KD - 1)
                    ins = pe.matmul(pp[2][:, 1, 0:P], ones[:], x_sq[:, k, SEQ:TOK], start=k == 0, stop=k == KD - 1)
            ins.then_inc(s["rstd_ps"], 1)

            columns = [768 + P * b for b in range(GB)] + [512] + [P * h for h in range(QPK)]
            for n, c in enumerate(columns):
                t = pp[n % 2]
                if n >= 2:
                    pe.wait_ge(s["proj_out"], n - 1)
                for k in range(KD):
                    if n == 0 and k % 4 == 0:
                        pe.wait_ge(s["xg_done"], k // 4 + 1)
                        pe.wait_ge(s[f"in_w{k // 4}"], 16)
                    pe.matmul(t[:, 0, :], w_in[:, k, c:c + P], x_t[:, k, 0:SEQ], start=k == 0, stop=k == KD - 1)
                    ins = pe.matmul(t[:, 1, 0:P], w_in[:, k, c:c + P], x_t[:, k, SEQ:TOK],
                                    start=k == 0, stop=k == KD - 1)
                ins.then_inc(s["proj_ps"], 1)
            pe.wait_ge(s["rstd_done"], 1)
            for i in range(NT):
                ins = pe.matmul(pp[3][:, 1, i:i + 1], rstd_row[0:1, P * i:P * i + P], ones[0:1, 0:1],
                                start=True, stop=True)
            ins.then_inc(s["stat_cols"], 1)
            for i in range(NT):
                t = pp[2 + i % 2][:, 0, 0:256]
                if i >= 2:
                    pe.wait_ge(s["kv_out"], i - 1)
                for k in range(KD):
                    ins = pe.matmul(t, x_t[:, k, P * i:P * i + P], w_in[:, k, 512:768], start=k == 0, stop=k == KD - 1)
                ins.then_inc(s["kv_ps"], 1)

            pe.wait_ge(s["out_tab_done"], 1)
            pe.wait_ge(s["proj_out"], 9)
            for q in range(4):
                if q >= 2:
                    pe.wait_ge(s["kern_out"], 2 * (q - 1))
                for j in range(4):
                    r = 4 * q + j
                    for m in range(2):
                        rows = slice(HD * m, HD * m + HD)
                        for i in range(2):
                            pe.matmul(pp[q % 2][0:GC, m, P * j:P * j + GC], bbar[rows, i, r, :], ssm_c[rows, i, r, :],
                                      start=i == 0, stop=i == 1)
                        for i in range(2):
                            ins = pe.matmul(pp[q % 2][0:GC, m, P * j + GC:P * j + P], bbar[rows, i, r, :],
                                            out_tab[rows, r, i, 0:T - 1, :], start=i == 0, stop=i == 1)
                ins.then_inc(s["kern_ps"], 1)
            pe.wait_ge(s["kv_out"], NT)
            for q in range(4):
                pe.wait_ge(s["bp_ready"], q + 1)
                if q >= 2:
                    pe.wait_ge(s["bp_out"], 2 * (q - 1))
                for j in range(4):
                    for i in range(2):
                        ins = pe.transpose(pp[2 + q % 2][:, j // 2, 256 * (j % 2) + P * i:256 * (j % 2) + P * i + P],
                                           bp[:, j, i].rearrange("p s c -> p (s c)"), ident[:])
                ins.then_inc(s["bp_tr"], 1)
            pe.wait_ge(s["bp_out"], 8)
            pe.wait_ge(s["u_in"], 16 * T)
            pe.wait_ge(s["kern_out"], 8)
            for q in range(4):
                if q >= 2:
                    pe.wait_ge(s["sum_out"], 2 * (q - 1))
                for j in range(4):
                    r = 4 * q + j
                    for i in range(2):
                        for m in range(2):
                            ins = pe.matmul(pp[q % 2][HD * m:HD * m + HD, i, NC * j:NC * j + NC],
                                            sum_w[:, r, i, HD * m:HD * m + HD], u_c[:, 2 * r + m, :],
                                            start=True, stop=True)
                ins.then_inc(s["sum_ps"], 1)

            def scores(n):
                m, v = n // 2, n % 2
                rows = slice(HD * v, HD * v + HD)
                sc = pp[v][:].rearrange("p b (h n) -> p (b h) n", h=2)
                if n >= 2:
                    pe.wait_ge(s["sc_read"], n - 1)
                lo = 0 if m else P
                for h in range(QPK):
                    ins = pe.matmul(sc[:, h, lo:256], q_t[rows, h, P * m:P * m + P],
                                    k_t[rows, P * (m - 1) + lo:P * (m + 1)], start=True, stop=True)
                ins.then_inc(s["sc_ps"], 1)

            def weighted(n):
                m, v = n // 2, n % 2
                pe.wait_ge(s["norm_done"], n + 1)
                if n >= 1:
                    pe.wait_ge(s["pt_out"], n)
                pr = probs[:, n % 2].rearrange("p (h n) -> p h n", h=QPK)
                for kt in range(0 if m else 1, 2):
                    for h in range(QPK):
                        ins = pe.transpose(pp[2][:, kt, P * h:P * h + P], pr[:, h, P * kt:P * kt + P], ident[:])
                ins.then_inc(s["pt_ps"], 1)
                pe.wait_ge(s["pt_out"], n + 1)
                if v == 0 and m >= 1:
                    pe.wait_ge(s["attn_done"], m)
                for kt in range(0 if m else 1, 2):
                    ins = pe.matmul(pp[3][HD * v:HD * v + HD, 0, :], kv_row[:, m - 1 + kt, P + HD * v:P + HD * v + HD],
                                    probs_t[:, 512 * kt:512 * kt + 512], start=kt == (0 if m else 1), stop=kt == 1)
                if v == 1:
                    ins.then_inc(s["av_ps"], 1)

            def squares(m):
                pe.wait_ge(s["av_sq"], m + 1)
                for h in range(QPK):
                    ins = pe.matmul(pp[3][:, 1, m:m + 1], rstd_row[:, P * h:P * h + P], ones[:, 0:1],
                                    start=h == 0, stop=h == QPK - 1)
                ins.then_inc(s["ssq_ps"], 1)

            pe.wait_ge(s["sum_out"], 8)
            pe.wait_ge(s["bp_out"], 8)
            scores(0)
            scores(1)
            pe.wait_ge(s["conv_in"], 16 * T)
            pe.wait_ge(s["states_done"], 3)
            for q in range(4):
                if q >= 2:
                    pe.wait_ge(s["y_out_done"], 2 * (q - 1))
                for j in range(4):
                    r = 4 * q + j
                    for m in range(2):
                        rows = slice(HD * m, HD * m + HD)
                        t = pp[2 + q % 2][:, m, NC * j:NC * j + NC]
                        pe.matmul(t, conv_w[:, 2 * r + m, :], u_c[:, 2 * r + m, :], start=True, stop=False)
                        for i in range(2):
                            ins = pe.matmul(t, out_tab[rows, r, i].rearrange("p t c -> p (t c)"), states[rows, r, i, :],
                                            start=False, stop=i == 1)
                ins.then_inc(s["y_ps"], 1)
            pe.wait_ge(s["y_out_done"], 8)
            for n in range(8):
                weighted(n)
                if n + 2 < 8:
                    scores(n + 2)
                if n % 2:
                    squares(n // 2)

            pe.wait_ge(s["in_attn"], 32)
            pe.wait_ge(s["sc_read"], 8)
            pe.wait_ge(s["vnew_in"], 16 * NB)
            for j in range(3):
                bs = range(3 * j, min(3 * j + 3, NB))
                for b in bs:
                    ins = pe.matmul(pp[j % 2][:, j // 2, NK * (b - 3 * j):NK * (b - 3 * j) + NK],
                                    q_z[:, b].rearrange("p v h t -> p (v h t)"), kd_t[:, b, :], start=True, stop=True)
                ins.then_inc(s["sc_ps"], 1)
            for j in range(3):
                bs = range(3 * j, min(3 * j + 3, NB))
                n = 8 + j
                pe.wait_ge(s["norm_done"], n + 1)
                pe.wait_ge(s["pt_out"], n)
                pr = probs[:, j % 2, 0:3 * NK].rearrange("p (b n) -> p b n", b=3)
                for b in bs:
                    c = P * (b - 3 * j)
                    pe.transpose(pp[2][:, 0, c:c + P], pr[:, b - 3 * j, 0:WIN], ident[:])
                    ins = pe.transpose(pp[2][0:LS, 1, c:c + P], pr[:, b - 3 * j, WIN:NK], ident[:])
                ins.then_inc(s["pt_ps"], 1)
                pe.wait_ge(s["pt_out"], n + 1)
                if j == 0:
                    pe.wait_ge(s["attn_done"], NT - 1)
                for b in bs:
                    for v in range(NKV):
                        c = P * (b - 3 * j) + HD * v
                        t = pp[3][HD * v:HD * v + HD, 0, HD * b:HD * b + HD]
                        pe.matmul(t, v_old[:, b, HD * v:HD * v + HD], probs_t[:, c:c + HD], start=True, stop=False)
                        ins = pe.matmul(t, v_new[:, b, HD * v:HD * v + HD], probs_t[0:LS, 512 + c:512 + c + HD],
                                        start=False, stop=True)
            ins.then_inc(s["av_ps"], 1)
            squares(NT - 1)

            pe.wait_ge(s["gelu_done"], 1)
            pe.wait_ge(s["out_w"], 32)
            pe.wait_ge(s["exp_done"], 11)
            for n in range(GB):
                if n >= 2:
                    pe.wait_ge(s["sig_done"], n - 1)
                for k in range(GB):
                    pe.matmul(pp[n % 2][:, 0, :], w_glu[:, k, P * n:P * n + P], y_g[:, k, 0:512],
                              start=k == 0, stop=k == GB - 1)
                    ins = pe.matmul(pp[n % 2][:, 1, 0:P], w_glu[:, k, P * n:P * n + P], y_g[:, k, 512:TOK],
                                    start=k == 0, stop=k == GB - 1)
                ins.then_inc(s["glu_ps"], 1)
            pe.wait_ge(s["mixsq_done"], GB)
            for i in range(NT):
                for b in range(GB):
                    ins = pe.matmul(pp[3][:, 1, NT + i:NT + i + 1], mix_sq[:, b, P * i:P * i + P], ones[:, 0:1],
                                    start=b == 0, stop=b == GB - 1)
            ins.then_inc(s["ssq_ps"], 1)

            def router(i):
                pe.wait_ge(s["ffn_done"], i + 1)
                if i >= 1:
                    pe.wait_ge(s["xf_out"], i)
                for k in range(KD):
                    ins = pe.transpose(pp[2][:, k // 4, P * (k % 4):P * (k % 4) + P], ffn_in[:, i, k:D:KD], ident[:])
                ins.then_inc(s["xf_tr"], 1)
                pe.wait_ge(s["xf_out"], i + 1)
                xf = probs[:, i % 2].rearrange("p (k t) -> p k t", k=KD)
                for k in range(KD):
                    ins = pe.matmul(pp[3][:, 0, NR * i:NR * i + NR], xf[:, k, :], w_r[:, k, :],
                                    start=k == 0, stop=k == KD - 1)
                ins.then_inc(s["lg_ps"], 1)

            pe.wait_ge(s["sig_done"], GB)
            pe.wait_ge(s["mix_done"], GB + 1)
            for i in range(NT):
                for m, left in enumerate((attn_t, mix_t)):
                    if i >= 1:
                        pe.wait_ge(s["op_out"], 2 * (i - 1) + m + 1)
                    for n in range(2):
                        for k in range(GB):
                            ins = pe.matmul(pp[m][:, n, :], left[:, k, P * i:P * i + P],
                                            w_out[:, 4 * m + k, 512 * n:512 * n + 512], start=k == 0, stop=k == GB - 1)
                    ins.then_inc(s["op_ps"], 1)
                if i >= 1:
                    router(i - 1)
            router(NT - 1)

            pe.wait_ge(s["pair_done"], 1)
            for i in range(NT):
                for j in range(i + 1):
                    pe.matmul(pp[3][:, 1, NE * i:NE * i + NE], before[:] if j == i else ones[:], both[:, j, :],
                              start=j == 0, stop=j == i)
            for i in range(NT):
                ins = pe.matmul(pp[3][:, 1, 256:256 + NE], ones[:], both[:, i, :], start=i == 0, stop=i == NT - 1)
            ins.then_inc(s["place_ps"], 1)

            gu, yp, gx, xtp, htp = pp[0][:, 0, :], pp[0][:, 1, :], pp[2][:, 0, :], pp[2][:, 1, :], pp[1][:, 0, 0:256]

            def pick(w=None):
                for i in range(NT):
                    if w is not None and i == NT - 1:
                        pe.wait_ge(s["h_ready"], w + 1)
                    for h in range(2):
                        ins = pe.matmul(gx[HD * h:HD * h + HD], sel[:, i, :], ffn_in[:, i, 512 * h:512 * h + 512],
                                        start=i == 0, stop=i == NT - 1)
                ins.then_inc(s["gx_ready"], 1)

            def turn():
                for c in range(4):
                    ins = pe.transpose(xtp[:, P * c:P * c + P], xrow[:, c:512:4], ident[:])
                ins.then_inc(s["xt_ready"], 1)

            pe.wait_ge(s["sel_ready"], 2)
            pick()
            pe.wait_ge(s["gx_copied"], 1)
            turn()
            with pe.Fori(0, NE // 2) as it:
                for q in range(2):
                    first, end = tiles_of(pe, it * 2 + q)
                    with pe.Fori(first, end) as w:
                        pe.wait_ge(s["xt_copied"], w + 1)
                        pe.wait_ge(gate_in[q], it * 16 + 16)
                        pe.wait_ge(up_in[q], it * 16 + 16)
                        for n in range(KD):
                            h, c = n // 4, n % 4
                            lhs = xt_e[:, c, TT * h:TT * h + TT]
                            pe.matmul(gu[0:TT], lhs, gate_w[q][:, h, c, :], start=n == 0, stop=n == KD - 1)
                            ins = pe.matmul(gu[TT:P], lhs, up_w[q][:, h, c, :], start=n == 0, stop=n == KD - 1)
                        ins.then_inc(s["gu_ready"], 1)
                        pe.wait_ge(s["sel_ready"], w + 3)
                        pick(w)
                        for k in range(KH):
                            ins = pe.transpose(htp[:, TT * k:TT * k + TT], hid[:, k:DE:KH], ident[0:TT, 0:TT])
                        ins.then_inc(s["ht_ready"], 1)
                        pe.wait_ge(s["gx_copied"], w + 2)
                        turn()
                        pe.wait_ge(s["ht_copied"], w + 1)
                        pe.wait_ge(down_in[q], it * 16 + 16)
                        pe.wait_ge(s["y_copied"], w + 1)
                        for k in range(KH):
                            for h in range(2):
                                ins = pe.matmul(yp[TT * h:TT * h + TT], hid_t[:, k, :],
                                                down_w[q][:, k, 512 * h:512 * h + 512],
                                                start=k == 0, stop=k == KH - 1)
                        ins.then_inc(s["y_ready"], 1)

        @block.scalar
        def _(act):
            for h in range(2):
                act.wait_ge(s[f"in_x{h}"], 16)
                kk = slice(4 * h, 4 * h + 4)
                act.activation(x_sq[:, kk, :], x_t[:, kk, :], ACT.Square).then_inc(s["sq_done"], 1)
            act.wait_ge(s["in_small"], 16 * (N_SMALL - 1))
            act.activation(prep[:, 3, :], prep[:, 2, :], ACT.Exp).then_inc(s["prep_act"], 1)
            act.wait_ge(s["prep_dve"], 1)
            act.activation(prep[:, 6, :], prep[:, 4, :], ACT.Exp).then_inc(s["prep_act"], 1)
            act.wait_ge(s["rstd_act"], 1)
            act.activation(rstd_row[:], rstd_row[:], ACT.Sqrt).then_inc(s["rstd_act"], 1)
            act.wait_ge(s["prep_dve"], 2)
            act.activation(prep[:, 9, :], prep[:, 8, :], ACT.Sin)
            act.activation(prep[:, 10, :], prep[:, 8, :], ACT.Sin, scale=0.5).then_inc(s["prep_act"], 1)

            kv = kern[0:GC].rearrange("p (r m) n -> p r m n", m=2)
            for q in range(4):
                act.wait_ge(s["kern_ps"], q + 1)
                for m in range(2):
                    act.copy(kv[:, 4 * q:4 * q + 4, m, :],
                             pp[q % 2][0:GC, m, :].rearrange("p (r n) -> p r n", r=4)).then_inc(s["kern_out"], 1)
            act.wait_ge(s["u_stored"], 16 * GB)
            for q in range(4):
                act.wait_ge(s["bp_tr"], q + 1)
                for j in range(2):
                    r = 4 * q + 2 * j
                    act.copy(sum_w[:, r:r + 2], pp[2 + q % 2][:, j, :].rearrange("p (r i m) -> p r i m", r=2, i=2))\
                        .then_inc(s["bp_out"], 1)
            for q in range(4):
                act.wait_ge(s["sum_ps"], q + 1)
                for i in range(2):
                    act.copy(sums[:, i, 4 * q:4 * q + 4, :],
                             pp[q % 2][:, i, 0:4 * NC].rearrange("p (r n) -> p r n", r=4)).then_inc(s["sum_out"], 1)
            uv = u_c.rearrange("p (r m) n -> p r m n", m=2)
            for q in range(4):
                act.wait_ge(s["y_ps"], q + 1)
                for m in range(2):
                    act.copy(uv[:, 4 * q:4 * q + 4, m, :],
                             pp[2 + q % 2][:, m, 0:4 * NC].rearrange("p (r n) -> p r n", r=4))\
                        .then_inc(s["y_out_done"], 1)

            def exps(n, rows, src):
                act.wait_ge(s["neg_done"], n + 1)
                act.activation(sm[:, n % 2, 4, 0:rows], sm[:, n % 2, 4, 0:rows], ACT.Exp)
                for h in range(rows):
                    dst, x = src(h)
                    ins = act.activation(dst, x, ACT.Exp, bias=sm[:, n % 2, 2, h:h + 1], scale=SCALE,
                                         accum_out=sm[:, n % 2, 3, h:h + 1])
                ins.then_inc(s["exp_done"], 1)

            def pt_copy(n):
                act.wait_ge(s["pt_ps"], n + 1)
                if n < 2:
                    act.copy(probs_t[:, 512:1024], pp[2][:, 1, :]).then_inc(s["pt_out"], 1)
                elif n < 8:
                    act.copy(probs_t[:], pp[2][:].rearrange("p b n -> p (b n)")).then_inc(s["pt_out"], 1)
                else:
                    w = P * min(3, NB - 3 * (n - 8))
                    act.copy(probs_t[:, 0:w], pp[2][:, 0, 0:w])
                    act.copy(probs_t[0:LS, 512:512 + w], pp[2][0:LS, 1, 0:w]).then_inc(s["pt_out"], 1)

            def unit(n):
                lo = 0 if n >= 2 else P
                pr = probs[:, n % 2].rearrange("p (h n) -> p h n", h=QPK)
                return lambda h: (pr[:, h, lo:256], pr[:, h, lo:256])

            def stream(j):
                pr = probs[:, j % 2, 0:3 * NK].rearrange("p (b n) -> p b n", b=3)
                sc = pp[j % 2][:, j // 2, 0:3 * NK].rearrange("p (b n) -> p b n", b=3)
                return lambda b: (pr[:, b, :], sc[:, b, :])

            for n in range(8):
                exps(n, QPK, unit(n))
                if n >= 1:
                    pt_copy(n - 1)
                if n >= 2 and n % 2 == 0:
                    m = n // 2 - 1
                    act.wait_ge(s["av_ps"], m + 1)
                    if m >= 1:
                        act.wait_ge(s["ssq_ps"], m)
                    act.activation(rstd_row[:, 0:512], pp[3][:, 0, :], ACT.Square).then_inc(s["av_sq"], 1)
            pt_copy(7)
            act.wait_ge(s["av_ps"], 4)
            act.wait_ge(s["ssq_ps"], 3)
            act.activation(rstd_row[:, 0:512], pp[3][:, 0, :], ACT.Square).then_inc(s["av_sq"], 1)
            for j in range(3):
                exps(8 + j, min(3, NB - 3 * j), stream(j))
                if j >= 1:
                    pt_copy(7 + j)
            pt_copy(10)
            act.wait_ge(s["av_ps"], NT)
            act.wait_ge(s["ssq_ps"], NT - 1)
            act.activation(rstd_row[:, 0:512].rearrange("p (h b t) -> p b h t", h=QPK, b=NB),
                           pp[3][:, 0, :].rearrange("p (b h t) -> p b h t", b=NB, h=QPK), ACT.Square)\
                .then_inc(s["av_sq"], 1)

            act.wait_ge(s["y_in"], 16)
            act.activation(y_g, y_t, ACT.Gelu_apprx_tanh).then_inc(s["gelu_done"], 1)
            for n in range(GB):
                act.wait_ge(s["glu_ps"], n + 1)
                act.activation(mix_sq[:, n, 0:512], pp[n % 2][:, 0, :], ACT.Sigmoid, bias=b_glu[:, n:n + 1])
                act.activation(mix_sq[:, n, 512:TOK], pp[n % 2][:, 1, 0:P], ACT.Sigmoid, bias=b_glu[:, n:n + 1])\
                    .then_inc(s["sig_done"], 1)
            for n in range(GB):
                act.wait_ge(s["mix_done"], n + 1)
                act.activation(mix_sq[:, n, :], mix_t[:, n, :], ACT.Square).then_inc(s["mixsq_done"], 1)
            act.wait_ge(s["rs_done"], 1)
            act.activation(stat[:, 1:3, :], stat[:, 1:3, :], ACT.Sqrt).then_inc(s["rs_act"], 1)
            for i in range(NT):
                act.wait_ge(s["op_out"], 2 * i + 2)
                act.activation(sums_f[:, 0:D], resid[:, i, :], ACT.Square, accum_out=stat[:, 3, i:i + 1])\
                    .then_inc(s["ffn_sq"], 1)
                act.wait_ge(s["ffn_ms"], i + 1)
                act.activation(stat[:, 4, i:i + 1], stat[:, 4, i:i + 1], ACT.Sqrt).then_inc(s["ffn_sqrt"], 1)
                act.wait_ge(s["xf_tr"], i + 1)
                if i >= 2:
                    act.wait_ge(s["lg_ps"], i - 1)
                act.copy(probs[:, i % 2], pp[2][:].rearrange("p b n -> p (b n)")).then_inc(s["xf_out"], 1)
            act.wait_ge(s["lg_out"], 2)
            act.activation(le_m[:, :, 0:NEG_G], le_m[:, :, 0:NEG_G], ACT.Exp).then_inc(s["route_act"], 1)
            act.wait_ge(s["lg_out"], 3)
            act.activation(rt[:, 4, :], rt[:, 4, :], ACT.Exp).then_inc(s["route_act"], 1)

            act.wait_ge(s["pos_done"], 1)
            act.wait_ge(s["zeroed"], 16)
            gu, yp, htp = pp[0][:, 0, :], pp[0][:, 1, :], pp[1][:, 0, 0:256]
            for q in range(2):
                act.sem_inc(y_kept[q], 32)
            act.sem_inc(s["y_copied"], 1)
            left = [act.alloc_register(f"left{q}") for q in range(2)]
            for q in range(2):
                act.reg_mov(left[q], 32)
            with act.Fori(0, NE // 2) as it:
                for q in range(2):
                    e = it * 2 + q
                    first, end = tiles_of(act, e)
                    with act.Fori(first, end) as w:
                        act.wait_ge(s["gu_ready"], w + 1)
                        act.activation(act_g, gu[0:TT], ACT.Silu).then_inc(s["sg_ready"], 1)
                        act.wait_ge(s["ht_ready"], w + 1)
                        act.copy(hid_t, htp.rearrange("p (k t) -> p k t", k=KH)).then_inc(s["ht_copied"], 1)
                        act.wait_ge(s["y_ready"], w + 1)
                        act.wait_ge(y_kept[q], left[q])
                        act.reg_add(left[q], left[q], 32)
                        act.copy(y_out[q], yp).then_inc(s["y_copied"], 1)
                        act.wait_ge(s["y_copied"], w + 2)
                        for h in range(2):
                            act.dma_start(y_slots[bass.ds(w * TT, TT), 512 * h:512 * h + 512],
                                          y_out[q][TT * h:TT * h + TT]).then_inc(y_kept[q], 16)
            for q in range(2):
                act.wait_ge(y_kept[q], left[q])
            act.sem_inc(s["rows_done"], 1)
            for i in range(NT):
                act.wait_ge(s["fin_sq"], i + 1)
                act.activation(junk, resid[:, i, :], ACT.Square, accum_out=stat[:, 5, i:i + 1])\
                    .then_inc(s["fin_ms"], 1)
                act.wait_ge(s["fin_ms"], 2 * i + 2)
                act.activation(stat[:, 6, i:i + 1], stat[:, 6, i:i + 1], ACT.Sqrt).then_inc(s["fin_sqrt"], 1)

        @block.vector
        def _(dve):
            steps = [0]

            def step(ins):
                steps[0] += 1
                ins.then_inc(s["dve_step"], 1)
                dve.wait_ge(s["dve_step"], steps[0])

            tt, ts, stt = dve.tensor_tensor, dve.tensor_scalar, dve.scalar_tensor_tensor
            pv = lambda i: prep[:, i, :]

            def cmul(out, x, y, tmp):
                step(tt(tmp[0], x[0], y[0], ALU.mult))
                step(tt(tmp[1], x[1], y[1], ALU.mult))
                step(tt(out[0], tmp[0], tmp[1], ALU.subtract))
                step(tt(tmp[0], x[0], y[1], ALU.mult))
                step(tt(tmp[1], x[1], y[0], ALU.mult))
                step(tt(out[1], tmp[0], tmp[1], ALU.add))

            def unit_length(x, t0, t1):
                step(tt(t0, x[0], x[0], ALU.mult))
                step(tt(t1, x[1], x[1], ALU.mult))
                step(tt(t0, t0, t1, ALU.add))
                step(ts(t0, t0, -0.5, 1.5, ALU.mult, ALU.add))
                for c in x:
                    step(tt(c, c, t0, ALU.mult))

            dve.wait_ge(s["in_small"], 16 * (N_SMALL - 1))
            for h in range(2):
                dve.wait_ge(s["sq_done"], h + 1)
                for k in range(4 * h, 4 * h + 4):
                    ins = ts(x_t[:, k, :], x_t[:, k, :], g_mix[:, k:k + 1], None, ALU.mult)
                ins.then_inc(s["xg_done"], 1)
            dve.wait_ge(s["prep_act"], 1)
            step(tt(pv(4), pv(0), pv(3), ALU.mult))
            tt(pv(5), pv(1), pv(3), ALU.mult).then_inc(s["prep_dve"], 1)
            dve.wait_ge(s["prep_dve"], 1)
            dve.wait_ge(s["rstd_ps"], 1)
            ts(rstd_row[:, 0:SEQ], pp[2][:, 0, :], 1.0 / D, EPS, ALU.mult, ALU.add)
            ts(rstd_row[:, SEQ:TOK], pp[2][:, 1, 0:P], 1.0 / D, EPS, ALU.mult, ALU.add).then_inc(s["rstd_act"], 1)
            step(ts(pv(7), pv(5), 1.0 / (2 * np.pi), MAGIC, ALU.mult, ALU.add))
            step(ts(pv(7), pv(7), -MAGIC, None, ALU.add))
            step(stt(pv(8), pv(7), -TWO_PI[0], pv(5), ALU.mult, ALU.add))
            step(stt(pv(8), pv(7), -TWO_PI[1], pv(8), ALU.mult, ALU.add))
            step(stt(pv(8), pv(7), -TWO_PI[2], pv(8), ALU.mult, ALU.add))
            ts(pv(8), pv(8), 3.1415925, -3.1415925, ALU.min, ALU.max).then_inc(s["prep_dve"], 1)
            dve.wait_ge(s["rstd_act"], 2)
            dve.reciprocal(rstd_row[:], rstd_row[:]).then_inc(s["rstd_done"], 1)
            dve.wait_ge(s["rstd_done"], 1)

            def proj_out(n):
                dve.wait_ge(s["proj_ps"], n + 1)
                t = pp[n % 2]
                if n < GB:
                    out = u_stage[:, n].rearrange("p s n -> p n s")
                    tt(out[:, 0:NCP, :], t[:, 0, :].rearrange("p (n s) -> p n s", s=T),
                       rstd_row[:, 0:SEQ].rearrange("p (n s) -> p n s", s=T), ALU.mult)
                    tt(out[:, NCP:NC, :], t[:, 1, 0:P].rearrange("p (n s) -> p n s", s=T),
                       rstd_row[:, SEQ:TOK].rearrange("p (n s) -> p n s", s=T), ALU.mult).then_inc(s["u_out"], 1)
                    dve.wait_ge(s["u_out"], n + 1)
                else:
                    out = k_t[:] if n == GB else q_t[:, n - GB - 1, :]
                    tt(out[:, 0:SEQ], t[:, 0, :], rstd_row[:, 0:SEQ], ALU.mult)
                    step(tt(out[:, SEQ:TOK], t[:, 1, 0:P], rstd_row[:, SEQ:TOK], ALU.mult))
                dve.sem_inc(s["proj_out"], 1)

            proj_out(0)
            dve.wait_ge(s["prep_act"], 3)
            step(tt(pv(10), pv(10), pv(10), ALU.mult))
            step(ts(pv(11), pv(10), -2.0, 1.0, ALU.mult, ALU.add))
            a1 = (pw[:, 0, T - 1, :], pw[:, 1, T - 1, :])
            step(tt(a1[0], pv(6), pv(11), ALU.mult))
            step(tt(a1[1], pv(6), pv(9), ALU.mult))
            step(tt(pv(12), pv(0), pv(0), ALU.mult))
            step(tt(pv(13), pv(1), pv(1), ALU.mult))
            step(tt(pv(12), pv(12), pv(13), ALU.add))
            step(dve.reciprocal(pv(13), pv(12)))
            step(ts(pv(14), a1[0], -1.0, None, ALU.add))
            step(tt(pv(15), pv(14), pv(0), ALU.mult))
            step(tt(pv(16), a1[1], pv(1), ALU.mult))
            step(tt(pv(15), pv(15), pv(16), ALU.add))
            step(tt(pv(16), a1[1], pv(0), ALU.mult))
            step(tt(pv(17), pv(14), pv(1), ALU.mult))
            step(tt(pv(16), pv(16), pv(17), ALU.subtract))
            step(tt(pv(15), pv(15), pv(13), ALU.mult))
            step(tt(pv(16), pv(16), pv(13), ALU.mult))
            proj_out(1)
            power = lambda n: (pw[:, 0, T - n, :], pw[:, 1, T - n, :])
            for n, (x, y) in {2: (1, 1), 3: (2, 1), 4: (2, 2), 5: (4, 1), 6: (4, 2), 7: (4, 3), 8: (4, 4)}.items():
                cmul(power(n), power(x), power(y), (pv(12), pv(14)))
            f = [pv(15 + i).unsqueeze(2).to_broadcast([P, R, GC]) for i in range(2)]
            c1 = probs[:, 1, 0:256].rearrange("p (r c) -> p r c", r=R)
            c2 = probs[:, 1, 256:512].rearrange("p (r c) -> p r c", r=R)
            cmul((bbar[:, 0], bbar[:, 1]), (ssm_b[:, 0], ssm_b[:, 1]), f, (c1, c2))
            step(dve.tensor_copy(pv(18), pv(11)))
            step(dve.tensor_copy(pv(19), pv(9)))
            unit_length((pv(18), pv(19)), pv(12), pv(14))
            for n in range(3):
                src, dst = ((pv(18), pv(19)), (pv(12), pv(14)))
                cmul(dst, src, src, (pv(13), pv(17)))
                step(dve.tensor_copy(pv(18), pv(12)))
                step(dve.tensor_copy(pv(19), pv(14)))
                step(tt(pv(6), pv(6), pv(6), ALU.mult))
            unit_length((pv(18), pv(19)), pv(12), pv(14))
            dve.sem_inc(s["bbar_done"], 1)
            proj_out(2)
            proj_out(3)
            step(ts(ssm_c[:, 1], ssm_c[:, 1], -1.0, None, ALU.mult))
            cr, ci = ssm_c[:, 0], ssm_c[:, 1]
            for t in range(T):
                ar, ai = [x.unsqueeze(2).to_broadcast([P, R, GC]) for x in power(t + 1)]
                tt(c1, cr, ar, ALU.mult)
                step(tt(c2, ci, ai, ALU.mult))
                step(tt(out_tab[:, :, 0, t, :], c1, c2, ALU.add))
                tt(c1, ci, ar, ALU.mult)
                step(tt(c2, cr, ai, ALU.mult))
                step(tt(out_tab[:, :, 1, t, :], c1, c2, ALU.subtract))
                if t % 2 and 4 + t // 2 < 9:
                    proj_out(4 + t // 2)
            dve.sem_inc(s["out_tab_done"], 1)
            proj_out(8)
            dve.wait_ge(s["stat_cols"], 1)
            step(dve.tensor_copy(stat[:, 0, :], pp[3][:, 1, 0:NT]))
            for i in range(NT):
                dve.wait_ge(s["kv_ps"], i + 1)
                ts(kv_row[:, i, :], pp[2 + i % 2][:, 0, 0:256], stat[:, 0, i:i + 1], None, ALU.mult)\
                    .then_inc(s["kv_out"], 1)
            dve.wait_ge(s["zeroed"], 16)
            skip_b = skip[:].unsqueeze(2).to_broadcast([GC, G, GC])
            step(tt(skip_tmp, skip_b, ident[0:GC, 0:GC].unsqueeze(1).to_broadcast([GC, G, GC]), ALU.mult))
            dve.memset(conv_w, 0.0).then_inc(s["conv_zero"], 1)
            dve.wait_ge(s["kern_out"], 8)
            tt(kern[0:GC, :, 0:GC], kern[0:GC, :, 0:GC], skip_tmp, ALU.add).then_inc(s["kern_done"], 1)
            dve.wait_ge(s["in_attn"], 32)
            dve.tensor_copy(kd_t[:, :, WIN:NK], k_t[:, SEQ:TOK].rearrange("p (b t) -> p b t", b=NB))
            dve.wait_ge(s["attn_z"], 1)
            for v in range(NKV):
                rows = slice(HD * v, HD * v + HD)
                ins = dve.tensor_copy(q_z[rows, :, v, :, :],
                                      q_t[rows, :, SEQ:TOK].rearrange("p h (b t) -> p b h t", b=NB))
            step(ins)

            dve.wait_ge(s["rot_ready"], 1)
            dve.wait_ge(s["conv_in"], 16 * T)
            dve.wait_ge(s["sum_out"], 8)
            sr, si = sums[:, 0, :, 0:NCP], sums[:, 1, :, 0:NCP]
            wr, wi = rot
            t0, t1, t2, t3 = rot_tmp
            dve.tensor_copy(t3, pv(6).unsqueeze(2).to_broadcast([P, R, NCP]))
            tt(t0, sr, wr, ALU.mult)
            step(tt(t1, si, wi, ALU.mult))
            step(tt(roll[0], t0, t1, ALU.add))
            step(dve.memset(t3[:, :, 0:1], 0.0))
            tt(t0, si, wr, ALU.mult)
            step(tt(t1, sr, wi, ALU.mult))
            step(tt(roll[1], t0, t1, ALU.subtract))
            fl = lambda x: x.rearrange("p r n -> p (r n)")
            for i in range(2):
                dve.tensor_tensor_scan(fl(rot_tmp[i]), fl(t3), fl(roll[i]), 0.0, ALU.mult, ALU.add)
            step(dve.memset(states[:, :, :, 0:1], 0.0))
            tt(roll[0], t0, wr, ALU.mult)
            step(tt(roll[1], t1, wi, ALU.mult))
            tt(states[:, :, 0, 1:NCP], roll[0][:, :, 0:NCP - 1], roll[1][:, :, 0:NCP - 1], ALU.subtract)
            step(tt(h_last[:, 0], roll[0][:, :, NCP - 1], roll[1][:, :, NCP - 1], ALU.subtract))
            tt(roll[0], t0, wi, ALU.mult)
            step(tt(roll[1], t1, wr, ALU.mult))
            tt(h_last[:, 1], roll[0][:, :, NCP - 1], roll[1][:, :, NCP - 1], ALU.add)
            tt(states[:, :, 1, 1:NCP], roll[0][:, :, 0:NCP - 1], roll[1][:, :, 0:NCP - 1], ALU.add)\
                .then_inc(s["states_done"], 1)

            def before_exp(n, rows, src, sink):
                mx, m, neg, es = [sm[:, n % 2, i, 0:rows] for i in (0, 1, 2, 4)]
                step(dve.tensor_reduce(mx, src, AX.X, ALU.max))
                if sink is None:
                    step(ts(m, mx, SCALE, sink_d, ALU.mult, ALU.max))
                    step(ts(es, m, -1.0, sink_d, ALU.mult, ALU.add))
                else:
                    step(stt(m, mx, SCALE, sink, ALU.mult, ALU.max))
                    step(tt(es, sink, m, ALU.subtract))
                ts(neg, m, -1.0, None, ALU.mult).then_inc(s["neg_done"], 1)

            def after_exp(n, rows, view):
                dve.wait_ge(s["exp_done"], n + 1)
                total, es, rd = [sm[:, n % 2, i, 0:rows] for i in (3, 4, 5)]
                step(tt(total, total, es, ALU.add))
                step(dve.reciprocal(rd, total))
                for h in range(rows):
                    ins = ts(view(h), view(h), rd[:, h:h + 1], None, ALU.mult)
                ins.then_inc(s["norm_done"], 1)

            def masked(n):
                m, v = n // 2, n % 2
                lo = 0 if m else P
                pr = probs[:, v].rearrange("p (h n) -> p h n", h=QPK)[:, :, lo:256]
                sc = pp[v][:].rearrange("p b (h n) -> p (b h) n", h=2)[:, :, lo:256]
                dve.wait_ge(s["sc_ps"], n + 1)
                if n >= 2:
                    dve.wait_ge(s["pt_ps"], n - 1)
                tt(pr, sc, mask[:, lo:256].unsqueeze(1).to_broadcast([P, QPK, 256 - lo]), ALU.add)\
                    .then_inc(s["sc_read"], 1)
                dve.wait_ge(s["sc_read"], n + 1)
                before_exp(n, QPK, pr, sink_row[:, QPK * v:QPK * v + QPK])

            def unit_out(n):
                lo = 0 if n >= 2 else P
                pr = probs[:, n % 2].rearrange("p (h n) -> p h n", h=QPK)
                after_exp(n, QPK, lambda h: pr[:, h, lo:256])

            def attn_out(m):
                dve.wait_ge(s["av_sq"], m + 1)
                src = pp[3][:, 0, :]
                if m < NT - 1:
                    dst = attn_t[:, :, P * m:P * m + P]
                    ins = tt(dst, src.rearrange("p (h t) -> p h t", h=QPK),
                       g_attn.unsqueeze(2).to_broadcast([P, QPK, P]), ALU.mult)
                else:
                    for h in range(QPK):
                        ins = ts(attn_t[:, h, SEQ:TOK].rearrange("p (b t) -> p b t", b=NB),
                           src.rearrange("p (b h t) -> p b h t", b=NB, h=QPK)[:, :, h, :],
                           g_attn[:, h:h + 1], None, ALU.mult)
                ins.then_inc(s["attn_done"], 1)

            masked(0)
            for n in range(8):
                if n + 1 < 8:
                    masked(n + 1)
                unit_out(n)
                if n % 2 == 0 and n >= 2:
                    attn_out(n // 2 - 1)
            attn_out(3)
            for j in range(3):
                nb = min(3, NB - 3 * j)
                n = 8 + j
                dve.wait_ge(s["sc_ps"], n + 1)
                sc = pp[j % 2][:, j // 2, 0:nb * NK].rearrange("p (b n) -> p b n", b=nb)
                dve.wait_ge(s["pt_ps"], n - 1)
                before_exp(n, nb, sc, None)
                pr = probs[:, j % 2, 0:3 * NK].rearrange("p (b n) -> p b n", b=3)
                after_exp(n, nb, lambda b: pr[:, b, :])
            attn_out(NT - 1)

            for n in range(GB):
                dve.wait_ge(s["sig_done"], n + 1)
                tt(mix_t[:, n, :].rearrange("p (n t) -> p t n", t=T), y_g[:, n, :].rearrange("p (t n) -> p t n", t=T),
                   mix_sq[:, n, :].rearrange("p (t n) -> p t n", t=T), ALU.mult).then_inc(s["mix_done"], 1)
            for n in range(GB):
                dve.wait_ge(s["mixsq_done"], n + 1)
                ins = ts(mix_t[:, n, :], mix_t[:, n, :], g_ssm[:, n:n + 1], None, ALU.mult)
            ins.then_inc(s["mix_done"], 1)
            dve.wait_ge(s["ssq_ps"], NT + 1)
            ts(stat[:, 1:3, :], pp[3][:, 1, 0:2 * NT].rearrange("p (m i) -> p m i", m=2), 1.0 / W, EPS,
               ALU.mult, ALU.add).then_inc(s["rs_done"], 1)
            dve.wait_ge(s["rs_act"], 1)
            step(dve.reciprocal(stat[:, 1:3, :], stat[:, 1:3, :]))

            def ffn_norm(i):
                dve.wait_ge(s["ffn_sq"], i + 1)
                ts(stat[:, 4, i:i + 1], stat[:, 3, i:i + 1], 1.0 / D, EPS, ALU.mult, ALU.add).then_inc(s["ffn_ms"], 1)
                dve.wait_ge(s["ffn_sqrt"], i + 1)
                step(dve.reciprocal(stat[:, 4, i:i + 1], stat[:, 4, i:i + 1]))
                stt(ffn_in[:, i, :], resid[:, i, :], stat[:, 4, i:i + 1], g_ffn[:], ALU.mult, ALU.mult)\
                    .then_inc(s["ffn_done"], 1)

            dve.wait_ge(s["in_resid"], 16)
            dve.wait_ge(s["in_rows"], 48)
            for i in range(NT):
                for m in range(2):
                    dve.wait_ge(s["op_ps"], 2 * i + m + 1)
                    stt(resid[:, i, :], pp[m][:].rearrange("p b n -> p (b n)"), stat[:, 1 + m, i:i + 1],
                        resid[:, i, :], ALU.mult, ALU.add).then_inc(s["op_out"], 1)
                    dve.wait_ge(s["op_out"], 2 * i + m + 1)
                ffn_norm(i)
            dve.wait_ge(s["lg_ps"], NT)
            lg = pp[3][:, 0, 0:NT * NR].rearrange("p (i n) -> p i n", i=NT)
            step(tt(logit, lg, b_r[:].unsqueeze(1).to_broadcast([P, NT, NR]), ALU.add))

            bc = lambda x, n: x.unsqueeze(2).to_broadcast([P, NT, n])
            experts = lambda: iota_e[:].unsqueeze(1).to_broadcast([P, NT, NE])
            step(dve.tensor_copy(pad8[:, :, 0:NEG_G], logit[:, :, 0:NEG_G]))
            for i in range(NT):
                ins = dve.max(top_g[:, i, :], pad8[:, i, :])
            step(ins)
            for i in range(NT):
                ins = dve.max_index(ig[:, i, :], top_g[:, i, :], pad8[:, i, :])
            ins.then_inc(s["lg_out"], 1)
            dve.wait_ge(s["lg_out"], 1)
            tt(le_m[:, :, 0:NEG_G], logit[:, :, 0:NEG_G], bc(top_g[:, :, 0], NEG_G), ALU.subtract)\
                .then_inc(s["lg_out"], 1)
            step(dve.tensor_copy(rt[:, 0, :], ig[:, :, 0]))
            step(tt(one_g, iota_e[:, 0:NEG_G].unsqueeze(1).to_broadcast([P, NT, NEG_G]), bc(rt[:, 0, :], NEG_G),
                    ALU.is_equal))
            dve.wait_ge(s["route_act"], 1)
            step(dve.tensor_reduce(rt[:, 1, :], le_m[:, :, 0:NEG_G], AX.X, ALU.add))
            step(tt(le_m.rearrange("p i (g e) -> p i g e", g=NEG_G),
                    logit[:, :, NEG_G:NR].rearrange("p i (g e) -> p i g e", g=NEG_G),
                    one_g.unsqueeze(3).to_broadcast([P, NT, NEG_G, EPG]), ALU.mult))
            step(dve.tensor_reduce(le_g, le_m.rearrange("p i (g e) -> p i e g", g=NEG_G), AX.X, ALU.add))
            for i in range(NT):
                ins = dve.max(top_e[:, i, :], le_g[:, i, :])
            step(ins)
            for i in range(NT):
                ins = dve.max_index(ie[:, i, :], top_e[:, i, :], le_g[:, i, :])
            step(ins)
            tt(rt[:, 4, :], top_e[:, :, 1], top_e[:, :, 0], ALU.subtract).then_inc(s["lg_out"], 1)
            for k in range(2):
                step(dve.tensor_copy(rt[:, 2 + k, :], ie[:, :, k]))
                step(stt(rt[:, 2 + k, :], rt[:, 0, :], float(EPG), rt[:, 2 + k, :], ALU.mult, ALU.add))
                step(tt(pair[:, k], experts(), bc(rt[:, 2 + k, :], NE), ALU.is_equal))
            tt(both, pair[:, 0], pair[:, 1], ALU.add).then_inc(s["pair_done"], 1)
            dve.wait_ge(s["route_act"], 2)
            step(ts(rt[:, 5, :], rt[:, 4, :], 1.0, None, ALU.add))
            step(tt(rt[:, 5, :], rt[:, 5, :], rt[:, 1, :], ALU.mult))
            step(dve.reciprocal(rt[:, 6, :], rt[:, 5, :]))
            step(tt(rt[:, 7, :], rt[:, 6, :], rt[:, 4, :], ALU.mult))
            dve.wait_ge(s["place_ps"], 1)
            pl = pp[3][:, 1, 0:NT * NE].rearrange("p (i e) -> p i e", i=NT)
            step(stt(place, pl, 1.0, both, ALU.add, ALU.mult))
            step(ts(place_e.rearrange("p e i -> p i e"), place, -1.0, None, ALU.add))
            step(ts(ntile[:, 0, :], pp[3][:, 1, 256:256 + NE], 1.0 / TT, (TT - 1) / (2.0 * TT), ALU.mult, ALU.add))
            step(ts(ntile[:, 0, :], ntile[:, 0, :], MAGIC, None, ALU.add))
            step(ts(ntile[:, 0, :], ntile[:, 0, :], -MAGIC, 1.0, ALU.add, ALU.max))
            step(dve.memset(first_f[:, 0:1], 0.0))
            step(dve.tensor_tensor_scan(first_f[:, 1:NE + 1], ones[:, 0:NE], ntile[:, 0, :], 0.0, ALU.mult, ALU.add))
            step(ts(ntile[:, 1, :], first_f[:, 0:NE], float(TT), None, ALU.mult))
            step(tt(place, pl, ntile[:, 1, :].unsqueeze(1).to_broadcast([P, NT, NE]), ALU.add))
            for k in range(2):
                step(tt(ptmp[:, k], place, pair[:, k], ALU.mult))
                step(dve.tensor_reduce(rt[:, 8 + k, :], ptmp[:, k], AX.X, ALU.add))
                step(dve.tensor_copy(pos_u[:, k, :], rt[:, 8 + k, :]))
            dve.tensor_copy(first_i[:], first_f[0:1, :]).then_inc(s["pos_done"], 1)
            dve.wait_ge(s["pos_done"], 1)

            gu, gx, xtp = pp[0][:, 0, :], pp[2][:, 0, :], pp[2][:, 1, :]

            def keep_x(w1):
                dve.wait_ge(s["gx_ready"], w1 + 1)
                dve.tensor_copy(xrow, gx).then_inc(s["gx_copied"], 1)

            def keep_xt(w1):
                dve.wait_ge(s["xt_ready"], w1)
                dve.tensor_copy(xt_e, xtp.rearrange("p (c n) -> p c n", c=4)).then_inc(s["xt_copied"], 1)

            def select(w1):
                dve.wait_ge(s["place_ready"], w1)
                dve.wait_ge(s["gx_ready"], w1)
                for i in range(NT):
                    ins = ts(sel[:, i, :], iota_t[:], place_c[:, i:i + 1], None, ALU.is_equal)
                ins.then_inc(s["sel_ready"], 1)

            dve.sem_inc(s["gx_ready"], 1)
            select(1)
            keep_x(1)
            keep_xt(1)
            with dve.Fori(0, NE) as e:
                first, end = tiles_of(dve, e)
                with dve.Fori(first, end) as w:
                    select(w + 2)
                    dve.wait_ge(s["sg_ready"], w + 1)
                    tt(hid, gu[TT:P], act_g, ALU.mult).then_inc(s["h_ready"], 1)
                    keep_x(w + 2)
                    keep_xt(w + 2)

            for i in range(NT):
                dve.wait_ge(got_in[i % 2], 32 * (i // 2 + 1))
                for k in range(2):
                    ins = stt(resid[:, i, :], got[i % 2][k], rt[:, 6 + k, i:i + 1], resid[:, i, :], ALU.mult, ALU.add)
                    if k == 0:
                        step(ins)
                ins.then_inc(s["fin_sq"], 1)
                dve.wait_ge(s["fin_ms"], 2 * i + 1)
                ts(stat[:, 6, i:i + 1], stat[:, 5, i:i + 1], 1.0 / D, EPS, ALU.mult, ALU.add).then_inc(s["fin_ms"], 1)
                dve.wait_ge(s["fin_sqrt"], i + 1)
                step(dve.reciprocal(stat[:, 6, i:i + 1], stat[:, 6, i:i + 1]))
                if i >= 2:
                    dve.wait_ge(fin_out[i % 2], 16 * (i // 2))
                stt(fin[i % 2], resid[:, i, :], stat[:, 6, i:i + 1], g_fin[:], ALU.mult, ALU.mult)\
                    .then_inc(s["fin_done"], 1)


def _layout(x):
    c = np.ascontiguousarray
    pairs = lambda v: v.reshape(R, 2, NS, *v.shape[2:]).transpose(1, 2, 0, *range(3, v.ndim + 1)).reshape(
        P, R, *v.shape[2:])
    rows = np.concatenate([x["x_prompt"].reshape(SEQ, D), x["x_sample"].reshape(NB * LS, D)], 0)
    w_in = x["w_in"][0]
    q = w_in[:, 0:W].reshape(D, NKV, QPK, HD).transpose(0, 2, 1, 3).reshape(D, W)
    w_out = x["w_out"][0]
    ssm_o = w_out[W:].reshape(GB, P, D).transpose(1, 0, 2)
    att_o = w_out[0:W].reshape(NKV, QPK, HD, D).transpose(0, 2, 1, 3).reshape(P, QPK, D)
    ck = x["cache_k"][0]
    return {
        "x_rows": c(rows),
        "x_t": c(rows.T.reshape(P, KD, TOK)),
        "w_in": c(np.concatenate([q, w_in[:, W:]], 1)),
        "w_out": c(np.concatenate([att_o, ssm_o], 1)),
        "w_glu": c(x["w_glu"][0]),
        "cache_k_t": c(ck.transpose(2, 3, 0, 1).reshape(P, NB, WIN)),
        "cache_k": c(ck.reshape(NB, WIN, P)),
        "cache_v": c(x["cache_v"][0].reshape(NB, WIN, P)),
        "g_norm_mix": c(x["g_norm_mix"][0].reshape(P, KD)),
        "g_attn": c(x["g_attn_out"][0].reshape(NKV, QPK, HD).transpose(0, 2, 1).reshape(P, QPK)),
        "g_ssm": c(x["g_ssm_out"][0].reshape(GB, P).T),
        "b_glu": c(x["b_glu"][0].reshape(GB, P).T),
        "g_norm_ffn": c(x["g_norm_ffn"]),
        "g_final": c(x["g_final"][None]),
        "sinks": c(x["attn_sinks"]),
        "sink_rows": c(np.repeat(x["attn_sinks"][0], LS)[:, None]),
        "ssm_d": c(x["ssm_d"][0].reshape(G, GC).T),
        "w_router": c(np.concatenate([x["w_router_group"][0], x["w_router_expert"][0]], 1)),
        "b_router": c(np.concatenate([x["b_router_group"], x["b_router_expert"]], 1)),
        "ssm_b": c(np.stack([pairs(x["ssm_b_re"][0]), pairs(x["ssm_b_im"][0])], 1)),
        "ssm_c": c(np.stack([pairs(x[n][0].transpose(0, 2, 1)) for n in ("ssm_c_re", "ssm_c_im")], 1)),
        "h0": c(np.stack([pairs(x[n][0].transpose(1, 2, 0)) for n in ("state_ssm_re", "state_ssm_im")], 1)),
        "a_re": c(pairs(x["ssm_a_re"][0])),
        "a_im": c(pairs(x["ssm_a_im"][0])),
        "log_dt": c(x["ssm_log_dt"][0].reshape(R, 2).T),
        "w_exp_gate": c(x["w_exp_gate"][0]),
        "w_exp_up": c(x["w_exp_up"][0]),
        "w_exp_down": c(x["w_exp_down"][0]),
    }


_OUTS = {
    "y": (TOK, D), "new_k_prompt": (WIN, P), "new_v_prompt": (WIN, P),
    "new_k_sample": (NB, WIN, P), "new_v_sample": (NB, WIN, P),
    "state_prompt": (P, 2, R), "state_sample": (P, 2, R, NB),
}


def kernel(**inputs):
    import concourse.bacc as _bacc
    from concourse.bass_utils import run_bass_kernel_spmd as _run

    arrays = _layout({k: np.asarray(v) for k, v in inputs.items()})
    nc = _bacc.Bacc("TRN2", target_bir_lowering=False, num_devices=1)
    a = {n: nc.dram_tensor(f"in_{n}", v.shape, mybir.dt.from_np(v.dtype), kind="ExternalInput").ap()
         for n, v in arrays.items()}
    o = {n: nc.dram_tensor(f"out_{n}", shape, F32, kind="ExternalOutput").ap() for n, shape in _OUTS.items()}
    build(nc, a, o)
    got = _run(nc, [{f"in_{n}": v for n, v in arrays.items()}], core_ids=[0]).results[0]
    got = {n: got[f"out_{n}"] for n in _OUTS}
    y = got["y"]
    states = lambda v, i: np.ascontiguousarray(v[:, i].reshape(2, NS, R, -1).transpose(3, 2, 0, 1)).reshape(
        1, -1, G, NS)
    heads = lambda v: v.reshape(1, -1, WIN, NKV, HD)
    return (y[0:SEQ].reshape(1, SEQ, D), y[SEQ:].reshape(NB, LS, D),
            heads(got["new_k_prompt"]), heads(got["new_v_prompt"]),
            states(got["state_prompt"], 0), states(got["state_prompt"], 1),
            heads(got["new_k_sample"]), heads(got["new_v_sample"]),
            states(got["state_sample"], 0), states(got["state_sample"], 1))
```

```python
from contextlib import ExitStack

import numpy as np

import concourse.bass as bass
from concourse import mybir

F32 = mybir.dt.float32
I32 = mybir.dt.int32
U32 = mybir.dt.uint32
ALU = mybir.AluOpType
ACT = mybir.ActivationFunctionType
AX = mybir.AxisListType

P = 128
D = 1024
SEQ = 512
NB, LS = 8, 16
TOK = SEQ + NB * LS
NT = TOK // P
KD = D // P
HD = 64
NKV, QPK = 2, 4
WIN = 128
NK = WIN + LS
G, GC, NS = 32, 16, 64
R = G // 2
T = 8
NC = TOK // T
NCP = SEQ // T
W = 512
GB = W // P
PROJ = 1280
NE, NEG_G, EPG, DE = 32, 4, 8, 512
NR = NEG_G + NE
TT = 64
KH = DE // P
TILES_MAX = 2 * TOK // TT + NE
SLOTS = TILES_MAX * TT
EPS = 1e-6
SCALE = HD ** -0.5
SSM_FROM = 2
TABLES = 2 * R + 4 * R * GC + 2 * R * NB
MASKED = -1e30
MAGIC = 1.5 * 2.0 ** 23
TWO_PI = (6.28125, 0.0019350051879882812, 3.019916050561733e-07)


def build(nc, a, o):
    with ExitStack() as ctx:
        def sb(name, shape, dt=F32):
            return ctx.enter_context(nc.sbuf_tensor(name, shape, dt))

        def sem(name):
            return ctx.enter_context(nc.semaphore(name))

        slot = [sb(f"slot{i}", [P, 12288]) for i in range(2)]
        reg_x = sb("reg_x", [P, 5120])
        reg_f = sb("reg_f", [P, 5120])
        reg_h = sb("reg_h", [P, 5120])

        gate_w = [s[:, 0:4096].rearrange("p (h c n) -> p h c n", h=2, c=4) for s in slot]
        up_w = [s[:, 4096:8192].rearrange("p (h c n) -> p h c n", h=2, c=4) for s in slot]
        down_w = [s[:, 8192:12288].rearrange("p (k n) -> p k n", k=KH) for s in slot]

        sum_w = slot[0][:, 0:4096].rearrange("p (r i m) -> p r i m", r=R, i=2)
        conv_w = slot[0][:, 4096:8192].rearrange("p (g m) -> p g m", g=G)
        out_tab = slot[0][:, 8192:12288].rearrange("p (r i t c) -> p r i t c", r=R, i=2, t=T)
        u_stage = slot[0][:, 0:2560].rearrange("p (b s n) -> p b s n", b=GB, s=T)
        rot_tmp = [slot[0][:, 1024 * i:1024 * i + 1024].rearrange("p (r n) -> p r n", r=R)
                   for i in range(3)]
        w_u = slot[1][:, 0:4096].rearrange("p (k n) -> p k n", k=KD)
        w_qkv = slot[1][:, 4096:10240].rearrange("p (k n) -> p k n", k=KD)
        w_out = slot[1][:, 0:8192].rearrange("p (k n) -> p k n", k=KD)
        w_glu = slot[1][:, 8192:10240].rearrange("p (k n) -> p k n", k=GB)
        rot = [slot[1][:, 10240 + 1024 * i:11264 + 1024 * i].rearrange("p (r n) -> p r n", r=R)
               for i in range(2)]
        kern = slot[1][:, 0:4096].rearrange("p (g m) -> p g m", g=G)
        skip_tmp = slot[1][0:GC, 4096:4608].rearrange("p (g c) -> p g c", g=G)
        decay = slot[1][:, 5120:6144].rearrange("p (r n) -> p r n", r=R)
        x_t = reg_h[:].rearrange("p (k t) -> p k t", k=KD)
        attn_t = reg_h[:, 0:2560].rearrange("p (h t) -> p h t", h=QPK)
        y_t = reg_h[:, 2560:5120].rearrange("p (b t) -> p b t", b=GB)
        mix_t = y_t
        roll = [reg_h[:, 2560 + 1024 * i:3584 + 1024 * i].rearrange("p (r n) -> p r n", r=R) for i in range(2)]
        x_sq = reg_x[:].rearrange("p (k t) -> p k t", k=KD)
        u_c = reg_x[:, 0:2560].rearrange("p (g n) -> p g n", g=G)
        y_g = reg_x[:, 0:2560].rearrange("p (b t) -> p b t", b=GB)
        states = reg_x[:, 2560:5120].rearrange("p (r i n) -> p r i n", r=R, i=2)
        mix_sq = reg_x[:, 2560:5120].rearrange("p (b t) -> p b t", b=GB)
        ffn_in = reg_x[:].rearrange("p (i n) -> p i n", i=NT)
        q_t = reg_f[:, 0:2560].rearrange("p (h t) -> p h t", h=QPK)
        kd_t = reg_f[:, 2560:3712].rearrange("p (b n) -> p b n", b=NB)
        v_old = reg_f[:, 3712:4736].rearrange("p (b n) -> p b n", b=NB)
        resid = reg_f[:].rearrange("p (i n) -> p i n", i=NT)

        k_t = sb("k_t", [P, TOK])
        kv_row = sb("kv_row", [P, NT, 256])
        sums = sb("sums", [P, 2, R, NC])
        v_new = sums[0:LS, 0].rearrange("p r n -> p (r n)")[:, 0:NB * P].rearrange("p (b n) -> p b n", b=NB)
        rstd_row = sb("rstd_row", [P, TOK])
        probs = sb("probs", [P, 2, 1024])
        probs_t = sb("probs_t", [P, 1024])
        bp_buf = sb("bp_buf", [P, 1024])
        bp = bp_buf[:].rearrange("p (r i s c) -> p r i s c", r=4, i=2, s=T)
        q_z = bp_buf[:].rearrange("p (b v h t) -> p b v h t", b=NB, v=NKV, h=QPK)
        tables = sb("tables", [P, TABLES])
        a_re, a_im = tables[:, 0:R], tables[:, R:2 * R]
        ssm_b, ssm_c = [tables[:, 2 * R + 2 * R * GC * n:2 * R + 2 * R * GC * (n + 1)]
                        .rearrange("p (i r c) -> p i r c", i=2, r=R) for n in range(2)]
        h0 = tables[:, 2 * R + 4 * R * GC:TABLES].rearrange("p (i r b) -> p i r b", i=2, r=R)
        bbar = sb("bbar", [P, 2, R, GC])
        pw = sb("pw", [P, 2, T, R])
        prep = sb("prep", [P, 32, R])
        h_last = sb("h_last", [P, 2, R])
        h_dec = sb("h_dec", [P, 2, R, NB])
        dec_tmp = bp_buf[:, 0:512].rearrange("p (i r b) -> p i r b", i=4, r=R)
        mask = reg_f[:, 4736:4992]
        ident = sb("ident", [P, P])
        ones = sb("ones", [P, P])
        before = sb("before", [P, P])
        cols = sb("cols", [P, 21])
        g_mix = cols[:, 0:8]
        g_attn = cols[:, 8:12]
        g_ssm = cols[:, 12:16]
        b_glu = cols[:, 16:20]
        sink_d = cols[:, 20:21]
        sink_row = sb("sink_row", [P, 8])
        skip = sb("skip", [GC, G])
        w_r = tables[:, 2 * R:2 * R + KD * NR].rearrange("p (k n) -> p k n", k=KD)
        b_r = sb("b_r", [P, NR])
        sm = sb("sm", [P, 2, 6, 4])
        stat = sb("stat", [P, 8, NT])
        g_ffn = probs_t
        g_fin = bp_buf
        kv_f = kv_row[:].rearrange("p i n -> p (i n)")
        pair = kv_f[:, 0:320].rearrange("p (k i e) -> p k i e", k=2, i=NT)
        ptmp = kv_f[:, 320:640].rearrange("p (k i e) -> p k i e", k=2, i=NT)
        both, place, le_m = [kv_f[:, 640 + 160 * n:800 + 160 * n].rearrange("p (i e) -> p i e", i=NT)
                             for n in range(3)]
        le_g, top_g, top_e = [kv_f[:, 1120 + 40 * n:1160 + 40 * n].rearrange("p (i e) -> p i e", i=NT)
                              for n in range(3)]
        one_g = kv_f[:, 1240:1260].rearrange("p (i e) -> p i e", i=NT)
        place_e = rstd_row[:, 0:160].rearrange("p (e i) -> p e i", e=NE)
        logit = rstd_row[:, 160:340].rearrange("p (i n) -> p i n", i=NT)
        pad8 = sb("pad8", [P, NT, 8])
        ig = sb("ig", [P, NT, 8], U32)
        ie = sb("ie", [P, NT, 8], U32)
        iota_e = sb("iota_e", [P, NE])
        iota_t = sb("iota_t", [P, TT])
        tile_tt = sb("tile_tt", [P, NT])
        zero_nt = sb("zero_nt", [P, NT])
        rt = sb("rt", [P, 12, NT])
        pos_u = sb("pos_u", [P, 2, NT], U32)
        ntile = sb("ntile", [P, 3, NE])
        first_f = sb("first_f", [P, NE + 1])
        first_i = sb("first_i", [1, NE + 1], I32)

        xrow = probs[:, 0, 0:512]
        xt_e = probs[:, 0, 512:1024].rearrange("p (c n) -> p c n", c=4)
        act_g = probs[0:TT, 1, 0:512]
        hid = probs[0:TT, 1, 512:1024]
        sums_f = sums[:].rearrange("p i r n -> p (i r n)")
        hid_t = sums_f[:, 0:256].rearrange("p (k t) -> p k t", k=KH)
        y_out = [sums_f[:, 256 + 512 * i:768 + 512 * i] for i in range(2)]
        sel = sums_f[:, 1280:1600].rearrange("p (i s) -> p i s", i=NT)
        place_b = sums_f[:, 1600:1605]
        place_c = sums_f[:, 1608:1613]
        got = [[slot[i][:, 1024 * k:1024 * k + 1024] for k in range(2)] for i in range(2)]
        fin = [slot[i][:, 2048:3072] for i in range(2)]
        junk = slot[0][:, 4096:5120]

        pp = [ctx.enter_context(nc.psum_tensor(f"pair{i}", [P, 2, 512], F32)) for i in range(4)]

        u_scr = nc.dram_tensor("u_scr", [W, T, NC], F32).ap()
        y_scr = nc.dram_tensor("y_scr", [W, T, NC], F32).ap()
        y_slots = nc.dram_tensor("y_slots", [SLOTS, D], F32).ap()

        names = """in_cols in_tables in_small in_x0 in_x1 in_w_u in_w_qkv cols_read decay_used streams_ready in_attn in_kv out_w in_resid in_rows
            const_done dve_step pool_step act_step sq_done rstd_ps rstd_act rstd_done xg_done proj_ps proj_out
            kv_ps kv_out tr_ps stat_cols u_out u_stored u_in prep_act prep_dve bbar_done bp_ready bp_tr bp_out
            out_tab_done kern_ps kern_out conv_zero kern_done conv_in sum_ps sum_out rot_done states_done
            y_ps y_out_done y_stored y_in gelu_done glu_ps sig_done mix_done mixsq_done
            sc_ps neg_done exp_done norm_done pt_ps pt_out av_ps av_sq attn_done attn_z
            vnew_in states_out cache_out ssq_ps ssq_out rs_act rs_done op_ps op_out rsf_act ffn_sq ffn_done
            xf_tr xf_out lg_ps lg_out route_act pair_done place_ps pos_done
            gate_in0 gate_in1 up_in0 up_in1 down_in0 down_in1 sel_ready gx_ready gx_copied xt_ready xt_copied
            gu_ready sg_ready h_ready ht_ready ht_copied y_ready y_copied y_kept0 y_kept1
            got0 got1 zero_ready zeroed fin_sq fin_ms fin_sqrt fin_done sc_read base_step place_ready rows_done stat_ready skip_ready ssq_read rot_ready ffn_ms ffn_sqrt rsf_ms op_read fin_out0 fin_out1""".split()
        s = {n: sem(n) for n in names}
        gate_in = [s["gate_in0"], s["gate_in1"]]
        up_in = [s["up_in0"], s["up_in1"]]
        down_in = [s["down_in0"], s["down_in1"]]
        y_kept = [s["y_kept0"], s["y_kept1"]]
        got_in = [s["got0"], s["got1"]]
        fin_out = [s["fin_out0"], s["fin_out1"]]

        block = ctx.enter_context(nc.Block())

        def tiles_of(eng, e):
            first = eng.value_load(first_i[0:1, bass.ds(e, 1)], min_val=0, max_val=TILES_MAX - 1)
            end = eng.value_load(first_i[0:1, bass.ds(e + 1, 1)], min_val=1, max_val=TILES_MAX)
            return first, end

        gate_v = a["w_exp_gate"].rearrange("e (h p c) n -> e p h c n", h=2, c=4)
        up_v = a["w_exp_up"].rearrange("e (h p c) n -> e p h c n", h=2, c=4)
        down_v = a["w_exp_down"].rearrange("e (p k) n -> e p k n", k=KH)

        @block.sync
        def _(sp):
            for h in range(2):
                kk = slice(4 * h, 4 * h + 4)
                sp.dma_start(x_t[:, kk, :], a["x_t"][:, kk, :]).then_inc(s[f"in_x{h}"], 16)
            sp.dma_start(w_u, a["w_in_u"].rearrange("(p k) n -> p k n", k=KD)).then_inc(s["in_w_u"], 16)
            sp.dma_start(w_qkv, a["w_in_qkv"].rearrange("(p k) n -> p k n", k=KD)).then_inc(s["in_w_qkv"], 16)
            sp.dma_start(kd_t[:, :, 0:WIN], a["cache_k_t"]).then_inc(s["in_attn"], 16)
            sp.dma_start(v_old, a["cache_v"].rearrange("b k n -> k b n")).then_inc(s["in_attn"], 16)
            sp.wait_ge(s["zero_ready"], 1)
            sp.dma_start(y_slots.rearrange("(i p) n -> p i n", p=P),
                         probs_t[:].unsqueeze(1).to_broadcast([P, SLOTS // P, D])).then_inc(s["zeroed"], 16)

            for b in range(GB):
                sp.wait_ge(s["u_out"], b + 1)
                sp.dma_start(u_scr[b * P:(b + 1) * P], u_stage[:, b]).then_inc(s["u_stored"], 16)
            sp.wait_ge(s["u_stored"], 16 * GB)
            sp.wait_ge(s["rstd_ps"], 1)
            us = u_scr.rearrange("(g c) s n -> s c g n", c=GC)
            for t in range(T):
                sp.dma_start(u_c[GC * t:GC * t + GC], us[t]).then_inc(s["u_in"], 16)
            sp.wait_ge(s["conv_zero"], 1)
            sp.wait_ge(s["kern_done"], 1)
            for t in range(T):
                sp.dma_start(conv_w[GC * t:GC * t + GC, :, GC * t:P], kern[0:GC, :, 0:P - GC * t])\
                    .then_inc(s["conv_in"], 16)
            sp.wait_ge(s["kv_out"], NT)
            for n, name in enumerate(("k", "v")):
                sp.dma_start(o[f"new_{name}_prompt"], kv_row[:, NT - 2, P * n:P * n + P])\
                    .then_inc(s["cache_out"], 16)
                for b in range(NB):
                    sp.dma_start(o[f"new_{name}_sample"][b, WIN - LS:WIN, :],
                                 kv_row[LS * b:LS * b + LS, NT - 1, P * n:P * n + P]).then_inc(s["cache_out"], 16)
                sp.dma_start(o[f"new_{name}_sample"][:, 0:WIN - LS, :], a[f"cache_{name}"][:, LS:WIN, :])\
                    .then_inc(s["cache_out"], 16)
            sp.wait_ge(s["conv_in"], 16 * T)
            sp.wait_ge(s["decay_used"], 2)
            sp.dma_start(w_out, a["w_out"]).then_inc(s["out_w"], 16)
            sp.dma_start(w_glu, a["w_glu"].rearrange("(k p) n -> p k n", p=P)).then_inc(s["out_w"], 16)
            sp.wait_ge(s["y_out_done"], 8)
            ys = y_scr.rearrange("(g c) t n -> t c g n", c=GC)
            for t in range(T):
                sp.dma_start(ys[t], u_c[GC * t:GC * t + GC]).then_inc(s["y_stored"], 16)
            sp.wait_ge(s["y_stored"], 16 * T)
            sp.dma_start(y_t, y_scr.rearrange("(b p) t n -> p b (t n)", p=P)).then_inc(s["y_in"], 16)
            sp.wait_ge(s["states_done"], 3)
            for b in range(NB):
                sp.dma_start(v_new[:, b, :], kv_row[LS * b:LS * b + LS, NT - 1, P:256]).then_inc(s["vnew_in"], 16)
            sp.dma_start(o["state_prompt"], h_last[:]).then_inc(s["states_out"], 16)
            sp.dma_start(o["state_sample"], h_dec[:]).then_inc(s["states_out"], 16)
            sp.wait_ge(s["y_ps"], 8)
            sp.dma_start(gate_w[0], gate_v[0]).then_inc(gate_in[0], 16)
            sp.dma_start(up_w[0], up_v[0]).then_inc(up_in[0], 16)
            sp.dma_start(down_w[0], down_v[0]).then_inc(down_in[0], 16)
            sp.wait_ge(s["av_ps"], NT)
            sp.dma_start(resid, a["x_rows"].rearrange("(i p) n -> p i n", p=P)).then_inc(s["in_resid"], 16)
            sp.dma_start(w_r, a["w_router"].rearrange("(p k) n -> p k n", k=KD)).then_inc(s["in_rows"], 16)
            sp.dma_start(g_ffn[:], a["g_norm_ffn"].to_broadcast((P, D))).then_inc(s["in_rows"], 16)
            sp.dma_start(g_fin[:], a["g_final"].to_broadcast((P, D))).then_inc(s["in_rows"], 16)
            sp.wait_ge(s["op_ps"], 2 * NT)
            sp.dma_start(gate_w[1], gate_v[1]).then_inc(gate_in[1], 16)
            sp.dma_start(up_w[1], up_v[1]).then_inc(up_in[1], 16)
            sp.dma_start(down_w[1], down_v[1]).then_inc(down_in[1], 16)
            sp.wait_ge(s["pos_done"], 1)
            with sp.Fori(1, NE // 2) as it:
                for q in range(2):
                    e = it * 2 + q
                    done = sp.value_load(first_i[0:1, bass.ds(e - 1, 1)], min_val=1, max_val=TILES_MAX)
                    sp.wait_ge(s["gu_ready"], done)
                    sp.dma_start(gate_w[q], gate_v[e]).then_inc(gate_in[q], 16)
                    sp.dma_start(up_w[q], up_v[e]).then_inc(up_in[q], 16)
                    sp.wait_ge(s["y_ready"], done)
                    sp.dma_start(down_w[q], down_v[e]).then_inc(down_in[q], 16)
            for i in range(NT):
                sp.wait_ge(s["fin_done"], i + 1)
                sp.dma_start(o["y"][P * i:P * i + P, :], fin[i % 2]).then_inc(fin_out[i % 2], 16)
            sp.wait_ge(fin_out[0], 16 * 3)
            sp.wait_ge(fin_out[1], 16 * 2)
            sp.wait_ge(s["states_out"], 32)
            sp.wait_ge(s["cache_out"], 16 * 2 * (NB + 2))

        @block.gpsimd
        def _(pool):
            steps = [0]

            def step(ins):
                steps[0] += 1
                ins.then_inc(s["pool_step"], 1)
                pool.wait_ge(s["pool_step"], steps[0])

            pool.memset(probs_t[:], 0.0).then_inc(s["zero_ready"], 1)
            pool.memset(conv_w, 0.0).then_inc(s["conv_zero"], 1)
            step(pool.memset(ident[:], 0.0))
            step(pool.affine_select(out=ident[:], in_=ident[:], compare_op=ALU.not_equal, fill=1.0, base=0,
                                    pattern=[[-1, P]], channel_multiplier=1))
            step(pool.memset(ones[:], 1.0))
            step(pool.affine_select(out=before[:], in_=ones[:], compare_op=ALU.is_gt, fill=0.0, base=0,
                                    pattern=[[1, P]], channel_multiplier=-1))
            step(pool.memset(tile_tt[:], float(TT)))
            step(pool.memset(zero_nt[:], 0.0))
            step(pool.memset(mask, 0.0))
            step(pool.memset(mask[0:HD, 192:256], MASKED))
            step(pool.memset(mask[HD:P, 0:HD], MASKED))
            step(pool.iota(iota_e[:], [[1, NE]], base=0, channel_multiplier=0, allow_small_or_imprecise_dtypes=True))
            step(pool.iota(iota_t[:], [[1, TT]], base=0, channel_multiplier=0,
                           allow_small_or_imprecise_dtypes=True))
            pool.memset(pad8[:], -3.0e38).then_inc(s["const_done"], 1)

            pool.wait_ge(s["bbar_done"], 1)
            t1 = sums_f[:, 0:448].rearrange("p (r s c) -> p r s c", r=4, s=7)
            t2 = sums_f[:, 512:960].rearrange("p (r s c) -> p r s c", r=4, s=7)
            for q in range(4):
                rr = slice(4 * q, 4 * q + 4)
                pr, pi = [pw[:, i, 1:T, rr].rearrange("p s r -> p r s").unsqueeze(3).to_broadcast([P, 4, T - 1, GC])
                          for i in range(2)]
                br, bi = [bbar[:, i, rr, :].unsqueeze(2).to_broadcast([P, 4, T - 1, GC]) for i in range(2)]
                if q >= 1:
                    pool.wait_ge(s["bp_tr"], 2 * q)
                for i in range(2):
                    pool.tensor_copy(bp[:, :, i, T - 1, :], bbar[:, i, rr, :])
                pool.tensor_tensor(t1, br, pr, ALU.mult)
                step(pool.tensor_tensor(t2, bi, pi, ALU.mult))
                step(pool.tensor_tensor(bp[:, :, 0, 0:T - 1, :], t1, t2, ALU.subtract))
                pool.tensor_tensor(t1, br, pi, ALU.mult)
                step(pool.tensor_tensor(t2, bi, pr, ALU.mult))
                pool.tensor_tensor(bp[:, :, 1, 0:T - 1, :], t1, t2, ALU.add).then_inc(s["bp_ready"], 1)

            re, im = rot
            wl = [prep[:, 20 + i, :] for i in range(4)]
            step(pool.memset(re[:, :, 0:1], 1.0))
            step(pool.memset(im[:, :, 0:1], 0.0))
            n = 1
            cur, nxt = (prep[:, 18, :], prep[:, 19, :]), wl[0:2]
            while n < NCP:
                cr, ci = [c.unsqueeze(2).to_broadcast([P, R, n]) for c in cur]
                m1 = probs[:, 0, 0:R * n].rearrange("p (r n) -> p r n", n=n)
                m2 = probs[:, 0, 512:512 + R * n].rearrange("p (r n) -> p r n", n=n)
                pool.tensor_tensor(m1, re[:, :, 0:n], cr, ALU.mult)
                step(pool.tensor_tensor(m2, im[:, :, 0:n], ci, ALU.mult))
                step(pool.tensor_tensor(re[:, :, n:2 * n], m1, m2, ALU.subtract))
                pool.tensor_tensor(m1, re[:, :, 0:n], ci, ALU.mult)
                step(pool.tensor_tensor(m2, im[:, :, 0:n], cr, ALU.mult))
                step(pool.tensor_tensor(im[:, :, n:2 * n], m1, m2, ALU.add))
                q1, q2 = prep[:, 24, :], prep[:, 25, :]
                pool.tensor_tensor(q1, cur[0], cur[0], ALU.mult)
                step(pool.tensor_tensor(q2, cur[1], cur[1], ALU.mult))
                step(pool.tensor_tensor(nxt[0], q1, q2, ALU.subtract))
                step(pool.tensor_tensor(q1, cur[0], cur[1], ALU.mult))
                step(pool.tensor_tensor(nxt[1], q1, q1, ALU.add))
                cur, nxt = nxt, (wl[2:4] if nxt is wl or nxt[0] is wl[0] else wl[0:2])
                n *= 2
            pool.sem_inc(s["rot_ready"], 1)

            pool.wait_ge(s["sum_out"], 8)
            ar, ai = [pw[:, i, 0, :].unsqueeze(2).to_broadcast([P, R, NB]) for i in range(2)]
            dec = states[:, :, :, NCP:NC].rearrange("p r i (b j) -> p r i b j", j=2)
            new = sums[:, :, :, NCP:NC].rearrange("p i r (b j) -> p i r b j", j=2)
            d0, d1 = dec_tmp[:, 0], dec_tmp[:, 1]
            for i in range(2):
                step(pool.tensor_copy(dec[:, :, i, :, 0], h0[:, i]))
            for j in range(2):
                hr, hi = (h0[:, 0], h0[:, 1]) if j == 0 else (dec_tmp[:, 2], dec_tmp[:, 3])
                tr, ti = (dec_tmp[:, 2], dec_tmp[:, 3]) if j == 0 else (h_dec[:, 0], h_dec[:, 1])
                for x, y, op, dst, i in ((ar, ai, ALU.subtract, tr, 0), (ai, ar, ALU.add, ti, 1)):
                    step(pool.tensor_tensor(d0, hr, x, ALU.mult))
                    step(pool.tensor_tensor(d1, hi, y, ALU.mult))
                    step(pool.tensor_tensor(d0, d0, d1, op))
                    step(pool.tensor_tensor(dst, d0, new[:, i, :, :, j], ALU.add))
                if j == 0:
                    for i in range(2):
                        step(pool.tensor_copy(dec[:, :, i, :, 1], dec_tmp[:, 2 + i]))
            pool.sem_inc(s["states_done"], 2)

            pool.wait_ge(s["kern_out"], 8)
            pool.wait_ge(s["in_small"], 48)
            step(pool.tensor_tensor(skip_tmp, skip[:].unsqueeze(2).to_broadcast([GC, G, GC]),
                                    ident[0:GC, 0:GC].unsqueeze(1).to_broadcast([GC, G, GC]), ALU.mult))
            pool.tensor_tensor(kern[0:GC, :, 0:GC], kern[0:GC, :, 0:GC], skip_tmp, ALU.add)\
                .then_inc(s["kern_done"], 1)

            pool.memset(bp_buf[:], 0.0).then_inc(s["attn_z"], 1)

            pool.wait_ge(s["pos_done"], 1)
            pool.sem_inc(s["base_step"], 1)
            pool.sem_inc(s["sel_ready"], 1)
            with pool.Fori(0, NE) as e:
                first, end = tiles_of(pool, e)
                pool.wait_ge(s["base_step"], e + first + 1)
                pool.tensor_copy(place_b, place_e[:, bass.ds(e, 1), :].rearrange("p e i -> p (e i)"))\
                    .then_inc(s["base_step"], 1)
                with pool.Fori(first, end) as w:
                    pool.wait_ge(s["base_step"], e + w + 2)
                    pool.wait_ge(s["sel_ready"], w + 1)
                    pool.tensor_tensor(place_c, place_b, zero_nt[:], ALU.add).then_inc(s["place_ready"], 1)
                    pool.wait_ge(s["place_ready"], w + 1)
                    pool.tensor_tensor(place_b, place_b, tile_tt[:], ALU.subtract).then_inc(s["base_step"], 1)
            pool.sem_inc(s["place_ready"], 1)

            pool.wait_ge(s["rows_done"], 1)
            for i in range(NT):
                if i >= 2:
                    pool.wait_ge(s["fin_done"], i - 1)
                for k in range(2):
                    pool.indirect_dma_start(got[i % 2][k], None, y_slots,
                                            bass.IndirectOffsetOnAxis(pos_u[:, k, i:i + 1], 0))\
                        .then_inc(got_in[i % 2], 16)

        @block.tensor
        def _(pe):
            pe.wait_ge(s["const_done"], 1)
            for h in range(2):
                pe.wait_ge(s["sq_done"], h + 1)
                for k in range(4 * h, 4 * h + 4):
                    pe.matmul(pp[2][:, 0, :], ones[:], x_sq[:, k, 0:SEQ], start=k == 0, stop=k == KD - 1)
                    ins = pe.matmul(pp[2][:, 1, 0:P], ones[:], x_sq[:, k, SEQ:TOK], start=k == 0, stop=k == KD - 1)
            ins.then_inc(s["rstd_ps"], 1)

            columns = [w_u[:, :, P * b:P * b + P] for b in range(GB)] + [w_qkv[:, :, W:W + P]]
            columns += [w_qkv[:, :, P * h:P * h + P] for h in range(QPK)]

            def project(n):
                t = pp[n % 2]
                if n >= 2:
                    pe.wait_ge(s["proj_out"], n - 1)
                if n == GB:
                    pe.wait_ge(s["in_w_qkv"], 16)
                for k in range(KD):
                    if n == 0 and k % 4 == 0:
                        pe.wait_ge(s["xg_done"], k // 4 + 1)
                    pe.matmul(t[:, 0, :], columns[n][:, k, :], x_t[:, k, 0:SEQ], start=k == 0, stop=k == KD - 1)
                    ins = pe.matmul(t[:, 1, 0:P], columns[n][:, k, :], x_t[:, k, SEQ:TOK],
                                    start=k == 0, stop=k == KD - 1)
                ins.then_inc(s["proj_ps"], 1)

            def turn_bp(q):
                pe.wait_ge(s["bp_ready"], q + 1)
                for side in range(2):
                    h = 2 * q + side
                    if h >= 2:
                        pe.wait_ge(s["bp_out"], h - 1)
                    for j in range(2):
                        for i in range(2):
                            c = 256 * j + P * i
                            ins = pe.transpose(pp[2][:, side, c:c + P],
                                               bp[:, 2 * side + j, i].rearrange("p s c -> p (s c)"), ident[:])
                    ins.then_inc(s["bp_tr"], 1)

            def chunk_sums(h):
                q, i = h // 2, h % 2
                if h >= 2:
                    pe.wait_ge(s["sum_out"], h - 1)
                for j in range(4):
                    r = 4 * q + j
                    for m in range(2):
                        ins = pe.matmul(pp[2][HD * m:HD * m + HD, i, NC * j:NC * j + NC],
                                        sum_w[:, r, i, HD * m:HD * m + HD], u_c[:, 2 * r + m, :],
                                        start=True, stop=True)
                ins.then_inc(s["sum_ps"], 1)

            def kernels(h):
                q, m = h // 2, h % 2
                if h >= 2:
                    pe.wait_ge(s["kern_out"], h - 1)
                rows = slice(HD * m, HD * m + HD)
                for j in range(4):
                    r = 4 * q + j
                    for i in range(2):
                        pe.matmul(pp[2][0:GC, m, P * j:P * j + GC], bbar[rows, i, r, :], ssm_c[rows, i, r, :],
                                  start=i == 0, stop=i == 1)
                    for i in range(2):
                        ins = pe.matmul(pp[2][0:GC, m, P * j + GC:P * j + P], bbar[rows, i, r, :],
                                        out_tab[rows, r, i, 0:T - 1, :], start=i == 0, stop=i == 1)
                ins.then_inc(s["kern_ps"], 1)

            def ssm_out(h):
                q, m = h // 2, h % 2
                if h >= 2:
                    pe.wait_ge(s["y_out_done"], h - 1)
                rows = slice(HD * m, HD * m + HD)
                for j in range(4):
                    r = 4 * q + j
                    t = pp[2][:, m, NC * j:NC * j + NC]
                    pe.matmul(t, conv_w[:, 2 * r + m, :], u_c[:, 2 * r + m, :], start=True, stop=False)
                    for i in range(2):
                        ins = pe.matmul(t, out_tab[rows, r, i].rearrange("p t c -> p (t c)"), states[rows, r, i, :],
                                        start=False, stop=i == 1)
                ins.then_inc(s["y_ps"], 1)

            pe.wait_ge(s["in_w_u"], 16)
            project(0)
            pe.wait_ge(s["rstd_done"], 1)
            for i in range(NT):
                ins = pe.matmul(pp[2][:, 0, i:i + 1], rstd_row[0:1, P * i:P * i + P], ones[0:1, 0:1],
                                start=True, stop=True)
            ins.then_inc(s["stat_cols"], 1)
            for n in range(1, GB):
                project(n)
            pe.wait_ge(s["cols_read"], 1)
            for n in range(GB, 9):
                if n > GB:
                    turn_bp(n - GB - 1)
                project(n)
            for i in range(NT):
                t = pp[3][:, i % 2, 0:256]
                if i >= 2:
                    pe.wait_ge(s["kv_out"], i - 1)
                for k in range(KD):
                    ins = pe.matmul(t, x_t[:, k, P * i:P * i + P], w_qkv[:, k, W:W + 256],
                                    start=k == 0, stop=k == KD - 1)
                ins.then_inc(s["kv_ps"], 1)
            pe.wait_ge(s["bp_out"], 8)
            pe.wait_ge(s["u_in"], 16 * T)
            for h in range(8):
                chunk_sums(h)
            pe.wait_ge(s["out_tab_done"], 1)
            pe.wait_ge(s["sum_out"], 8)

            def scores(n):
                m, v = n // 2, n % 2
                rows = slice(HD * v, HD * v + HD)
                sc = pp[0][:].rearrange("p b (h n) -> p (b h) n", h=2)
                if n >= 1:
                    pe.wait_ge(s["sc_read"], n)
                else:
                    pe.wait_ge(s["proj_out"], 9)
                lo = 0 if m else P
                for h in range(QPK):
                    ins = pe.matmul(sc[:, h, lo:256], q_t[rows, h, P * m:P * m + P],
                                    k_t[rows, P * (m - 1) + lo:P * (m + 1)], start=True, stop=True)
                ins.then_inc(s["sc_ps"], 1)

            def turn_probs(n):
                m = n // 2
                pe.wait_ge(s["norm_done"], n + 1)
                if n >= 1:
                    pe.wait_ge(s["pt_out"], n)
                pr = probs[:, n % 2].rearrange("p (h n) -> p h n", h=QPK)
                for kt in range(0 if m else 1, 2):
                    for h in range(QPK):
                        ins = pe.transpose(pp[1][:, kt, P * h:P * h + P], pr[:, h, P * kt:P * kt + P], ident[:])
                ins.then_inc(s["pt_ps"], 1)

            def weighted(n):
                m, v = n // 2, n % 2
                pe.wait_ge(s["pt_out"], n + 1)
                if v == 0 and m >= 1:
                    pe.wait_ge(s["attn_done"], m)
                for kt in range(0 if m else 1, 2):
                    ins = pe.matmul(pp[3][HD * v:HD * v + HD, 0, :], kv_row[:, m - 1 + kt, P + HD * v:P + HD * v + HD],
                                    probs_t[:, 512 * kt:512 * kt + 512], start=kt == (0 if m else 1), stop=kt == 1)
                if v == 1:
                    ins.then_inc(s["av_ps"], 1)

            def squares(m):
                pe.wait_ge(s["av_sq"], m + 1)
                for h in range(QPK):
                    ins = pe.matmul(pp[3][:, 1, m:m + 1], rstd_row[:, P * h:P * h + P], ones[:, 0:1],
                                    start=h == 0, stop=h == QPK - 1)
                ins.then_inc(s["ssq_ps"], 1)

            for h in range(8):
                kernels(h)
            scores(0)
            scores(1)
            pe.wait_ge(s["kv_out"], NT)
            for n in range(8):
                turn_probs(n)
                if n + 2 < 8:
                    scores(n + 2)
                if n == SSM_FROM:
                    pe.wait_ge(s["conv_in"], 16 * T)
                    pe.wait_ge(s["kern_out"], 8)
                    pe.wait_ge(s["states_done"], 3)
                if SSM_FROM <= n < SSM_FROM + 4:
                    ssm_out(2 * (n - SSM_FROM))
                    ssm_out(2 * (n - SSM_FROM) + 1)
                weighted(n)
                if n % 2:
                    squares(n // 2)

            pe.wait_ge(s["streams_ready"], 1)
            pe.wait_ge(s["in_attn"], 32)
            pe.wait_ge(s["sc_read"], 8)
            pe.wait_ge(s["vnew_in"], 16 * NB)
            for j in range(3):
                bs = range(3 * j, min(3 * j + 3, NB))
                if j == 2:
                    pe.wait_ge(s["exp_done"], 9)
                for b in bs:
                    ins = pe.matmul(pp[0][:, j % 2, NK * (b - 3 * j):NK * (b - 3 * j) + NK],
                                    q_z[:, b].rearrange("p v h t -> p (v h t)"), kd_t[:, b, :], start=True, stop=True)
                ins.then_inc(s["sc_ps"], 1)
            for j in range(3):
                bs = range(3 * j, min(3 * j + 3, NB))
                n = 8 + j
                pe.wait_ge(s["norm_done"], n + 1)
                pe.wait_ge(s["pt_out"], n)
                pr = probs[:, j % 2, 0:3 * NK].rearrange("p (b n) -> p b n", b=3)
                for b in bs:
                    c = P * (b - 3 * j)
                    pe.transpose(pp[1][:, 0, c:c + P], pr[:, b - 3 * j, 0:WIN], ident[:])
                    ins = pe.transpose(pp[1][0:LS, 1, c:c + P], pr[:, b - 3 * j, WIN:NK], ident[:])
                ins.then_inc(s["pt_ps"], 1)
                pe.wait_ge(s["pt_out"], n + 1)
                if j == 0:
                    pe.wait_ge(s["attn_done"], NT - 1)
                for b in bs:
                    for v in range(NKV):
                        c = P * (b - 3 * j) + HD * v
                        t = pp[3][HD * v:HD * v + HD, 0, HD * b:HD * b + HD]
                        pe.matmul(t, v_old[:, b, HD * v:HD * v + HD], probs_t[:, c:c + HD], start=True, stop=False)
                        ins = pe.matmul(t, v_new[:, b, HD * v:HD * v + HD], probs_t[0:LS, 512 + c:512 + c + HD],
                                        start=False, stop=True)
            ins.then_inc(s["av_ps"], 1)
            squares(NT - 1)

            pe.wait_ge(s["gelu_done"], 1)
            pe.wait_ge(s["out_w"], 32)
            pe.wait_ge(s["exp_done"], 11)
            pe.wait_ge(s["pt_out"], 11)
            for n in range(GB):
                if n >= 2:
                    pe.wait_ge(s["sig_done"], n - 1)
                for k in range(GB):
                    pe.matmul(pp[n % 2][:, 0, :], w_glu[:, k, P * n:P * n + P], y_g[:, k, 0:512],
                              start=k == 0, stop=k == GB - 1)
                    ins = pe.matmul(pp[n % 2][:, 1, 0:P], w_glu[:, k, P * n:P * n + P], y_g[:, k, 512:TOK],
                                    start=k == 0, stop=k == GB - 1)
                ins.then_inc(s["glu_ps"], 1)
            pe.wait_ge(s["mixsq_done"], GB)
            for i in range(NT):
                for b in range(GB):
                    ins = pe.matmul(pp[3][:, 1, NT + i:NT + i + 1], mix_sq[:, b, P * i:P * i + P], ones[:, 0:1],
                                    start=b == 0, stop=b == GB - 1)
            ins.then_inc(s["ssq_ps"], 1)

            def router(i):
                pe.wait_ge(s["ffn_done"], i + 1)
                if i >= 1:
                    pe.wait_ge(s["xf_out"], i)
                for k in range(KD):
                    ins = pe.transpose(pp[2][:, k // 4, P * (k % 4):P * (k % 4) + P], ffn_in[:, i, k:D:KD], ident[:])
                ins.then_inc(s["xf_tr"], 1)
                pe.wait_ge(s["xf_out"], i + 1)
                xf = probs[:, i % 2].rearrange("p (k t) -> p k t", k=KD)
                for k in range(KD):
                    ins = pe.matmul(pp[3][:, 0, NR * i:NR * i + NR], xf[:, k, :], w_r[:, k, :],
                                    start=k == 0, stop=k == KD - 1)
                ins.then_inc(s["lg_ps"], 1)

            pe.wait_ge(s["sig_done"], GB)
            pe.wait_ge(s["mix_done"], GB + 1)
            for i in range(NT):
                for m, left in enumerate((attn_t, mix_t)):
                    if i >= 1:
                        pe.wait_ge(s["op_out"], 2 * (i - 1) + m + 1)
                    for n in range(2):
                        for k in range(GB):
                            ins = pe.matmul(pp[m][:, n, :], left[:, k, P * i:P * i + P],
                                            w_out[:, 4 * m + k, 512 * n:512 * n + 512], start=k == 0, stop=k == GB - 1)
                    ins.then_inc(s["op_ps"], 1)
                if i >= 1:
                    router(i - 1)
            router(NT - 1)

            pe.wait_ge(s["pair_done"], 1)
            for i in range(NT):
                for j in range(i + 1):
                    pe.matmul(pp[3][:, 1, NE * i:NE * i + NE], before[:] if j == i else ones[:], both[:, j, :],
                              start=j == 0, stop=j == i)
            for i in range(NT):
                ins = pe.matmul(pp[3][:, 1, 256:256 + NE], ones[:], both[:, i, :], start=i == 0, stop=i == NT - 1)
            ins.then_inc(s["place_ps"], 1)

            gu, yp, gx, xtp, htp = pp[0][:, 0, :], pp[0][:, 1, :], pp[2][:, 0, :], pp[2][:, 1, :], pp[1][:, 0, 0:256]

            def pick(w=None):
                for i in range(NT):
                    if w is not None and i == NT - 1:
                        pe.wait_ge(s["h_ready"], w + 1)
                    for h in range(2):
                        ins = pe.matmul(gx[HD * h:HD * h + HD], sel[:, i, :], ffn_in[:, i, 512 * h:512 * h + 512],
                                        start=i == 0, stop=i == NT - 1)
                ins.then_inc(s["gx_ready"], 1)

            def turn():
                for c in range(4):
                    ins = pe.transpose(xtp[:, P * c:P * c + P], xrow[:, c:512:4], ident[:])
                ins.then_inc(s["xt_ready"], 1)

            pe.wait_ge(s["sel_ready"], 2)
            pick()
            pe.wait_ge(s["gx_copied"], 1)
            turn()
            with pe.Fori(0, NE // 2) as it:
                for q in range(2):
                    first, end = tiles_of(pe, it * 2 + q)
                    with pe.Fori(first, end) as w:
                        pe.wait_ge(s["xt_copied"], w + 1)
                        pe.wait_ge(gate_in[q], it * 16 + 16)
                        pe.wait_ge(up_in[q], it * 16 + 16)
                        for n in range(KD):
                            h, c = n // 4, n % 4
                            lhs = xt_e[:, c, TT * h:TT * h + TT]
                            pe.matmul(gu[0:TT], lhs, gate_w[q][:, h, c, :], start=n == 0, stop=n == KD - 1)
                            ins = pe.matmul(gu[TT:P], lhs, up_w[q][:, h, c, :], start=n == 0, stop=n == KD - 1)
                        ins.then_inc(s["gu_ready"], 1)
                        pe.wait_ge(s["sel_ready"], w + 3)
                        pick(w)
                        for k in range(KH):
                            ins = pe.transpose(htp[:, TT * k:TT * k + TT], hid[:, k:DE:KH], ident[0:TT, 0:TT])
                        ins.then_inc(s["ht_ready"], 1)
                        pe.wait_ge(s["gx_copied"], w + 2)
                        turn()
                        pe.wait_ge(s["ht_copied"], w + 1)
                        pe.wait_ge(down_in[q], it * 16 + 16)
                        pe.wait_ge(s["y_copied"], w + 1)
                        for k in range(KH):
                            for h in range(2):
                                ins = pe.matmul(yp[TT * h:TT * h + TT], hid_t[:, k, :],
                                                down_w[q][:, k, 512 * h:512 * h + 512],
                                                start=k == 0, stop=k == KH - 1)
                        ins.then_inc(s["y_ready"], 1)

        @block.scalar
        def _(act):
            act.dma_start(cols[:], a["cols"]).then_inc(s["in_cols"], 16)
            act.dma_start(tables[:], a["tables"]).then_inc(s["in_tables"], 16)
            for m in range(2):
                act.dma_start(prep[HD * m:HD * m + HD, 2, :], a["log_dt"][m:m + 1, :].to_broadcast((HD, R)))\
                    .then_inc(s["in_tables"], 16)
            act.dma_start(sink_row[:], a["sinks"].to_broadcast((P, 8))).then_inc(s["in_small"], 16)
            act.dma_start(skip[:], a["ssm_d"]).then_inc(s["in_small"], 16)
            act.dma_start(b_r[:], a["b_router"].to_broadcast((P, NR))).then_inc(s["in_small"], 16)
            for h in range(2):
                act.wait_ge(s[f"in_x{h}"], 16)
                kk = slice(4 * h, 4 * h + 4)
                act.activation(x_sq[:, kk, :], x_t[:, kk, :], ACT.Square).then_inc(s["sq_done"], 1)
            act.wait_ge(s["in_tables"], 48)
            act.activation(prep[:, 3, :], prep[:, 2, :], ACT.Exp).then_inc(s["prep_act"], 1)
            act.wait_ge(s["prep_dve"], 1)
            act.activation(prep[:, 6, :], prep[:, 4, :], ACT.Exp).then_inc(s["prep_act"], 1)
            act.wait_ge(s["rstd_act"], 1)
            act.activation(rstd_row[:], rstd_row[:], ACT.Sqrt).then_inc(s["rstd_act"], 1)
            act.wait_ge(s["prep_dve"], 2)
            act.activation(prep[:, 9, :], prep[:, 8, :], ACT.Sin)
            act.activation(prep[:, 10, :], prep[:, 8, :], ACT.Sin, scale=0.5).then_inc(s["prep_act"], 1)

            act.wait_ge(s["u_stored"], 16 * GB)
            for h in range(8):
                act.wait_ge(s["bp_tr"], h + 1)
                act.copy(sum_w[:, 2 * h:2 * h + 2], pp[2][:, h % 2, :].rearrange("p (r i m) -> p r i m", r=2, i=2))\
                    .then_inc(s["bp_out"], 1)
            for h in range(8):
                q, i = h // 2, h % 2
                act.wait_ge(s["sum_ps"], h + 1)
                act.copy(sums[:, i, 4 * q:4 * q + 4, :],
                         pp[2][:, i, 0:4 * NC].rearrange("p (r n) -> p r n", r=4)).then_inc(s["sum_out"], 1)
            kv = kern[0:GC].rearrange("p (r m) n -> p r m n", m=2)
            for h in range(8):
                q, m = h // 2, h % 2
                act.wait_ge(s["kern_ps"], h + 1)
                act.copy(kv[:, 4 * q:4 * q + 4, m, :],
                         pp[2][0:GC, m, :].rearrange("p (r n) -> p r n", r=4)).then_inc(s["kern_out"], 1)
            uv = u_c.rearrange("p (r m) n -> p r m n", m=2)

            def ssm_copy(h):
                q, m = h // 2, h % 2
                act.wait_ge(s["y_ps"], h + 1)
                act.copy(uv[:, 4 * q:4 * q + 4, m, :],
                         pp[2][:, m, 0:4 * NC].rearrange("p (r n) -> p r n", r=4)).then_inc(s["y_out_done"], 1)

            def exps(n, rows, src):
                act.wait_ge(s["neg_done"], n + 1)
                act.activation(sm[:, n % 2, 4, 0:rows], sm[:, n % 2, 4, 0:rows], ACT.Exp)
                for h in range(rows):
                    dst, x = src(h)
                    ins = act.activation(dst, x, ACT.Exp, bias=sm[:, n % 2, 2, h:h + 1], scale=SCALE,
                                         accum_out=sm[:, n % 2, 3, h:h + 1])
                ins.then_inc(s["exp_done"], 1)

            def pt_copy(n):
                act.wait_ge(s["pt_ps"], n + 1)
                if n < 2:
                    act.copy(probs_t[:, 512:1024], pp[1][:, 1, :]).then_inc(s["pt_out"], 1)
                elif n < 8:
                    act.copy(probs_t[:], pp[1][:].rearrange("p b n -> p (b n)")).then_inc(s["pt_out"], 1)
                else:
                    w = P * min(3, NB - 3 * (n - 8))
                    act.copy(probs_t[:, 0:w], pp[1][:, 0, 0:w])
                    act.copy(probs_t[0:LS, 512:512 + w], pp[1][0:LS, 1, 0:w]).then_inc(s["pt_out"], 1)

            def unit(n):
                lo = 0 if n >= 2 else P
                pr = probs[:, n % 2].rearrange("p (h n) -> p h n", h=QPK)
                return lambda h: (pr[:, h, lo:256], pr[:, h, lo:256])

            def stream(j):
                pr = probs[:, j % 2, 0:3 * NK].rearrange("p (b n) -> p b n", b=3)
                sc = pp[0][:, j % 2, 0:3 * NK].rearrange("p (b n) -> p b n", b=3)
                return lambda b: (pr[:, b, :], sc[:, b, :])

            act.wait_ge(s["zeroed"], 16)
            for n in range(8):
                exps(n, QPK, unit(n))
                if n >= 1:
                    pt_copy(n - 1)
                if SSM_FROM < n <= SSM_FROM + 4:
                    ssm_copy(2 * (n - 1 - SSM_FROM))
                    ssm_copy(2 * (n - 1 - SSM_FROM) + 1)
                if n >= 2 and n % 2 == 0:
                    m = n // 2 - 1
                    act.wait_ge(s["av_ps"], m + 1)
                    if m >= 1:
                        act.wait_ge(s["ssq_ps"], m)
                    act.activation(rstd_row[:, 0:512], pp[3][:, 0, :], ACT.Square).then_inc(s["av_sq"], 1)
            pt_copy(7)
            act.wait_ge(s["av_ps"], 4)
            act.wait_ge(s["ssq_ps"], 3)
            act.activation(rstd_row[:, 0:512], pp[3][:, 0, :], ACT.Square).then_inc(s["av_sq"], 1)
            for j in range(3):
                exps(8 + j, min(3, NB - 3 * j), stream(j))
                if j >= 1:
                    pt_copy(7 + j)
            pt_copy(10)
            act.wait_ge(s["av_ps"], NT)
            act.wait_ge(s["ssq_ps"], NT - 1)
            act.activation(rstd_row[:, 0:512].rearrange("p (h b t) -> p b h t", h=QPK, b=NB),
                           pp[3][:, 0, :].rearrange("p (b h t) -> p b h t", b=NB, h=QPK), ACT.Square)\
                .then_inc(s["av_sq"], 1)

            act.wait_ge(s["y_in"], 16)
            act.activation(y_g, y_t, ACT.Gelu_apprx_tanh).then_inc(s["gelu_done"], 1)
            for n in range(GB):
                act.wait_ge(s["glu_ps"], n + 1)
                act.activation(mix_sq[:, n, 0:512], pp[n % 2][:, 0, :], ACT.Sigmoid, bias=b_glu[:, n:n + 1])
                act.activation(mix_sq[:, n, 512:TOK], pp[n % 2][:, 1, 0:P], ACT.Sigmoid, bias=b_glu[:, n:n + 1])\
                    .then_inc(s["sig_done"], 1)
            for n in range(GB):
                act.wait_ge(s["mix_done"], n + 1)
                act.activation(mix_sq[:, n, :], mix_t[:, n, :], ACT.Square).then_inc(s["mixsq_done"], 1)
            act.wait_ge(s["rs_done"], 1)
            act.activation(stat[:, 1:3, :], stat[:, 1:3, :], ACT.Sqrt).then_inc(s["rs_act"], 1)
            for i in range(NT):
                act.wait_ge(s["op_out"], 2 * i + 2)
                act.activation(sums_f[:, 0:D], resid[:, i, :], ACT.Square, accum_out=stat[:, 3, i:i + 1])\
                    .then_inc(s["ffn_sq"], 1)
                act.wait_ge(s["ffn_ms"], i + 1)
                act.activation(stat[:, 4, i:i + 1], stat[:, 4, i:i + 1], ACT.Sqrt).then_inc(s["ffn_sqrt"], 1)
                act.wait_ge(s["xf_tr"], i + 1)
                if i >= 2:
                    act.wait_ge(s["lg_ps"], i - 1)
                act.copy(probs[:, i % 2], pp[2][:].rearrange("p b n -> p (b n)")).then_inc(s["xf_out"], 1)
            act.wait_ge(s["lg_out"], 2)
            act.activation(le_m[:, :, 0:NEG_G], le_m[:, :, 0:NEG_G], ACT.Exp).then_inc(s["route_act"], 1)
            act.wait_ge(s["lg_out"], 3)
            act.activation(rt[:, 4, :], rt[:, 4, :], ACT.Exp).then_inc(s["route_act"], 1)

            act.wait_ge(s["pos_done"], 1)
            act.wait_ge(s["zeroed"], 16)
            gu, yp, htp = pp[0][:, 0, :], pp[0][:, 1, :], pp[1][:, 0, 0:256]
            for q in range(2):
                act.sem_inc(y_kept[q], 32)
            act.sem_inc(s["y_copied"], 1)
            left = [act.alloc_register(f"left{q}") for q in range(2)]
            for q in range(2):
                act.reg_mov(left[q], 32)
            with act.Fori(0, NE // 2) as it:
                for q in range(2):
                    e = it * 2 + q
                    first, end = tiles_of(act, e)
                    with act.Fori(first, end) as w:
                        act.wait_ge(s["gu_ready"], w + 1)
                        act.activation(act_g, gu[0:TT], ACT.Silu).then_inc(s["sg_ready"], 1)
                        act.wait_ge(s["ht_ready"], w + 1)
                        act.copy(hid_t, htp.rearrange("p (k t) -> p k t", k=KH)).then_inc(s["ht_copied"], 1)
                        act.wait_ge(s["y_ready"], w + 1)
                        act.wait_ge(y_kept[q], left[q])
                        act.reg_add(left[q], left[q], 32)
                        act.copy(y_out[q], yp).then_inc(s["y_copied"], 1)
                        act.wait_ge(s["y_copied"], w + 2)
                        for h in range(2):
                            act.dma_start(y_slots[bass.ds(w * TT, TT), 512 * h:512 * h + 512],
                                          y_out[q][TT * h:TT * h + TT]).then_inc(y_kept[q], 16)
            for q in range(2):
                act.wait_ge(y_kept[q], left[q])
            act.sem_inc(s["rows_done"], 1)
            for i in range(NT):
                act.wait_ge(s["fin_sq"], i + 1)
                act.activation(junk, resid[:, i, :], ACT.Square, accum_out=stat[:, 5, i:i + 1])\
                    .then_inc(s["fin_ms"], 1)
                act.wait_ge(s["fin_ms"], 2 * i + 2)
                act.activation(stat[:, 6, i:i + 1], stat[:, 6, i:i + 1], ACT.Sqrt).then_inc(s["fin_sqrt"], 1)

        @block.vector
        def _(dve):
            steps = [0]

            def step(ins):
                steps[0] += 1
                ins.then_inc(s["dve_step"], 1)
                dve.wait_ge(s["dve_step"], steps[0])

            tt, ts, stt = dve.tensor_tensor, dve.tensor_scalar, dve.scalar_tensor_tensor
            pv = lambda i: prep[:, i, :]

            def cmul(out, x, y, tmp):
                step(tt(tmp[0], x[0], y[0], ALU.mult))
                step(tt(tmp[1], x[1], y[1], ALU.mult))
                step(tt(out[0], tmp[0], tmp[1], ALU.subtract))
                step(tt(tmp[0], x[0], y[1], ALU.mult))
                step(tt(tmp[1], x[1], y[0], ALU.mult))
                step(tt(out[1], tmp[0], tmp[1], ALU.add))

            def unit_length(x, t0, t1):
                step(tt(t0, x[0], x[0], ALU.mult))
                step(tt(t1, x[1], x[1], ALU.mult))
                step(tt(t0, t0, t1, ALU.add))
                step(ts(t0, t0, -0.5, 1.5, ALU.mult, ALU.add))
                for c in x:
                    step(tt(c, c, t0, ALU.mult))

            dve.wait_ge(s["in_cols"], 16)
            for h in range(2):
                dve.wait_ge(s["sq_done"], h + 1)
                for k in range(4 * h, 4 * h + 4):
                    ins = ts(x_t[:, k, :], x_t[:, k, :], g_mix[:, k:k + 1], None, ALU.mult)
                ins.then_inc(s["xg_done"], 1)
            dve.wait_ge(s["prep_act"], 1)
            step(tt(pv(4), a_re, pv(3), ALU.mult))
            tt(pv(5), a_im, pv(3), ALU.mult).then_inc(s["prep_dve"], 1)
            dve.wait_ge(s["prep_dve"], 1)
            dve.wait_ge(s["rstd_ps"], 1)
            ts(rstd_row[:, 0:SEQ], pp[2][:, 0, :], 1.0 / D, EPS, ALU.mult, ALU.add)
            ts(rstd_row[:, SEQ:TOK], pp[2][:, 1, 0:P], 1.0 / D, EPS, ALU.mult, ALU.add).then_inc(s["rstd_act"], 1)
            step(ts(pv(7), pv(5), 1.0 / (2 * np.pi), MAGIC, ALU.mult, ALU.add))
            step(ts(pv(7), pv(7), -MAGIC, None, ALU.add))
            step(stt(pv(8), pv(7), -TWO_PI[0], pv(5), ALU.mult, ALU.add))
            step(stt(pv(8), pv(7), -TWO_PI[1], pv(8), ALU.mult, ALU.add))
            step(stt(pv(8), pv(7), -TWO_PI[2], pv(8), ALU.mult, ALU.add))
            ts(pv(8), pv(8), 3.1415925, -3.1415925, ALU.min, ALU.max).then_inc(s["prep_dve"], 1)
            dve.wait_ge(s["rstd_act"], 2)
            dve.reciprocal(rstd_row[:], rstd_row[:]).then_inc(s["rstd_done"], 1)
            dve.wait_ge(s["rstd_done"], 1)

            def proj_out(n):
                dve.wait_ge(s["proj_ps"], n + 1)
                t = pp[n % 2]
                if n < GB:
                    out = u_stage[:, n].rearrange("p s n -> p n s")
                    tt(out[:, 0:NCP, :], t[:, 0, :].rearrange("p (n s) -> p n s", s=T),
                       rstd_row[:, 0:SEQ].rearrange("p (n s) -> p n s", s=T), ALU.mult)
                    tt(out[:, NCP:NC, :], t[:, 1, 0:P].rearrange("p (n s) -> p n s", s=T),
                       rstd_row[:, SEQ:TOK].rearrange("p (n s) -> p n s", s=T), ALU.mult).then_inc(s["u_out"], 1)
                    dve.wait_ge(s["u_out"], n + 1)
                else:
                    out = k_t[:] if n == GB else q_t[:, n - GB - 1, :]
                    tt(out[:, 0:SEQ], t[:, 0, :], rstd_row[:, 0:SEQ], ALU.mult)
                    step(tt(out[:, SEQ:TOK], t[:, 1, 0:P], rstd_row[:, SEQ:TOK], ALU.mult))
                dve.sem_inc(s["proj_out"], 1)

            proj_out(0)
            dve.wait_ge(s["stat_cols"], 1)
            dve.tensor_copy(stat[:, 0, :], pp[2][:, 0, 0:NT]).then_inc(s["cols_read"], 1)
            dve.wait_ge(s["prep_act"], 3)
            step(tt(pv(10), pv(10), pv(10), ALU.mult))
            step(ts(pv(11), pv(10), -2.0, 1.0, ALU.mult, ALU.add))
            a1 = (pw[:, 0, T - 1, :], pw[:, 1, T - 1, :])
            step(tt(a1[0], pv(6), pv(11), ALU.mult))
            step(tt(a1[1], pv(6), pv(9), ALU.mult))
            step(tt(pv(12), a_re, a_re, ALU.mult))
            step(tt(pv(13), a_im, a_im, ALU.mult))
            step(tt(pv(12), pv(12), pv(13), ALU.add))
            step(dve.reciprocal(pv(13), pv(12)))
            step(ts(pv(14), a1[0], -1.0, None, ALU.add))
            step(tt(pv(15), pv(14), a_re, ALU.mult))
            step(tt(pv(16), a1[1], a_im, ALU.mult))
            step(tt(pv(15), pv(15), pv(16), ALU.add))
            step(tt(pv(16), a1[1], a_re, ALU.mult))
            step(tt(pv(17), pv(14), a_im, ALU.mult))
            step(tt(pv(16), pv(16), pv(17), ALU.subtract))
            step(tt(pv(15), pv(15), pv(13), ALU.mult))
            step(tt(pv(16), pv(16), pv(13), ALU.mult))
            proj_out(1)
            power = lambda n: (pw[:, 0, T - n, :], pw[:, 1, T - n, :])
            for n, (x, y) in {2: (1, 1), 3: (2, 1), 4: (2, 2), 5: (4, 1), 6: (4, 2), 7: (4, 3), 8: (4, 4)}.items():
                cmul(power(n), power(x), power(y), (pv(12), pv(14)))
            f = [pv(15 + i).unsqueeze(2).to_broadcast([P, R, GC]) for i in range(2)]
            c1 = probs[:, 1, 0:256].rearrange("p (r c) -> p r c", r=R)
            c2 = probs[:, 1, 256:512].rearrange("p (r c) -> p r c", r=R)
            cmul((bbar[:, 0], bbar[:, 1]), (ssm_b[:, 0], ssm_b[:, 1]), f, (c1, c2))
            step(dve.tensor_copy(pv(18), pv(11)))
            step(dve.tensor_copy(pv(19), pv(9)))
            unit_length((pv(18), pv(19)), pv(12), pv(14))
            for n in range(3):
                src, dst = ((pv(18), pv(19)), (pv(12), pv(14)))
                cmul(dst, src, src, (pv(13), pv(17)))
                step(dve.tensor_copy(pv(18), pv(12)))
                step(dve.tensor_copy(pv(19), pv(14)))
                step(tt(pv(6), pv(6), pv(6), ALU.mult))
            unit_length((pv(18), pv(19)), pv(12), pv(14))
            dve.sem_inc(s["bbar_done"], 1)
            proj_out(2)
            proj_out(3)
            step(ts(ssm_c[:, 1], ssm_c[:, 1], -1.0, None, ALU.mult))
            cr, ci = ssm_c[:, 0], ssm_c[:, 1]
            for t in range(T):
                ar, ai = [x.unsqueeze(2).to_broadcast([P, R, GC]) for x in power(t + 1)]
                tt(c1, cr, ar, ALU.mult)
                step(tt(c2, ci, ai, ALU.mult))
                step(tt(out_tab[:, :, 0, t, :], c1, c2, ALU.add))
                tt(c1, ci, ar, ALU.mult)
                step(tt(c2, cr, ai, ALU.mult))
                step(tt(out_tab[:, :, 1, t, :], c1, c2, ALU.subtract))
                if t % 2 and 4 + t // 2 < 9:
                    proj_out(4 + t // 2)
            dve.sem_inc(s["out_tab_done"], 1)
            proj_out(8)
            dve.wait_ge(s["cols_read"], 1)
            for i in range(NT):
                dve.wait_ge(s["kv_ps"], i + 1)
                ts(kv_row[:, i, :], pp[3][:, i % 2, 0:256], stat[:, 0, i:i + 1], None, ALU.mult)\
                    .then_inc(s["kv_out"], 1)
            step(dve.tensor_copy(decay, pv(6).unsqueeze(2).to_broadcast([P, R, NCP])))
            dve.memset(decay[:, :, 0:1], 0.0)

            dve.wait_ge(s["rot_ready"], 1)
            dve.wait_ge(s["sum_out"], 8)
            sr, si = sums[:, 0, :, 0:NCP], sums[:, 1, :, 0:NCP]
            wr, wi = rot
            t0, t1, t2 = rot_tmp
            tt(t0, sr, wr, ALU.mult)
            step(tt(t1, si, wi, ALU.mult))
            step(tt(roll[0], t0, t1, ALU.add))
            tt(t0, si, wr, ALU.mult)
            step(tt(t1, sr, wi, ALU.mult))
            step(tt(roll[1], t0, t1, ALU.subtract))
            fl = lambda x: x.rearrange("p r n -> p (r n)")
            for i in range(2):
                dve.tensor_tensor_scan(fl(rot_tmp[i]), fl(decay), fl(roll[i]), 0.0, ALU.mult, ALU.add)\
                    .then_inc(s["decay_used"], 1)
            step(dve.memset(states[:, :, :, 0:1], 0.0))
            tt(roll[0], t0, wr, ALU.mult)
            step(tt(roll[1], t1, wi, ALU.mult))
            tt(states[:, :, 0, 1:NCP], roll[0][:, :, 0:NCP - 1], roll[1][:, :, 0:NCP - 1], ALU.subtract)
            step(tt(h_last[:, 0], roll[0][:, :, NCP - 1], roll[1][:, :, NCP - 1], ALU.subtract))
            tt(roll[0], t0, wi, ALU.mult)
            step(tt(roll[1], t1, wr, ALU.mult))
            tt(h_last[:, 1], roll[0][:, :, NCP - 1], roll[1][:, :, NCP - 1], ALU.add)
            tt(states[:, :, 1, 1:NCP], roll[0][:, :, 0:NCP - 1], roll[1][:, :, 0:NCP - 1], ALU.add)\
                .then_inc(s["states_done"], 1)

            def before_exp(n, rows, src, sink):
                mx, m, neg, es = [sm[:, n % 2, i, 0:rows] for i in (0, 1, 2, 4)]
                step(dve.tensor_reduce(mx, src, AX.X, ALU.max))
                if sink is None:
                    step(ts(m, mx, SCALE, sink_d, ALU.mult, ALU.max))
                    step(ts(es, m, -1.0, sink_d, ALU.mult, ALU.add))
                else:
                    step(stt(m, mx, SCALE, sink, ALU.mult, ALU.max))
                    step(tt(es, sink, m, ALU.subtract))
                ts(neg, m, -1.0, None, ALU.mult).then_inc(s["neg_done"], 1)

            def after_exp(n, rows, view):
                dve.wait_ge(s["exp_done"], n + 1)
                total, es, rd = [sm[:, n % 2, i, 0:rows] for i in (3, 4, 5)]
                step(tt(total, total, es, ALU.add))
                step(dve.reciprocal(rd, total))
                for h in range(rows):
                    ins = ts(view(h), view(h), rd[:, h:h + 1], None, ALU.mult)
                ins.then_inc(s["norm_done"], 1)

            def masked(n):
                m, v = n // 2, n % 2
                lo = 0 if m else P
                pr = probs[:, v].rearrange("p (h n) -> p h n", h=QPK)[:, :, lo:256]
                sc = pp[0][:].rearrange("p b (h n) -> p (b h) n", h=2)[:, :, lo:256]
                dve.wait_ge(s["sc_ps"], n + 1)
                if n >= 2:
                    dve.wait_ge(s["pt_ps"], n - 1)
                tt(pr, sc, mask[:, lo:256].unsqueeze(1).to_broadcast([P, QPK, 256 - lo]), ALU.add)\
                    .then_inc(s["sc_read"], 1)
                dve.wait_ge(s["sc_read"], n + 1)
                before_exp(n, QPK, pr, sink_row[:, QPK * v:QPK * v + QPK])

            def unit_out(n):
                lo = 0 if n >= 2 else P
                pr = probs[:, n % 2].rearrange("p (h n) -> p h n", h=QPK)
                after_exp(n, QPK, lambda h: pr[:, h, lo:256])

            def attn_out(m):
                dve.wait_ge(s["av_sq"], m + 1)
                src = pp[3][:, 0, :]
                if m < NT - 1:
                    dst = attn_t[:, :, P * m:P * m + P]
                    ins = tt(dst, src.rearrange("p (h t) -> p h t", h=QPK),
                       g_attn.unsqueeze(2).to_broadcast([P, QPK, P]), ALU.mult)
                else:
                    for h in range(QPK):
                        ins = ts(attn_t[:, h, SEQ:TOK].rearrange("p (b t) -> p b t", b=NB),
                           src.rearrange("p (b h t) -> p b h t", b=NB, h=QPK)[:, :, h, :],
                           g_attn[:, h:h + 1], None, ALU.mult)
                ins.then_inc(s["attn_done"], 1)

            dve.wait_ge(s["in_small"], 48)
            masked(0)
            for n in range(8):
                if n + 1 < 8:
                    masked(n + 1)
                unit_out(n)
                if n % 2 == 0 and n >= 2:
                    attn_out(n // 2 - 1)
            attn_out(3)
            dve.wait_ge(s["in_attn"], 32)
            dve.tensor_copy(kd_t[:, :, WIN:NK], k_t[:, SEQ:TOK].rearrange("p (b t) -> p b t", b=NB))
            dve.wait_ge(s["attn_z"], 1)
            for v in range(NKV):
                rows = slice(HD * v, HD * v + HD)
                ins = dve.tensor_copy(q_z[rows, :, v, :, :],
                                      q_t[rows, :, SEQ:TOK].rearrange("p h (b t) -> p b h t", b=NB))
            ins.then_inc(s["streams_ready"], 1)
            for j in range(3):
                nb = min(3, NB - 3 * j)
                n = 8 + j
                dve.wait_ge(s["sc_ps"], n + 1)
                sc = pp[0][:, j % 2, 0:nb * NK].rearrange("p (b n) -> p b n", b=nb)
                dve.wait_ge(s["pt_ps"], n - 1)
                before_exp(n, nb, sc, None)
                pr = probs[:, j % 2, 0:3 * NK].rearrange("p (b n) -> p b n", b=3)
                after_exp(n, nb, lambda b: pr[:, b, :])
            attn_out(NT - 1)

            for n in range(GB):
                dve.wait_ge(s["sig_done"], n + 1)
                tt(mix_t[:, n, :].rearrange("p (n t) -> p t n", t=T), y_g[:, n, :].rearrange("p (t n) -> p t n", t=T),
                   mix_sq[:, n, :].rearrange("p (t n) -> p t n", t=T), ALU.mult).then_inc(s["mix_done"], 1)
            for n in range(GB):
                dve.wait_ge(s["mixsq_done"], n + 1)
                ins = ts(mix_t[:, n, :], mix_t[:, n, :], g_ssm[:, n:n + 1], None, ALU.mult)
            ins.then_inc(s["mix_done"], 1)
            dve.wait_ge(s["ssq_ps"], NT + 1)
            ts(stat[:, 1:3, :], pp[3][:, 1, 0:2 * NT].rearrange("p (m i) -> p m i", m=2), 1.0 / W, EPS,
               ALU.mult, ALU.add).then_inc(s["rs_done"], 1)
            dve.wait_ge(s["rs_act"], 1)
            step(dve.reciprocal(stat[:, 1:3, :], stat[:, 1:3, :]))

            def ffn_norm(i):
                dve.wait_ge(s["ffn_sq"], i + 1)
                ts(stat[:, 4, i:i + 1], stat[:, 3, i:i + 1], 1.0 / D, EPS, ALU.mult, ALU.add).then_inc(s["ffn_ms"], 1)
                dve.wait_ge(s["ffn_sqrt"], i + 1)
                step(dve.reciprocal(stat[:, 4, i:i + 1], stat[:, 4, i:i + 1]))
                stt(ffn_in[:, i, :], resid[:, i, :], stat[:, 4, i:i + 1], g_ffn[:], ALU.mult, ALU.mult)\
                    .then_inc(s["ffn_done"], 1)

            dve.wait_ge(s["in_resid"], 16)
            dve.wait_ge(s["in_rows"], 48)
            for i in range(NT):
                for m in range(2):
                    dve.wait_ge(s["op_ps"], 2 * i + m + 1)
                    stt(resid[:, i, :], pp[m][:].rearrange("p b n -> p (b n)"), stat[:, 1 + m, i:i + 1],
                        resid[:, i, :], ALU.mult, ALU.add).then_inc(s["op_out"], 1)
                    dve.wait_ge(s["op_out"], 2 * i + m + 1)
                ffn_norm(i)
            dve.wait_ge(s["lg_ps"], NT)
            lg = pp[3][:, 0, 0:NT * NR].rearrange("p (i n) -> p i n", i=NT)
            step(tt(logit, lg, b_r[:].unsqueeze(1).to_broadcast([P, NT, NR]), ALU.add))

            bc = lambda x, n: x.unsqueeze(2).to_broadcast([P, NT, n])
            experts = lambda: iota_e[:].unsqueeze(1).to_broadcast([P, NT, NE])
            step(dve.tensor_copy(pad8[:, :, 0:NEG_G], logit[:, :, 0:NEG_G]))
            for i in range(NT):
                ins = dve.max(top_g[:, i, :], pad8[:, i, :])
            step(ins)
            for i in range(NT):
                ins = dve.max_index(ig[:, i, :], top_g[:, i, :], pad8[:, i, :])
            ins.then_inc(s["lg_out"], 1)
            dve.wait_ge(s["lg_out"], 1)
            tt(le_m[:, :, 0:NEG_G], logit[:, :, 0:NEG_G], bc(top_g[:, :, 0], NEG_G), ALU.subtract)\
                .then_inc(s["lg_out"], 1)
            step(dve.tensor_copy(rt[:, 0, :], ig[:, :, 0]))
            step(tt(one_g, iota_e[:, 0:NEG_G].unsqueeze(1).to_broadcast([P, NT, NEG_G]), bc(rt[:, 0, :], NEG_G),
                    ALU.is_equal))
            dve.wait_ge(s["route_act"], 1)
            step(dve.tensor_reduce(rt[:, 1, :], le_m[:, :, 0:NEG_G], AX.X, ALU.add))
            step(tt(le_m.rearrange("p i (g e) -> p i g e", g=NEG_G),
                    logit[:, :, NEG_G:NR].rearrange("p i (g e) -> p i g e", g=NEG_G),
                    one_g.unsqueeze(3).to_broadcast([P, NT, NEG_G, EPG]), ALU.mult))
            step(dve.tensor_reduce(le_g, le_m.rearrange("p i (g e) -> p i e g", g=NEG_G), AX.X, ALU.add))
            for i in range(NT):
                ins = dve.max(top_e[:, i, :], le_g[:, i, :])
            step(ins)
            for i in range(NT):
                ins = dve.max_index(ie[:, i, :], top_e[:, i, :], le_g[:, i, :])
            step(ins)
            tt(rt[:, 4, :], top_e[:, :, 1], top_e[:, :, 0], ALU.subtract).then_inc(s["lg_out"], 1)
            for k in range(2):
                step(dve.tensor_copy(rt[:, 2 + k, :], ie[:, :, k]))
                step(stt(rt[:, 2 + k, :], rt[:, 0, :], float(EPG), rt[:, 2 + k, :], ALU.mult, ALU.add))
                step(tt(pair[:, k], experts(), bc(rt[:, 2 + k, :], NE), ALU.is_equal))
            tt(both, pair[:, 0], pair[:, 1], ALU.add).then_inc(s["pair_done"], 1)
            dve.wait_ge(s["route_act"], 2)
            step(ts(rt[:, 5, :], rt[:, 4, :], 1.0, None, ALU.add))
            step(tt(rt[:, 5, :], rt[:, 5, :], rt[:, 1, :], ALU.mult))
            step(dve.reciprocal(rt[:, 6, :], rt[:, 5, :]))
            step(tt(rt[:, 7, :], rt[:, 6, :], rt[:, 4, :], ALU.mult))
            dve.wait_ge(s["place_ps"], 1)
            pl = pp[3][:, 1, 0:NT * NE].rearrange("p (i e) -> p i e", i=NT)
            step(stt(place, pl, 1.0, both, ALU.add, ALU.mult))
            step(ts(place_e.rearrange("p e i -> p i e"), place, -1.0, None, ALU.add))
            step(ts(ntile[:, 0, :], pp[3][:, 1, 256:256 + NE], 1.0 / TT, (TT - 1) / (2.0 * TT), ALU.mult, ALU.add))
            step(ts(ntile[:, 0, :], ntile[:, 0, :], MAGIC, None, ALU.add))
            step(ts(ntile[:, 0, :], ntile[:, 0, :], -MAGIC, 1.0, ALU.add, ALU.max))
            step(dve.memset(first_f[:, 0:1], 0.0))
            step(dve.tensor_tensor_scan(first_f[:, 1:NE + 1], ones[:, 0:NE], ntile[:, 0, :], 0.0, ALU.mult, ALU.add))
            step(ts(ntile[:, 1, :], first_f[:, 0:NE], float(TT), None, ALU.mult))
            step(tt(place, pl, ntile[:, 1, :].unsqueeze(1).to_broadcast([P, NT, NE]), ALU.add))
            for k in range(2):
                step(tt(ptmp[:, k], place, pair[:, k], ALU.mult))
                step(dve.tensor_reduce(rt[:, 8 + k, :], ptmp[:, k], AX.X, ALU.add))
                step(dve.tensor_copy(pos_u[:, k, :], rt[:, 8 + k, :]))
            dve.tensor_copy(first_i[:], first_f[0:1, :]).then_inc(s["pos_done"], 1)
            dve.wait_ge(s["pos_done"], 1)

            gu, gx, xtp = pp[0][:, 0, :], pp[2][:, 0, :], pp[2][:, 1, :]

            def keep_x(w1):
                dve.wait_ge(s["gx_ready"], w1 + 1)
                dve.tensor_copy(xrow, gx).then_inc(s["gx_copied"], 1)

            def keep_xt(w1):
                dve.wait_ge(s["xt_ready"], w1)
                dve.tensor_copy(xt_e, xtp.rearrange("p (c n) -> p c n", c=4)).then_inc(s["xt_copied"], 1)

            def select(w1):
                dve.wait_ge(s["place_ready"], w1)
                dve.wait_ge(s["gx_ready"], w1)
                for i in range(NT):
                    ins = ts(sel[:, i, :], iota_t[:], place_c[:, i:i + 1], None, ALU.is_equal)
                ins.then_inc(s["sel_ready"], 1)

            dve.sem_inc(s["gx_ready"], 1)
            select(1)
            keep_x(1)
            keep_xt(1)
            with dve.Fori(0, NE) as e:
                first, end = tiles_of(dve, e)
                with dve.Fori(first, end) as w:
                    select(w + 2)
                    dve.wait_ge(s["sg_ready"], w + 1)
                    tt(hid, gu[TT:P], act_g, ALU.mult).then_inc(s["h_ready"], 1)
                    keep_x(w + 2)
                    keep_xt(w + 2)

            for i in range(NT):
                dve.wait_ge(got_in[i % 2], 32 * (i // 2 + 1))
                for k in range(2):
                    ins = stt(resid[:, i, :], got[i % 2][k], rt[:, 6 + k, i:i + 1], resid[:, i, :], ALU.mult, ALU.add)
                    if k == 0:
                        step(ins)
                ins.then_inc(s["fin_sq"], 1)
                dve.wait_ge(s["fin_ms"], 2 * i + 1)
                ts(stat[:, 6, i:i + 1], stat[:, 5, i:i + 1], 1.0 / D, EPS, ALU.mult, ALU.add).then_inc(s["fin_ms"], 1)
                dve.wait_ge(s["fin_sqrt"], i + 1)
                step(dve.reciprocal(stat[:, 6, i:i + 1], stat[:, 6, i:i + 1]))
                if i >= 2:
                    dve.wait_ge(fin_out[i % 2], 16 * (i // 2))
                stt(fin[i % 2], resid[:, i, :], stat[:, 6, i:i + 1], g_fin[:], ALU.mult, ALU.mult)\
                    .then_inc(s["fin_done"], 1)


def _layout(x):
    c = np.ascontiguousarray
    pairs = lambda v: v.reshape(R, 2, NS, *v.shape[2:]).transpose(1, 2, 0, *range(3, v.ndim + 1)).reshape(
        P, R, *v.shape[2:])
    rows = np.concatenate([x["x_prompt"].reshape(SEQ, D), x["x_sample"].reshape(NB * LS, D)], 0)
    w_in = x["w_in"][0]
    q = w_in[:, 0:W].reshape(D, NKV, QPK, HD).transpose(0, 2, 1, 3).reshape(D, W)
    w_out = x["w_out"][0]
    ssm_o = w_out[W:].reshape(GB, P, D).transpose(1, 0, 2)
    att_o = w_out[0:W].reshape(NKV, QPK, HD, D).transpose(0, 2, 1, 3).reshape(P, QPK, D)
    ck = x["cache_k"][0]
    return {
        "x_rows": c(rows),
        "x_t": c(rows.T.reshape(P, KD, TOK)),
        "w_in_u": c(w_in[:, W + 2 * P:]),
        "w_in_qkv": c(np.concatenate([q, w_in[:, W:W + 2 * P]], 1)),
        "w_out": c(np.concatenate([att_o, ssm_o], 1)),
        "w_glu": c(x["w_glu"][0]),
        "cache_k_t": c(ck.transpose(2, 3, 0, 1).reshape(P, NB, WIN)),
        "cache_k": c(ck.reshape(NB, WIN, P)),
        "cache_v": c(x["cache_v"][0].reshape(NB, WIN, P)),
        "cols": c(np.concatenate(
            [x["g_norm_mix"][0].reshape(P, KD),
             x["g_attn_out"][0].reshape(NKV, QPK, HD).transpose(0, 2, 1).reshape(P, QPK),
             x["g_ssm_out"][0].reshape(GB, P).T, x["b_glu"][0].reshape(GB, P).T,
             np.repeat(x["attn_sinks"][0], LS)[:, None]], 1)),
        "g_norm_ffn": c(x["g_norm_ffn"]),
        "g_final": c(x["g_final"][None]),
        "sinks": c(x["attn_sinks"]),
        "ssm_d": c(x["ssm_d"][0].reshape(G, GC).T),
        "w_router": c(np.concatenate([x["w_router_group"][0], x["w_router_expert"][0]], 1)),
        "b_router": c(np.concatenate([x["b_router_group"], x["b_router_expert"]], 1)),
        "tables": c(np.concatenate(
            [pairs(x[n][0]).reshape(P, -1) for n in ("ssm_a_re", "ssm_a_im", "ssm_b_re", "ssm_b_im")]
            + [pairs(x[n][0].transpose(0, 2, 1)).reshape(P, -1) for n in ("ssm_c_re", "ssm_c_im")]
            + [pairs(x[n][0].transpose(1, 2, 0)).reshape(P, -1) for n in ("state_ssm_re", "state_ssm_im")], 1)),
        "log_dt": c(x["ssm_log_dt"][0].reshape(R, 2).T),
        "w_exp_gate": c(x["w_exp_gate"][0]),
        "w_exp_up": c(x["w_exp_up"][0]),
        "w_exp_down": c(x["w_exp_down"][0]),
    }


_OUTS = {
    "y": (TOK, D), "new_k_prompt": (WIN, P), "new_v_prompt": (WIN, P),
    "new_k_sample": (NB, WIN, P), "new_v_sample": (NB, WIN, P),
    "state_prompt": (P, 2, R), "state_sample": (P, 2, R, NB),
}


def kernel(**inputs):
    import concourse.bacc as _bacc
    from concourse.bass_utils import run_bass_kernel_spmd as _run

    arrays = _layout({k: np.asarray(v) for k, v in inputs.items()})
    nc = _bacc.Bacc("TRN2", target_bir_lowering=False, num_devices=1)
    a = {n: nc.dram_tensor(f"in_{n}", v.shape, mybir.dt.from_np(v.dtype), kind="ExternalInput").ap()
         for n, v in arrays.items()}
    o = {n: nc.dram_tensor(f"out_{n}", shape, F32, kind="ExternalOutput").ap() for n, shape in _OUTS.items()}
    build(nc, a, o)
    got = _run(nc, [{f"in_{n}": v for n, v in arrays.items()}], core_ids=[0]).results[0]
    got = {n: got[f"out_{n}"] for n in _OUTS}
    y = got["y"]
    states = lambda v, i: np.ascontiguousarray(v[:, i].reshape(2, NS, R, -1).transpose(3, 2, 0, 1)).reshape(
        1, -1, G, NS)
    heads = lambda v: v.reshape(1, -1, WIN, NKV, HD)
    return (y[0:SEQ].reshape(1, SEQ, D), y[SEQ:].reshape(NB, LS, D),
            heads(got["new_k_prompt"]), heads(got["new_v_prompt"]),
            states(got["state_prompt"], 0), states(got["state_prompt"], 1),
            heads(got["new_k_sample"]), heads(got["new_v_sample"]),
            states(got["state_sample"], 0), states(got["state_sample"], 1))
```

```python
from contextlib import ExitStack

import numpy as np

import concourse.bass as bass
from concourse import mybir

F32 = mybir.dt.float32
BF16 = mybir.dt.bfloat16
I32 = mybir.dt.int32
U32 = mybir.dt.uint32
ALU = mybir.AluOpType
ACT = mybir.ActivationFunctionType
AX = mybir.AxisListType

P = 128
D = 1024
SEQ = 512
NB, LS = 8, 16
TOK = SEQ + NB * LS
NT = TOK // P
KD = D // P
HD = 64
NKV, QPK = 2, 4
WIN = 128
NK = WIN + LS
G, GC, NS = 32, 16, 64
R = G // 2
T = 8
NC = TOK // T
NCP = SEQ // T
W = 512
GB = W // P
PROJ = 1280
NE, NEG_G, EPG, DE = 32, 4, 8, 512
NR = NEG_G + NE
TT = 64
KH = DE // P
TILES_MAX = 2 * TOK // TT + NE
SLOTS = TILES_MAX * TT
EPS = 1e-6
SCALE = HD ** -0.5
OP_PAIR = (2, 0, 2, 0, 2, 1, 2, 1, 2, 1)
BESIDE = ((), (), (), (0, 1, 2), (3, 4), (5, 6), (7,), ())
TABLES = 2 * R + 4 * R * GC + 2 * R * NB
MASKED = -1e30
MAGIC = 1.5 * 2.0 ** 23
TWO_PI = (6.28125, 0.0019350051879882812, 3.019916050561733e-07)


def build(nc, a, o):
    with ExitStack() as ctx:
        def sb(name, shape, dt=F32):
            return ctx.enter_context(nc.sbuf_tensor(name, shape, dt))

        def sem(name):
            return ctx.enter_context(nc.semaphore(name))

        slot = [sb(f"slot{i}", [P, 12288]) for i in range(2)]
        reg_x = sb("reg_x", [P, 5120])
        reg_f = sb("reg_f", [P, 5120])
        reg_h = sb("reg_h", [P, 5120])

        sum_w = slot[0][:, 0:4096].rearrange("p (r i m) -> p r i m", r=R, i=2)
        conv_w = slot[0][:, 4096:8192].rearrange("p (g m) -> p g m", g=G)
        out_tab = slot[0][:, 8192:12288].rearrange("p (r i t c) -> p r i t c", r=R, i=2, t=T)
        u_stage = slot[0][:, 0:2560].rearrange("p (b s n) -> p b s n", b=GB, s=T)
        rot_tmp = [slot[0][:, 1024 * i:1024 * i + 1024].rearrange("p (r n) -> p r n", r=R)
                   for i in range(3)]
        w_u = slot[1][:, 0:4096].rearrange("p (k n) -> p k n", k=KD)
        w_qkv = slot[1][:, 4096:10240].rearrange("p (k n) -> p k n", k=KD)
        w_out = slot[1][:, 0:8192].rearrange("p (k n) -> p k n", k=KD)
        w_glu = slot[1][:, 8192:10240].rearrange("p (k n) -> p k n", k=GB)
        rot = [slot[1][:, 10240 + 1024 * i:11264 + 1024 * i].rearrange("p (r n) -> p r n", r=R)
               for i in range(2)]
        kern = slot[1][:, 0:4096].rearrange("p (g m) -> p g m", g=G)
        skip_tmp = slot[1][0:GC, 4096:4608].rearrange("p (g c) -> p g c", g=G)
        decay = slot[1][:, 5120:6144].rearrange("p (r n) -> p r n", r=R)
        x_t = reg_h[:].rearrange("p (k t) -> p k t", k=KD)
        attn_t = reg_h[:, 0:2560].rearrange("p (h t) -> p h t", h=QPK)
        y_t = reg_h[:, 2560:5120].rearrange("p (b t) -> p b t", b=GB)
        mix_t = y_t
        roll = [reg_h[:, 2560 + 1024 * i:3584 + 1024 * i].rearrange("p (r n) -> p r n", r=R) for i in range(2)]
        x_sq = reg_x[:].rearrange("p (k t) -> p k t", k=KD)
        u_c = reg_x[:, 0:2560].rearrange("p (g n) -> p g n", g=G)
        y_g = reg_x[:, 0:2560].rearrange("p (b t) -> p b t", b=GB)
        states = reg_x[:, 2560:5120].rearrange("p (r i n) -> p r i n", r=R, i=2)
        mix_sq = reg_x[:, 2560:5120].rearrange("p (b t) -> p b t", b=GB)
        q_t = reg_f[:, 0:2560].rearrange("p (h t) -> p h t", h=QPK)
        kd_t = reg_f[:, 2560:3712].rearrange("p (b n) -> p b n", b=NB)
        v_old = reg_f[:, 3712:4736].rearrange("p (b n) -> p b n", b=NB)
        resid = reg_f[:].rearrange("p (i n) -> p i n", i=NT)

        k_t = sb("k_t", [P, TOK])
        kv_row = sb("kv_row", [P, NT, 256])
        sums = sb("sums", [P, 2, R, NC])
        sums_f = sums[:].rearrange("p i r n -> p (i r n)")
        v_t = sums_f[:, 1920:2560]
        v_new = sums[0:LS, 0].rearrange("p r n -> p (r n)")[:, 0:NB * P].rearrange("p (b n) -> p b n", b=NB)
        kv_f = kv_row[:].rearrange("p i n -> p (i n)")
        rstd_row = sb("rstd_row", [P, TOK])
        probs = sb("probs", [P, 2, 1024])
        soft = [probs[:, 0], probs[:, 1], slot[1][:, 10240:11264]]
        probs_t = sb("probs_t", [P, 1024])
        turned = [probs_t[:], slot[1][:, 11264:12288]]
        bp_buf = sb("bp_buf", [P, 1024])
        bp = bp_buf[:].rearrange("p (r i s c) -> p r i s c", r=4, i=2, s=T)
        q_z = bp_buf[:].rearrange("p (b v h t) -> p b v h t", b=NB, v=NKV, h=QPK)
        tables = sb("tables", [P, TABLES])
        a_re, a_im = tables[:, 0:R], tables[:, R:2 * R]
        ssm_b, ssm_c = [tables[:, 2 * R + 2 * R * GC * n:2 * R + 2 * R * GC * (n + 1)]
                        .rearrange("p (i r c) -> p i r c", i=2, r=R) for n in range(2)]
        h0 = tables[:, 2 * R + 4 * R * GC:TABLES].rearrange("p (i r b) -> p i r b", i=2, r=R)
        bbar = sb("bbar", [P, 2, R, GC])
        bbar_f = bbar[:].rearrange("p i r c -> p (i r c)")
        pw = sb("pw", [P, 2, T, R])
        prep = sb("prep", [P, 32, R])
        h_last = sb("h_last", [P, 2, R])
        h_dec = sb("h_dec", [P, 2, R, NB])
        dec_tmp = bp_buf[:, 0:512].rearrange("p (i r b) -> p i r b", i=4, r=R)
        mask = reg_f[:, 4736:4992]
        ident = sb("ident", [P, P])
        ones = sb("ones", [P, P])
        before = sb("before", [P, P])
        cols = sb("cols", [P, 21])
        g_mix = cols[:, 0:8]
        g_attn = cols[:, 8:12]
        g_ssm = cols[:, 12:16]
        b_glu = cols[:, 16:20]
        sink_d = cols[:, 20:21]
        sink_row = sb("sink_row", [P, 8])
        skip = sb("skip", [GC, G])
        w_r = tables[:, 2 * R:2 * R + KD * NR].rearrange("p (k n) -> p k n", k=KD)
        b_r = sb("b_r", [P, NR])
        sm = sb("sm", [P, 3, 6, 4])
        stat = sb("stat", [P, 8, NT])
        g_ffn = probs_t
        g_fin = bp_buf
        pair = kv_f[:, 0:320].rearrange("p (k i e) -> p k i e", k=2, i=NT)
        ptmp = kv_f[:, 320:640].rearrange("p (k i e) -> p k i e", k=2, i=NT)
        both, place, le_m = [kv_f[:, 640 + 160 * n:800 + 160 * n].rearrange("p (i e) -> p i e", i=NT)
                             for n in range(3)]
        le_g, top_g, top_e = [kv_f[:, 1120 + 40 * n:1160 + 40 * n].rearrange("p (i e) -> p i e", i=NT)
                              for n in range(3)]
        one_g = kv_f[:, 1240:1260].rearrange("p (i e) -> p i e", i=NT)
        place_e = rstd_row[:, 0:160].rearrange("p (e i) -> p e i", e=NE)
        tiles_before = rstd_row[:, 340:532].rearrange("p (i e) -> p i e", e=NE)
        logit = rstd_row[:, 160:340].rearrange("p (i n) -> p i n", i=NT)
        pad8 = sb("pad8", [P, NT, 8])
        ig = sb("ig", [P, NT, 8], U32)
        ie = sb("ie", [P, NT, 8], U32)
        iota_e = sb("iota_e", [P, NE])
        iota_t = sb("iota_t", [P, TT])
        tile_tt = sb("tile_tt", [P, NT])
        zero_nt = sb("zero_nt", [P, NT])
        rt = sb("rt", [P, 12, NT])
        pos_u = sb("pos_u", [P, 2, NT], U32)
        ntile = sb("ntile", [P, 3, NE])
        first_f = sb("first_f", [P, NE + 1])
        first_i = sb("first_i", [1, NE + 1], I32)

        ffn_in = [slot[1][:, 10240 + 1024 * i:11264 + 1024 * i] for i in range(2)]
        parts = [[reg_x[:, 2560 * n + 512 * i:2560 * n + 512 * i + 512].bitcast(BF16) for i in range(NT)]
                 for n in range(2)]
        parts += [[r.bitcast(BF16) for r in (k_t[:, 0:512], sums_f[:, 1456:1968], sums_f[:, 1968:2480],
                                             tables[:, 320:832], bbar_f[:, 0:512])]]
        halves = lambda x: x.rearrange("p (h c n) -> p h c n", h=2, c=4)
        gate_w = [halves(r[:, 0:4096]) for r in (slot[0], slot[1], reg_h)]
        up_w = [halves(r) for r in (slot[0][:, 4096:8192], slot[1][:, 4096:8192], reg_f[:, 0:4096])]
        down_w = [[x[:, 8192 + D * k:8192 + D * k + D] for k in range(KH)] for x in slot]
        down_w += [[reg_h[:, 4096:5120], reg_f[:, 4096:5120], probs_t[:], kv_f[:, 0:D]]]

        xrow = probs[:, 0, 0:512]
        xt_e = probs[:, 0, 512:1024].rearrange("p (c n) -> p c n", c=4)
        act_g = probs[0:TT, 1, 0:512]
        hid = probs[0:TT, 1, 512:1024]
        hid_t = sums_f[:, 0:256].rearrange("p (k t) -> p k t", k=KH)
        y_out = [sums_f[:, 256 + 512 * i:768 + 512 * i] for i in range(2)]
        sel = sums_f[:, 1280:1440].bitcast(BF16).rearrange("p (i s) -> p i s", i=NT)
        place_b = sums_f[:, 1440:1445]
        place_c = sums_f[:, 1448:1453]
        got = [[slot[0][:, 2048 * i + 1024 * k:2048 * i + 1024 * k + 1024] for k in range(2)] for i in range(NT)]
        fin = [slot[1][:, 1024 * i:1024 * i + 1024] for i in range(NT)]

        pp = [ctx.enter_context(nc.psum_tensor(f"pair{i}", [P, 2, 512], F32)) for i in range(4)]

        u_scr = nc.dram_tensor("u_scr", [W, T, NC], F32).ap()
        y_scr = nc.dram_tensor("y_scr", [W, T, NC], F32).ap()
        resid_scr = nc.dram_tensor("resid_scr", [TOK, D], F32).ap()
        y_slots = nc.dram_tensor("y_slots", [SLOTS, D], F32).ap()

        names = """
            in_cols in_tables in_small in_x0 in_x1 in_x2 in_x3 in_w_u in_w_qkv in_attn in_resid in_rows
            out_w
            zero_ready zeroed decay_used streams_ready high_done rest_done mid_done parts_done
            const_done dve_step pool_step sq_done rstd_ps rstd_act rstd_done xg_done proj_ps proj_out
            kv_ps kv_out u_out u_stored u_in prep_act prep_dve bbar_done bp_ready bp_tr bp_out
            out_tab_done kern_ps kern_out conv_zero kern_done conv_in sum_ps sum_out states_done y_ps
            y_out_done y_stored y_in gelu_done glu_ps sig_done mix_done mixsq_done sc_ps neg_done
            exp_done norm_done pt_ps pt_out av_ps av_sq attn_done attn_z vnew_in states_out cache_out
            ssq_ps rs_act rs_done op_ps op_out ffn_sq ffn_done xf_tr xf_out lg_ps lg_out route_act
            pair_done place_ps pos_done mixsum_done weighed resid_kept resid_back pairs_used sel_ready
            gx_ready gx_copied xt_ready xt_copied gu_ready sg_ready h_ready ht_ready ht_copied y_ready
            y_copied fin_out fin_sq fin_ms fin_sqrt fin_done sc_read base_step place_ready rows_done
            rot_ready ffn_ms ffn_sqrt fin_ss""".split()
        names += [f"{n}_in{q}" for n in ("gate", "up", "down") for q in range(3)]
        names += [f"y_kept{q}" for q in range(2)] + [f"got{i}" for i in range(NT)]
        s = {n: sem(n) for n in names}
        gate_in, up_in, down_in = [[s[f"{n}_in{q}"] for q in range(3)] for n in ("gate", "up", "down")]
        y_kept = [s["y_kept0"], s["y_kept1"]]
        got_in = [s[f"got{i}"] for i in range(NT)]

        block = ctx.enter_context(nc.Block())

        def tiles_of(eng, e):
            first = eng.value_load(first_i[0:1, bass.ds(e, 1)], min_val=0, max_val=TILES_MAX - 1)
            end = eng.value_load(first_i[0:1, bass.ds(e + 1, 1)], min_val=1, max_val=TILES_MAX)
            return first, end

        gate_v = a["w_exp_gate"].rearrange("e (h p c) n -> e p h c n", h=2, c=4)
        up_v = a["w_exp_up"].rearrange("e (h p c) n -> e p h c n", h=2, c=4)
        down_v = a["w_exp_down"].rearrange("e (p k) n -> e p k n", k=KH)

        @block.sync
        def _(sp):
            for h in range(4):
                kk = slice(2 * h, 2 * h + 2)
                sp.dma_start(x_t[:, kk, :], a["x_t"][:, kk, :]).then_inc(s[f"in_x{h}"], 16)
            sp.dma_start(w_u, a["w_in_u"].rearrange("(p k) n -> p k n", k=KD)).then_inc(s["in_w_u"], 16)
            sp.dma_start(w_qkv, a["w_in_qkv"].rearrange("(p k) n -> p k n", k=KD)).then_inc(s["in_w_qkv"], 16)
            sp.dma_start(kd_t[:, :, 0:WIN], a["cache_k_t"]).then_inc(s["in_attn"], 16)
            sp.dma_start(v_old, a["cache_v"].rearrange("b k n -> k b n")).then_inc(s["in_attn"], 16)
            sp.wait_ge(s["zero_ready"], 1)
            sp.dma_start(y_slots.rearrange("(i p) n -> p i n", p=P),
                         probs_t[:].unsqueeze(1).to_broadcast([P, SLOTS // P, D])).then_inc(s["zeroed"], 16)

            for b in range(GB):
                sp.wait_ge(s["u_out"], b + 1)
                sp.dma_start(u_scr[b * P:(b + 1) * P], u_stage[:, b]).then_inc(s["u_stored"], 16)
            sp.wait_ge(s["u_stored"], 16 * GB)
            sp.wait_ge(s["rstd_ps"], 1)
            us = u_scr.rearrange("(g c) s n -> s c g n", c=GC)
            for t in range(T):
                sp.dma_start(u_c[GC * t:GC * t + GC], us[t]).then_inc(s["u_in"], 16)
            sp.wait_ge(s["conv_zero"], 1)
            sp.wait_ge(s["kern_done"], 1)
            for t in range(T):
                sp.dma_start(conv_w[GC * t:GC * t + GC, :, GC * t:P], kern[0:GC, :, 0:P - GC * t])\
                    .then_inc(s["conv_in"], 16)
            sp.wait_ge(s["kv_out"], 3)
            for n, name in enumerate(("k", "v")):
                sp.dma_start(o[f"new_{name}_prompt"], kv_row[:, NT - 2, P * n:P * n + P])\
                    .then_inc(s["cache_out"], 16)
                for b in range(NB):
                    sp.dma_start(o[f"new_{name}_sample"][b, WIN - LS:WIN, :],
                                 kv_row[LS * b:LS * b + LS, NT - 1, P * n:P * n + P]).then_inc(s["cache_out"], 16)
                sp.dma_start(o[f"new_{name}_sample"][:, 0:WIN - LS, :], a[f"cache_{name}"][:, LS:WIN, :])\
                    .then_inc(s["cache_out"], 16)
            sp.wait_ge(s["conv_in"], 16 * T)
            sp.wait_ge(s["decay_used"], 2)
            sp.dma_start(w_out, a["w_out"]).then_inc(s["out_w"], 16)
            sp.dma_start(w_glu, a["w_glu"].rearrange("(k p) n -> p k n", p=P)).then_inc(s["out_w"], 16)
            sp.wait_ge(s["states_done"], 3)
            for b in range(NB):
                sp.dma_start(v_new[:, b, :], kv_row[LS * b:LS * b + LS, NT - 1, P:256]).then_inc(s["vnew_in"], 16)
            sp.wait_ge(s["y_out_done"], 8)
            ys = y_scr.rearrange("(g c) t n -> t c g n", c=GC)
            for t in range(T):
                sp.dma_start(ys[t], u_c[GC * t:GC * t + GC]).then_inc(s["y_stored"], 16)
            sp.wait_ge(s["y_stored"], 16 * T)
            sp.dma_start(y_t, y_scr.rearrange("(b p) t n -> p b (t n)", p=P)).then_inc(s["y_in"], 16)
            sp.dma_start(o["state_prompt"], h_last[:]).then_inc(s["states_out"], 16)
            sp.dma_start(o["state_sample"], h_dec[:]).then_inc(s["states_out"], 16)

            def load_gate_up(q, e):
                sp.dma_start(gate_w[q], gate_v[e]).then_inc(gate_in[q], 16)
                sp.dma_start(up_w[q], up_v[e]).then_inc(up_in[q], 16)

            def load_down(q, e):
                if q < 2:
                    w = slot[q][:, 8192:12288].rearrange("p (k n) -> p k n", k=KH)
                    for k in range(0, KH, 2):
                        sp.dma_start(w[:, k:k + 2], down_v[e, :, k:k + 2]).then_inc(down_in[q], 16)
                else:
                    for k in range(KH):
                        sp.dma_start(down_w[q][k], down_v[e, :, k]).then_inc(down_in[q], 16)

            sp.wait_ge(s["y_ps"], 8)
            load_gate_up(0, 0)
            load_down(0, 0)
            rows_of = lambda x: x.rearrange("(i p) n -> p i n", p=P)
            sp.wait_ge(s["av_ps"], NT)
            sp.dma_start(resid, rows_of(a["x_rows"])).then_inc(s["in_resid"], 16)
            sp.dma_start(w_r, a["w_router"].rearrange("(p k) n -> p k n", k=KD)).then_inc(s["in_rows"], 16)
            sp.dma_start(g_ffn[:], a["g_norm_ffn"].to_broadcast((P, D))).then_inc(s["in_rows"], 16)
            sp.dma_start(g_fin[:], a["g_final"].to_broadcast((P, D))).then_inc(s["in_rows"], 16)
            sp.wait_ge(s["glu_ps"], GB)
            sp.dma_start(slot[1][:, 8192:10240].rearrange("p (k n) -> p k n", k=2), down_v[1, :, 0:2])\
                .then_inc(down_in[1], 16)
            sp.wait_ge(s["op_ps"], NT)
            sp.dma_start(gate_w[1], gate_v[1]).then_inc(gate_in[1], 16)
            for i in range(NT - 1):
                sp.wait_ge(s["op_out"], NT + i + 1)
                sp.dma_start(rows_of(resid_scr)[:, i], resid[:, i, :]).then_inc(s["resid_kept"], 16)

            sp.wait_ge(s["op_ps"], 2 * NT)
            sp.dma_start(up_w[1], up_v[1]).then_inc(up_in[1], 16)
            sp.dma_start(gate_w[2], gate_v[2]).then_inc(gate_in[2], 16)
            sp.wait_ge(s["op_out"], 2 * NT)
            sp.dma_start(rows_of(resid_scr)[:, NT - 1], resid[:, NT - 1, :]).then_inc(s["resid_kept"], 16)
            sp.wait_ge(s["parts_done"], NT)
            sp.dma_start(slot[1][:, 10240:12288].rearrange("p (k n) -> p k n", k=2), down_v[1, :, 2:4])\
                .then_inc(down_in[1], 16)
            sp.wait_ge(s["ffn_sq"], NT)
            sp.wait_ge(s["ffn_done"], NT)
            sp.wait_ge(s["resid_kept"], 16 * NT)
            sp.dma_start(up_w[2], up_v[2]).then_inc(up_in[2], 16)
            for k in range(KH - 1):
                sp.dma_start(down_w[2][k], down_v[2, :, k]).then_inc(down_in[2], 16)
            sp.wait_ge(s["pairs_used"], 1)
            sp.dma_start(down_w[2][KH - 1], down_v[2, :, KH - 1]).then_inc(down_in[2], 16)

            def load_expert(q, e):
                done = sp.value_load(first_i[0:1, bass.ds(e - 2, 1)], min_val=1, max_val=TILES_MAX)
                sp.wait_ge(s["gu_ready"], done)
                load_gate_up(q, e)
                sp.wait_ge(s["y_ready"], done)
                load_down(q, e)

            with sp.Fori(1, NE // 3) as it:
                for q in range(3):
                    load_expert(q, it * 3 + q)
            for e in range(NE - NE % 3, NE):
                load_expert(e % 3, e)
            done = sp.value_load(first_i[0:1, NE - NE % 3:NE - NE % 3 + 1], min_val=1, max_val=TILES_MAX)
            sp.wait_ge(s["y_ready"], done)
            sp.dma_start(resid, rows_of(resid_scr)).then_inc(s["resid_back"], 16)

            for i in range(NT):
                sp.wait_ge(s["fin_done"], i + 1)
                sp.dma_start(o["y"][P * i:P * i + P, :], fin[i]).then_inc(s["fin_out"], 16)
            sp.wait_ge(s["fin_out"], 16 * NT)
            sp.wait_ge(s["states_out"], 32)
            sp.wait_ge(s["cache_out"], 16 * 2 * (NB + 2))

        @block.gpsimd
        def _(pool):
            steps = [0]

            def step(ins):
                steps[0] += 1
                ins.then_inc(s["pool_step"], 1)
                pool.wait_ge(s["pool_step"], steps[0])

            pool.memset(probs_t[:], 0.0).then_inc(s["zero_ready"], 1)
            pool.memset(conv_w, 0.0).then_inc(s["conv_zero"], 1)
            step(pool.memset(ident[:], 0.0))
            step(pool.affine_select(out=ident[:], in_=ident[:], compare_op=ALU.not_equal, fill=1.0, base=0,
                                    pattern=[[-1, P]], channel_multiplier=1))
            step(pool.memset(ones[:], 1.0))
            step(pool.affine_select(out=before[:], in_=ones[:], compare_op=ALU.is_gt, fill=0.0, base=0,
                                    pattern=[[1, P]], channel_multiplier=-1))
            step(pool.memset(tile_tt[:], float(TT)))
            step(pool.memset(zero_nt[:], 0.0))
            step(pool.memset(mask, 0.0))
            step(pool.memset(mask[0:HD, 192:256], MASKED))
            step(pool.memset(mask[HD:P, 0:HD], MASKED))
            step(pool.iota(iota_e[:], [[1, NE]], base=0, channel_multiplier=0, allow_small_or_imprecise_dtypes=True))
            step(pool.iota(iota_t[:], [[1, TT]], base=0, channel_multiplier=0,
                           allow_small_or_imprecise_dtypes=True))
            pool.memset(pad8[:], -3.0e38).then_inc(s["const_done"], 1)

            pool.wait_ge(s["bbar_done"], 1)
            t1 = sums_f[:, 0:448].rearrange("p (r s c) -> p r s c", r=4, s=7)
            t2 = sums_f[:, 512:960].rearrange("p (r s c) -> p r s c", r=4, s=7)

            def step_table(q):
                rr = slice(4 * q, 4 * q + 4)
                pr, pi = [pw[:, i, 1:T, rr].rearrange("p s r -> p r s").unsqueeze(3).to_broadcast([P, 4, T - 1, GC])
                          for i in range(2)]
                br, bi = [bbar[:, i, rr, :].unsqueeze(2).to_broadcast([P, 4, T - 1, GC]) for i in range(2)]
                if q >= 1:
                    pool.wait_ge(s["bp_tr"], 2 * q)
                for i in range(2):
                    pool.tensor_copy(bp[:, :, i, T - 1, :], bbar[:, i, rr, :])
                pool.tensor_tensor(t1, br, pr, ALU.mult)
                step(pool.tensor_tensor(t2, bi, pi, ALU.mult))
                step(pool.tensor_tensor(bp[:, :, 0, 0:T - 1, :], t1, t2, ALU.subtract))
                pool.tensor_tensor(t1, br, pi, ALU.mult)
                step(pool.tensor_tensor(t2, bi, pr, ALU.mult))
                pool.tensor_tensor(bp[:, :, 1, 0:T - 1, :], t1, t2, ALU.add).then_inc(s["bp_ready"], 1)

            re, im = rot
            step(pool.memset(re[:, :, 0:1], 1.0))
            step(pool.memset(im[:, :, 0:1], 0.0))
            powers = [(prep[:, 18, :], prep[:, 19, :])] + [(prep[:, 20 + 2 * i, :], prep[:, 21 + 2 * i, :])
                                                           for i in (0, 1)] * 3

            def double(b):
                n, cur, nxt = 2 ** b, powers[b], powers[b + 1]
                cr, ci = [c.unsqueeze(2).to_broadcast([P, R, n]) for c in cur]
                m1 = probs[:, 0, 0:R * n].rearrange("p (r n) -> p r n", n=n)
                m2 = probs[:, 0, 512:512 + R * n].rearrange("p (r n) -> p r n", n=n)
                pool.tensor_tensor(m1, re[:, :, 0:n], cr, ALU.mult)
                step(pool.tensor_tensor(m2, im[:, :, 0:n], ci, ALU.mult))
                step(pool.tensor_tensor(re[:, :, n:2 * n], m1, m2, ALU.subtract))
                pool.tensor_tensor(m1, re[:, :, 0:n], ci, ALU.mult)
                step(pool.tensor_tensor(m2, im[:, :, 0:n], cr, ALU.mult))
                step(pool.tensor_tensor(im[:, :, n:2 * n], m1, m2, ALU.add))
                q1, q2 = prep[:, 24, :], prep[:, 25, :]
                pool.tensor_tensor(q1, cur[0], cur[0], ALU.mult)
                step(pool.tensor_tensor(q2, cur[1], cur[1], ALU.mult))
                step(pool.tensor_tensor(nxt[0], q1, q2, ALU.subtract))
                step(pool.tensor_tensor(q1, cur[0], cur[1], ALU.mult))
                step(pool.tensor_tensor(nxt[1], q1, q1, ALU.add))

            for q, doublings in enumerate(((0,), (1, 2), (3,), (4, 5))):
                step_table(q)
                for b in doublings:
                    double(b)
            pool.sem_inc(s["rot_ready"], 1)

            pool.wait_ge(s["sum_out"], 8)
            ar, ai = [pw[:, i, 0, :].unsqueeze(2).to_broadcast([P, R, NB]) for i in range(2)]
            dec = states[:, :, :, NCP:NC].rearrange("p r i (b j) -> p r i b j", j=2)
            new = sums[:, :, :, NCP:NC].rearrange("p i r (b j) -> p i r b j", j=2)
            d0, d1 = dec_tmp[:, 0], dec_tmp[:, 1]
            for i in range(2):
                step(pool.tensor_copy(dec[:, :, i, :, 0], h0[:, i]))
            for j in range(2):
                hr, hi = (h0[:, 0], h0[:, 1]) if j == 0 else (dec_tmp[:, 2], dec_tmp[:, 3])
                tr, ti = (dec_tmp[:, 2], dec_tmp[:, 3]) if j == 0 else (h_dec[:, 0], h_dec[:, 1])
                for x, y, op, dst, i in ((ar, ai, ALU.subtract, tr, 0), (ai, ar, ALU.add, ti, 1)):
                    step(pool.tensor_tensor(d0, hr, x, ALU.mult))
                    step(pool.tensor_tensor(d1, hi, y, ALU.mult))
                    step(pool.tensor_tensor(d0, d0, d1, op))
                    step(pool.tensor_tensor(dst, d0, new[:, i, :, :, j], ALU.add))
                if j == 0:
                    for i in range(2):
                        step(pool.tensor_copy(dec[:, :, i, :, 1], dec_tmp[:, 2 + i]))
            pool.sem_inc(s["states_done"], 2)

            pool.wait_ge(s["kern_out"], 8)
            pool.wait_ge(s["in_small"], 48)
            step(pool.tensor_tensor(skip_tmp, skip[:].unsqueeze(2).to_broadcast([GC, G, GC]),
                                    ident[0:GC, 0:GC].unsqueeze(1).to_broadcast([GC, G, GC]), ALU.mult))
            pool.tensor_tensor(kern[0:GC, :, 0:GC], kern[0:GC, :, 0:GC], skip_tmp, ALU.add)\
                .then_inc(s["kern_done"], 1)

            pool.memset(bp_buf[:], 0.0).then_inc(s["attn_z"], 1)

            for n in range(1, GB):
                pool.wait_ge(s["mixsq_done"], n + 1)
                ins = pool.tensor_tensor(mix_sq[:, 0, :], mix_sq[:, 0, :], mix_sq[:, n, :], ALU.add)
                if n < GB - 1:
                    step(ins)
            ins.then_inc(s["mixsum_done"], 1)

            for i in range(NT):
                x = ffn_in[i % 2]
                pool.wait_ge(s["high_done"], i + 1)
                pool.wait_ge(s["xf_tr"], i + 1)
                pool.tensor_tensor(x, x, parts[0][i], ALU.subtract).then_inc(s["rest_done"], 1)
                pool.wait_ge(s["mid_done"], i + 1)
                pool.tensor_tensor(parts[2][i], x, parts[1][i], ALU.subtract).then_inc(s["parts_done"], 1)

            pool.sem_inc(s["sel_ready"], 1)
            pool.wait_ge(s["pos_done"], 1)
            pool.sem_inc(s["base_step"], 1)
            with pool.Fori(0, NE) as e:
                first, end = tiles_of(pool, e)
                pool.wait_ge(s["base_step"], e + first + 1)
                pool.tensor_copy(place_b, place_e[:, bass.ds(e, 1), :].rearrange("p e i -> p (e i)"))\
                    .then_inc(s["base_step"], 1)
                with pool.Fori(first, end) as w:
                    pool.wait_ge(s["base_step"], e + w + 2)
                    pool.wait_ge(s["sel_ready"], w + 1)
                    pool.tensor_tensor(place_c, place_b, zero_nt[:], ALU.add).then_inc(s["place_ready"], 1)
                    pool.wait_ge(s["place_ready"], w + 1)
                    pool.tensor_tensor(place_b, place_b, tile_tt[:], ALU.subtract).then_inc(s["base_step"], 1)
            pool.sem_inc(s["place_ready"], 1)

            pool.wait_ge(s["rows_done"], 1)
            for i in range(NT):
                for k in range(2):
                    pool.indirect_dma_start(got[i][k], None, y_slots,
                                            bass.IndirectOffsetOnAxis(pos_u[:, k, i:i + 1], 0))\
                        .then_inc(got_in[i], 16)

        @block.tensor
        def _(pe):
            pe.wait_ge(s["const_done"], 1)
            for h in range(4):
                pe.wait_ge(s["sq_done"], h + 1)
                for k in range(2 * h, 2 * h + 2):
                    pe.matmul(pp[2][:, 0, :], ones[:], x_sq[:, k, 0:SEQ], start=k == 0, stop=k == KD - 1)
                    ins = pe.matmul(pp[2][:, 1, 0:P], ones[:], x_sq[:, k, SEQ:TOK], start=k == 0, stop=k == KD - 1)
            ins.then_inc(s["rstd_ps"], 1)

            columns = [w_u[:, :, P * b:P * b + P] for b in range(GB)] + [w_qkv[:, :, W:W + P]]
            columns += [w_qkv[:, :, P * h:P * h + P] for h in range(QPK)] + [w_qkv[:, :, W + P:W + 2 * P]]

            def project(n):
                t = pp[n % 2]
                if n >= 2:
                    pe.wait_ge(s["proj_out"], n - 1)
                if n == GB:
                    pe.wait_ge(s["in_w_qkv"], 16)
                for k in range(KD):
                    if n == 0 and k % 2 == 0:
                        pe.wait_ge(s["xg_done"], k // 2 + 1)
                    pe.matmul(t[:, 0, :], columns[n][:, k, :], x_t[:, k, 0:SEQ], start=k == 0, stop=k == KD - 1)
                    ins = pe.matmul(t[:, 1, 0:P], columns[n][:, k, :], x_t[:, k, SEQ:TOK],
                                    start=k == 0, stop=k == KD - 1)
                ins.then_inc(s["proj_ps"], 1)

            def turn_bp(q):
                pe.wait_ge(s["bp_ready"], q + 1)
                for side in range(2):
                    h = 2 * q + side
                    if h >= 2:
                        pe.wait_ge(s["bp_out"], h - 1)
                    for j in range(2):
                        for i in range(2):
                            c = 256 * j + P * i
                            ins = pe.transpose(pp[2][:, side, c:c + P],
                                               bp[:, 2 * side + j, i].rearrange("p s c -> p (s c)"), ident[:])
                    ins.then_inc(s["bp_tr"], 1)

            def chunk_sums(h):
                q, i = h // 2, h % 2
                if h >= 2:
                    pe.wait_ge(s["sum_out"], h - 1)
                for j in range(4):
                    r = 4 * q + j
                    for m in range(2):
                        ins = pe.matmul(pp[2][HD * m:HD * m + HD, i, NC * j:NC * j + NC],
                                        sum_w[:, r, i, HD * m:HD * m + HD], u_c[:, 2 * r + m, :],
                                        start=True, stop=True)
                ins.then_inc(s["sum_ps"], 1)

            def kernels(h):
                q, m = h // 2, h % 2
                if h >= 2:
                    pe.wait_ge(s["kern_out"], h - 1)
                rows = slice(HD * m, HD * m + HD)
                for j in range(4):
                    r = 4 * q + j
                    for i in range(2):
                        pe.matmul(pp[2][0:GC, m, P * j:P * j + GC], bbar[rows, i, r, :], ssm_c[rows, i, r, :],
                                  start=i == 0, stop=i == 1)
                    for i in range(2):
                        ins = pe.matmul(pp[2][0:GC, m, P * j + GC:P * j + P], bbar[rows, i, r, :],
                                        out_tab[rows, r, i, 0:T - 1, :], start=i == 0, stop=i == 1)
                ins.then_inc(s["kern_ps"], 1)

            def ssm_out(h):
                q, m = h // 2, h % 2
                if h >= 2:
                    pe.wait_ge(s["y_out_done"], h - 1)
                rows = slice(HD * m, HD * m + HD)
                for j in range(4):
                    r = 4 * q + j
                    t = pp[2][:, m, NC * j:NC * j + NC]
                    pe.matmul(t, conv_w[:, 2 * r + m, :], u_c[:, 2 * r + m, :], start=True, stop=False)
                    for i in range(2):
                        ins = pe.matmul(t, out_tab[rows, r, i].rearrange("p t c -> p (t c)"), states[rows, r, i, :],
                                        start=False, stop=i == 1)
                ins.then_inc(s["y_ps"], 1)

            pe.wait_ge(s["in_w_u"], 16)
            for n in range(10):
                project(n)
                if GB < n < 9:
                    turn_bp(n - GB - 1)
            pe.wait_ge(s["proj_out"], 10)
            for n, (x, i) in enumerate([(v_t, i) for i in range(NT)] + [(k_t, NT - 2), (k_t, NT - 1)]):
                ins = pe.transpose(pp[3][:, n // 4, P * (n % 4):P * (n % 4) + P], x[:, P * i:P * i + P], ident[:])
            ins.then_inc(s["kv_ps"], 1)
            pe.wait_ge(s["bp_out"], 8)
            pe.wait_ge(s["u_in"], 16 * T)
            for h in range(8):
                chunk_sums(h)
            pe.wait_ge(s["out_tab_done"], 1)
            pe.wait_ge(s["sum_out"], 8)

            def scores(n):
                m, v = n // 2, n % 2
                rows = slice(HD * v, HD * v + HD)
                sc = pp[0][:].rearrange("p b (h n) -> p (b h) n", h=2)
                if n >= 1:
                    pe.wait_ge(s["sc_read"], n)
                else:
                    pe.wait_ge(s["proj_out"], 9)
                lo = 0 if m else P
                for h in range(QPK):
                    ins = pe.matmul(sc[:, h, lo:256], q_t[rows, h, P * m:P * m + P],
                                    k_t[rows, P * (m - 1) + lo:P * (m + 1)], start=True, stop=True)
                ins.then_inc(s["sc_ps"], 1)

            def turn_probs(n):
                m = n // 2
                pe.wait_ge(s["norm_done"], n + 1)
                if n >= 1:
                    pe.wait_ge(s["pt_out"], n)
                pr = soft[n % 3].rearrange("p (h n) -> p h n", h=QPK)
                for kt in range(0 if m else 1, 2):
                    for h in range(QPK):
                        ins = pe.transpose(pp[1][:, kt, P * h:P * h + P], pr[:, h, P * kt:P * kt + P], ident[:])
                ins.then_inc(s["pt_ps"], 1)

            def weighted(m):
                pe.wait_ge(s["pt_out"], 2 * m + 2)
                if m >= 1:
                    pe.wait_ge(s["attn_done"], m)
                first = 0 if m else 1
                for kt in range(first, 2):
                    for v in range(NKV):
                        ins = pe.matmul(pp[3][HD * v:HD * v + HD, 0, :],
                                        kv_row[:, m - 1 + kt, P + HD * v:P + HD * v + HD],
                                        turned[v][:, 512 * kt:512 * kt + 512], start=kt == first, stop=kt == 1)
                ins.then_inc(s["av_ps"], 1)

            def squares(m):
                pe.wait_ge(s["av_sq"], m + 1)
                for h in range(QPK):
                    ins = pe.matmul(pp[3][:, 1, m:m + 1], rstd_row[:, P * h:P * h + P], ones[:, 0:1],
                                    start=h == 0, stop=h == QPK - 1)
                ins.then_inc(s["ssq_ps"], 1)

            for h in range(8):
                kernels(h)
            scores(0)
            scores(1)
            pe.wait_ge(s["kv_out"], 3)
            for n in range(8):
                if n + 2 < 8:
                    scores(n + 2)
                turn_probs(n)
                if n % 2 == 0 and n >= 2:
                    squares(n // 2 - 1)
                for h in BESIDE[n]:
                    if h == 0:
                        pe.wait_ge(s["conv_in"], 16 * T)
                        pe.wait_ge(s["kern_out"], 8)
                        pe.wait_ge(s["states_done"], 3)
                    ssm_out(h)
                if n % 2:
                    weighted(n // 2)
            squares(3)

            def out_project(t, n):
                i, m = t % NT, t // NT
                left = (attn_t, mix_t)[m]
                if n == 0 and t >= 2:
                    earlier = [u + 1 for u in range(t) if OP_PAIR[u] == OP_PAIR[t]]
                    if earlier:
                        pe.wait_ge(s["op_out"], earlier[-1])
                for k in range(GB):
                    ins = pe.matmul(pp[OP_PAIR[t]][:, n, :], left[:, k, P * i:P * i + P],
                                    w_out[:, 4 * m + k, 512 * n:512 * n + 512], start=k == 0, stop=k == GB - 1)
                if n == 1:
                    ins.then_inc(s["op_ps"], 1)

            pe.wait_ge(s["streams_ready"], 1)
            pe.wait_ge(s["in_attn"], 32)
            pe.wait_ge(s["sc_read"], 8)
            for j in range(3):
                bs = range(3 * j, min(3 * j + 3, NB))
                if j == 2:
                    pe.wait_ge(s["y_out_done"], 8)
                    pe.wait_ge(s["out_w"], 32)
                    out_project(0, 0)
                    pe.wait_ge(s["exp_done"], 9)
                for b in bs:
                    ins = pe.matmul(pp[0][:, j % 2, NK * (b - 3 * j):NK * (b - 3 * j) + NK],
                                    q_z[:, b].rearrange("p v h t -> p (v h t)"), kd_t[:, b, :], start=True, stop=True)
                ins.then_inc(s["sc_ps"], 1)
            for j in range(3):
                bs = range(3 * j, min(3 * j + 3, NB))
                n = 8 + j
                pe.wait_ge(s["norm_done"], n + 1)
                pe.wait_ge(s["pt_out"], n)
                pr = soft[(8 + j) % 3][:, 0:3 * NK].rearrange("p (b n) -> p b n", b=3)
                for b in bs:
                    c = P * (b - 3 * j)
                    pe.transpose(pp[1][:, 0, c:c + P], pr[:, b - 3 * j, 0:WIN], ident[:])
                    ins = pe.transpose(pp[1][0:LS, 1, c:c + P], pr[:, b - 3 * j, WIN:NK], ident[:])
                ins.then_inc(s["pt_ps"], 1)
                if j == 1:
                    out_project(0, 1)
                pe.wait_ge(s["pt_out"], n + 1)
                if j == 0:
                    pe.wait_ge(s["attn_done"], NT - 1)
                    pe.wait_ge(s["vnew_in"], 16 * NB)
                for b in bs:
                    for v in range(NKV):
                        c = P * (b - 3 * j) + HD * v
                        t = pp[3][HD * v:HD * v + HD, 0, HD * b:HD * b + HD]
                        pe.matmul(t, v_old[:, b, HD * v:HD * v + HD], probs_t[:, c:c + HD], start=True, stop=False)
                        ins = pe.matmul(t, v_new[:, b, HD * v:HD * v + HD], probs_t[0:LS, 512 + c:512 + c + HD],
                                        start=False, stop=True)
            ins.then_inc(s["av_ps"], 1)

            pe.wait_ge(s["gelu_done"], 1)
            pe.wait_ge(s["exp_done"], 11)
            pe.wait_ge(s["pt_out"], 11)
            for n in range(GB):
                if n == 1:
                    squares(NT - 1)
                if n >= 2:
                    pe.wait_ge(s["sig_done"], n - 1)
                for k in range(GB):
                    pe.matmul(pp[n % 2][:, 0, :], w_glu[:, k, P * n:P * n + P], y_g[:, k, 0:512],
                              start=k == 0, stop=k == GB - 1)
                    ins = pe.matmul(pp[n % 2][:, 1, 0:P], w_glu[:, k, P * n:P * n + P], y_g[:, k, 512:TOK],
                                    start=k == 0, stop=k == GB - 1)
                ins.then_inc(s["glu_ps"], 1)

            def router_turn(i):
                pe.wait_ge(s["ffn_done"], i + 1)
                if i >= 1:
                    pe.wait_ge(s["xf_out"], i)
                for k in range(KD):
                    ins = pe.transpose(pp[0][:, k // 4, P * (k % 4):P * (k % 4) + P], ffn_in[i % 2][:, k:D:KD],
                                       ident[:])
                ins.then_inc(s["xf_tr"], 1)

            def router(i):
                pe.wait_ge(s["xf_out"], i + 1)
                xf = probs[:, i % 2].rearrange("p (k t) -> p k t", k=KD)
                for k in range(KD):
                    ins = pe.matmul(pp[3][:, 0, NR * i:NR * i + NR], xf[:, k, :], w_r[:, k, :],
                                    start=k == 0, stop=k == KD - 1)
                ins.then_inc(s["lg_ps"], 1)

            for t in range(1, 2 * NT):
                i = t - NT
                if t == 1:
                    pe.wait_ge(s["sig_done"], GB - 1)
                if i == 0:
                    pe.wait_ge(s["weighed"], GB)
                out_project(t, 0)
                if i >= 2:
                    router(i - 2)
                out_project(t, 1)
                if t == 1:
                    pe.wait_ge(s["mixsum_done"], 1)
                    for j in range(NT):
                        ins = pe.matmul(pp[3][:, 1, NT + j:NT + j + 1], mix_sq[:, 0, P * j:P * j + P],
                                        ones[:, 0:1], start=True, stop=True)
                    ins.then_inc(s["ssq_ps"], 1)
                if i >= 1:
                    router_turn(i - 1)
            router(NT - 2)
            router_turn(NT - 1)
            router(NT - 1)

            pe.wait_ge(s["pair_done"], 1)
            n = NT * NE
            pe.matmul(pp[3][:, 1, 0:n], before[:], both.rearrange("p i e -> p (i e)"), start=True, stop=False)
            pe.matmul(pp[3][:, 1, 0:n], ones[:], tiles_before[:, 0:NT].rearrange("p i e -> p (i e)"),
                      start=False, stop=True)
            pe.matmul(pp[3][:, 1, n:n + NE], ones[:], tiles_before[:, NT], start=True, stop=True)\
                .then_inc(s["place_ps"], 1)

            gu, yp, gx, xtp, htp = pp[0][:, 0, :], pp[0][:, 1, :], pp[2][:, 0, :], pp[2][:, 1, :], pp[1][:, 0, 0:256]

            def pick(w=None):
                for i in range(NT):
                    if w is not None and i == 3:
                        pe.wait_ge(s["h_ready"], w + 1)
                    for n, part in enumerate(parts):
                        for h in range(2):
                            ins = pe.matmul(gx[HD * h:HD * h + HD], sel[:, i, :], part[i][:, 512 * h:512 * h + 512],
                                            start=i == 0 and n == 0, stop=i == NT - 1 and n == 2)
                        if w is not None and (i, n) == (3, 0):
                            for k in range(KH):
                                ins = pe.transpose(htp[:, TT * k:TT * k + TT], hid[:, k:DE:KH], ident[0:TT, 0:TT])
                            ins.then_inc(s["ht_ready"], 1)
                ins.then_inc(s["gx_ready"], 1)

            def turn():
                for c in range(4):
                    ins = pe.transpose(xtp[:, P * c:P * c + P], xrow[:, c:512:4], ident[:])
                ins.then_inc(s["xt_ready"], 1)

            pe.wait_ge(s["parts_done"], NT)
            pe.wait_ge(s["sel_ready"], 2)
            pick()
            pe.wait_ge(s["gx_copied"], 1)
            turn()
            pe.wait_ge(s["pos_done"], 1)

            def expert(q, e, loads):
                first, end = tiles_of(pe, e)
                with pe.Fori(first, end) as w:
                    pe.wait_ge(s["xt_copied"], w + 1)
                    pe.wait_ge(gate_in[q], loads * 16)
                    pe.wait_ge(up_in[q], loads * 16)
                    for n in range(KD):
                        h, c = n // 4, n % 4
                        lhs = xt_e[:, c, TT * h:TT * h + TT]
                        pe.matmul(gu[0:TT], lhs, gate_w[q][:, h, c, :], start=n == 0, stop=n == KD - 1)
                        ins = pe.matmul(gu[TT:P], lhs, up_w[q][:, h, c, :], start=n == 0, stop=n == KD - 1)
                    ins.then_inc(s["gu_ready"], 1)
                    pe.wait_ge(s["sel_ready"], w + 3)
                    pick(w)
                    pe.wait_ge(s["ht_copied"], w + 1)
                    pe.wait_ge(down_in[q], loads * (32 if q < 2 else 16 * KH))
                    pe.wait_ge(s["y_copied"], w + 1)
                    for k in range(KH):
                        if k == 1:
                            pe.wait_ge(s["gx_copied"], w + 2)
                            turn()
                        for h in range(2):
                            ins = pe.matmul(yp[TT * h:TT * h + TT], hid_t[:, k, :],
                                            down_w[q][k][:, 512 * h:512 * h + 512],
                                            start=k == 0, stop=k == KH - 1)
                    ins.then_inc(s["y_ready"], 1)

            with pe.Fori(0, NE // 3) as it:
                for q in range(3):
                    expert(q, it * 3 + q, it + 1)
            for e in range(NE - NE % 3, NE):
                expert(e % 3, e, NE // 3 + 1)

        @block.scalar
        def _(act):
            act.dma_start(cols[:], a["cols"]).then_inc(s["in_cols"], 16)
            act.dma_start(tables[:], a["tables"]).then_inc(s["in_tables"], 16)
            for m in range(2):
                act.dma_start(prep[HD * m:HD * m + HD, 2, :], a["log_dt"][m:m + 1, :].to_broadcast((HD, R)))\
                    .then_inc(s["in_tables"], 16)
            act.dma_start(sink_row[:], a["sinks"].to_broadcast((P, 8))).then_inc(s["in_small"], 16)
            act.dma_start(skip[:], a["ssm_d"]).then_inc(s["in_small"], 16)
            act.dma_start(b_r[:], a["b_router"].to_broadcast((P, NR))).then_inc(s["in_small"], 16)
            for h in range(4):
                act.wait_ge(s[f"in_x{h}"], 16)
                kk = slice(2 * h, 2 * h + 2)
                act.activation(x_sq[:, kk, :], x_t[:, kk, :], ACT.Square).then_inc(s["sq_done"], 1)
            act.wait_ge(s["in_tables"], 48)
            act.activation(prep[:, 3, :], prep[:, 2, :], ACT.Exp).then_inc(s["prep_act"], 1)
            act.wait_ge(s["prep_dve"], 1)
            act.activation(prep[:, 6, :], prep[:, 4, :], ACT.Exp).then_inc(s["prep_act"], 1)
            act.wait_ge(s["rstd_act"], 1)
            act.activation(rstd_row[:], rstd_row[:], ACT.Sqrt).then_inc(s["rstd_act"], 1)
            act.wait_ge(s["prep_dve"], 2)
            act.activation(prep[:, 9, :], prep[:, 8, :], ACT.Sin)
            act.activation(prep[:, 10, :], prep[:, 8, :], ACT.Sin, scale=0.5).then_inc(s["prep_act"], 1)

            act.wait_ge(s["u_stored"], 16 * GB)
            for h in range(8):
                act.wait_ge(s["bp_tr"], h + 1)
                act.copy(sum_w[:, 2 * h:2 * h + 2], pp[2][:, h % 2, :].rearrange("p (r i m) -> p r i m", r=2, i=2))\
                    .then_inc(s["bp_out"], 1)
            for h in range(8):
                q, i = h // 2, h % 2
                act.wait_ge(s["sum_ps"], h + 1)
                act.copy(sums[:, i, 4 * q:4 * q + 4, :],
                         pp[2][:, i, 0:4 * NC].rearrange("p (r n) -> p r n", r=4)).then_inc(s["sum_out"], 1)
            kv = kern[0:GC].rearrange("p (r m) n -> p r m n", m=2)
            for h in range(8):
                q, m = h // 2, h % 2
                act.wait_ge(s["kern_ps"], h + 1)
                act.copy(kv[:, 4 * q:4 * q + 4, m, :],
                         pp[2][0:GC, m, :].rearrange("p (r n) -> p r n", r=4)).then_inc(s["kern_out"], 1)
            uv = u_c.rearrange("p (r m) n -> p r m n", m=2)

            def ssm_copy(h):
                q, m = h // 2, h % 2
                act.wait_ge(s["y_ps"], h + 1)
                act.copy(uv[:, 4 * q:4 * q + 4, m, :],
                         pp[2][:, m, 0:4 * NC].rearrange("p (r n) -> p r n", r=4)).then_inc(s["y_out_done"], 1)

            def exps(n, rows, src):
                act.wait_ge(s["neg_done"], n + 1)
                act.activation(sm[:, n % 3, 4, 0:rows], sm[:, n % 3, 4, 0:rows], ACT.Exp)
                for h in range(rows):
                    dst, x = src(h)
                    ins = act.activation(dst, x, ACT.Exp, bias=sm[:, n % 3, 2, h:h + 1], scale=SCALE,
                                         accum_out=sm[:, n % 3, 3, h:h + 1])
                ins.then_inc(s["exp_done"], 1)

            def pt_copy(n):
                act.wait_ge(s["pt_ps"], n + 1)
                if n < 2:
                    act.copy(turned[n % 2][:, 512:1024], pp[1][:, 1, :]).then_inc(s["pt_out"], 1)
                elif n < 8:
                    act.copy(turned[n % 2], pp[1][:].rearrange("p b n -> p (b n)")).then_inc(s["pt_out"], 1)
                else:
                    w = P * min(3, NB - 3 * (n - 8))
                    act.copy(probs_t[:, 0:w], pp[1][:, 0, 0:w])
                    act.copy(probs_t[0:LS, 512:512 + w], pp[1][0:LS, 1, 0:w]).then_inc(s["pt_out"], 1)

            def unit(n):
                lo = 0 if n >= 2 else P
                pr = soft[n % 3].rearrange("p (h n) -> p h n", h=QPK)
                return lambda h: (pr[:, h, lo:256], pr[:, h, lo:256])

            def stream(j):
                pr = soft[(8 + j) % 3][:, 0:3 * NK].rearrange("p (b n) -> p b n", b=3)
                sc = pp[0][:, j % 2, 0:3 * NK].rearrange("p (b n) -> p b n", b=3)
                return lambda b: (pr[:, b, :], sc[:, b, :])

            def square_out(m):
                act.wait_ge(s["av_ps"], m + 1)
                if m >= 1:
                    act.wait_ge(s["ssq_ps"], m)
                act.activation(rstd_row[:, 0:512], pp[3][:, 0, :], ACT.Square).then_inc(s["av_sq"], 1)

            act.wait_ge(s["zeroed"], 16)
            exps(0, QPK, unit(0))
            exps(1, QPK, unit(1))
            for n in range(8):
                pt_copy(n)
                for h in BESIDE[n]:
                    ssm_copy(h)
                if n + 2 < 8:
                    exps(n + 2, QPK, unit(n + 2))
                if n % 2:
                    square_out(n // 2)
            for j in range(3):
                exps(8 + j, min(3, NB - 3 * j), stream(j))
                if j == 1:
                    pt_copy(8)
            act.wait_ge(s["y_in"], 16)
            act.activation(y_g, y_t, ACT.Gelu_apprx_tanh).then_inc(s["gelu_done"], 1)
            pt_copy(9)
            pt_copy(10)
            act.wait_ge(s["av_ps"], NT)
            act.wait_ge(s["ssq_ps"], NT - 1)
            act.activation(rstd_row[:, 0:512].rearrange("p (h b t) -> p b h t", h=QPK, b=NB),
                           pp[3][:, 0, :].rearrange("p (b h t) -> p b h t", b=NB, h=QPK), ACT.Square)\
                .then_inc(s["av_sq"], 1)

            def rs_root(m):
                act.wait_ge(s["rs_done"], m + 1)
                act.activation(stat[:, 1 + m, :], stat[:, 1 + m, :], ACT.Sqrt).then_inc(s["rs_act"], 1)

            rs_root(0)

            def mix_square(n):
                act.wait_ge(s["mix_done"], n + 1)
                act.activation(mix_sq[:, n, :], mix_t[:, n, :], ACT.Square).then_inc(s["mixsq_done"], 1)

            for n in range(GB):
                act.wait_ge(s["glu_ps"], n + 1)
                act.activation(mix_sq[:, n, 0:512], pp[n % 2][:, 0, :], ACT.Sigmoid, bias=b_glu[:, n:n + 1])
                act.activation(mix_sq[:, n, 512:TOK], pp[n % 2][:, 1, 0:P], ACT.Sigmoid, bias=b_glu[:, n:n + 1])\
                    .then_inc(s["sig_done"], 1)
                if n >= 1:
                    mix_square(n - 1)
            mix_square(GB - 1)
            rs_root(1)

            def middle(i):
                act.wait_ge(s["rest_done"], i + 1)
                act.copy(parts[1][i], ffn_in[i % 2]).then_inc(s["mid_done"], 1)

            for i in range(NT):
                act.wait_ge(s["op_out"], NT + i + 1)
                act.activation(sums_f[:, 0:D], resid[:, i, :], ACT.Square, accum_out=stat[:, 3, i:i + 1])\
                    .then_inc(s["ffn_sq"], 1)
                act.wait_ge(s["ffn_ms"], i + 1)
                act.activation(stat[:, 4, i:i + 1], stat[:, 4, i:i + 1], ACT.Sqrt).then_inc(s["ffn_sqrt"], 1)
                act.wait_ge(s["ffn_done"], i + 1)
                act.copy(parts[0][i], ffn_in[i % 2]).then_inc(s["high_done"], 1)
                if i >= 1:
                    middle(i - 1)
                act.wait_ge(s["xf_tr"], i + 1)
                if i >= 2:
                    act.wait_ge(s["lg_ps"], i - 1)
                act.copy(probs[:, i % 2], pp[0][:].rearrange("p b n -> p (b n)")).then_inc(s["xf_out"], 1)
            middle(NT - 1)
            act.wait_ge(s["lg_out"], 2)
            act.activation(le_m[:, :, 0:NEG_G], le_m[:, :, 0:NEG_G], ACT.Exp).then_inc(s["route_act"], 1)
            act.wait_ge(s["lg_out"], 3)
            act.activation(rt[:, 4, :], rt[:, 4, :], ACT.Exp).then_inc(s["route_act"], 1)

            act.wait_ge(s["pos_done"], 1)
            act.wait_ge(s["zeroed"], 16)
            gu, yp, htp = pp[0][:, 0, :], pp[0][:, 1, :], pp[1][:, 0, 0:256]
            for q in range(2):
                act.sem_inc(y_kept[q], 32)
            act.sem_inc(s["y_copied"], 1)
            left = [act.alloc_register(f"left{q}") for q in range(2)]
            for q in range(2):
                act.reg_mov(left[q], 32)
            with act.Fori(0, NE // 2) as it:
                for q in range(2):
                    e = it * 2 + q
                    first, end = tiles_of(act, e)
                    with act.Fori(first, end) as w:
                        act.wait_ge(s["gu_ready"], w + 1)
                        act.activation(act_g, gu[0:TT], ACT.Silu).then_inc(s["sg_ready"], 1)
                        act.wait_ge(s["ht_ready"], w + 1)
                        act.copy(hid_t, htp.rearrange("p (k t) -> p k t", k=KH)).then_inc(s["ht_copied"], 1)
                        act.wait_ge(s["y_ready"], w + 1)
                        act.wait_ge(y_kept[q], left[q])
                        act.reg_add(left[q], left[q], 32)
                        act.copy(y_out[q], yp).then_inc(s["y_copied"], 1)
                        act.wait_ge(s["y_copied"], w + 2)
                        for h in range(2):
                            act.dma_start(y_slots[bass.ds(w * TT, TT), 512 * h:512 * h + 512],
                                          y_out[q][TT * h:TT * h + TT]).then_inc(y_kept[q], 16)
            for q in range(2):
                act.wait_ge(y_kept[q], left[q])
            act.sem_inc(s["rows_done"], 1)
            for i in range(NT):
                act.wait_ge(s["fin_sq"], i + 1)
                act.activation(fin[i], resid[:, i, :], ACT.Square, accum_out=stat[:, 5, i:i + 1])\
                    .then_inc(s["fin_ss"], 1)
                act.wait_ge(s["fin_ms"], i + 1)
                act.activation(stat[:, 6, i:i + 1], stat[:, 6, i:i + 1], ACT.Sqrt).then_inc(s["fin_sqrt"], 1)

        @block.vector
        def _(dve):
            steps = [0]

            def step(ins):
                steps[0] += 1
                ins.then_inc(s["dve_step"], 1)
                dve.wait_ge(s["dve_step"], steps[0])

            tt, ts, stt = dve.tensor_tensor, dve.tensor_scalar, dve.scalar_tensor_tensor
            pv = lambda i: prep[:, i, :]

            def cmul(out, x, y, tmp):
                step(tt(tmp[0], x[0], y[0], ALU.mult))
                step(tt(tmp[1], x[1], y[1], ALU.mult))
                step(tt(out[0], tmp[0], tmp[1], ALU.subtract))
                step(tt(tmp[0], x[0], y[1], ALU.mult))
                step(tt(tmp[1], x[1], y[0], ALU.mult))
                step(tt(out[1], tmp[0], tmp[1], ALU.add))

            def unit_length(x, t0, t1):
                step(tt(t0, x[0], x[0], ALU.mult))
                step(tt(t1, x[1], x[1], ALU.mult))
                step(tt(t0, t0, t1, ALU.add))
                step(ts(t0, t0, -0.5, 1.5, ALU.mult, ALU.add))
                for c in x:
                    step(tt(c, c, t0, ALU.mult))

            dve.wait_ge(s["in_cols"], 16)
            for h in range(4):
                dve.wait_ge(s["sq_done"], h + 1)
                for k in range(2 * h, 2 * h + 2):
                    ins = ts(x_t[:, k, :], x_t[:, k, :], g_mix[:, k:k + 1], None, ALU.mult)
                ins.then_inc(s["xg_done"], 1)
            dve.wait_ge(s["prep_act"], 1)
            step(tt(pv(4), a_re, pv(3), ALU.mult))
            tt(pv(5), a_im, pv(3), ALU.mult).then_inc(s["prep_dve"], 1)
            dve.wait_ge(s["prep_dve"], 1)
            dve.wait_ge(s["rstd_ps"], 1)
            ts(rstd_row[:, 0:SEQ], pp[2][:, 0, :], 1.0 / D, EPS, ALU.mult, ALU.add)
            ts(rstd_row[:, SEQ:TOK], pp[2][:, 1, 0:P], 1.0 / D, EPS, ALU.mult, ALU.add).then_inc(s["rstd_act"], 1)
            step(ts(pv(7), pv(5), 1.0 / (2 * np.pi), MAGIC, ALU.mult, ALU.add))
            step(ts(pv(7), pv(7), -MAGIC, None, ALU.add))
            step(stt(pv(8), pv(7), -TWO_PI[0], pv(5), ALU.mult, ALU.add))
            step(stt(pv(8), pv(7), -TWO_PI[1], pv(8), ALU.mult, ALU.add))
            step(stt(pv(8), pv(7), -TWO_PI[2], pv(8), ALU.mult, ALU.add))
            ts(pv(8), pv(8), 3.1415925, -3.1415925, ALU.min, ALU.max).then_inc(s["prep_dve"], 1)
            dve.wait_ge(s["rstd_act"], 2)
            dve.reciprocal(rstd_row[:], rstd_row[:]).then_inc(s["rstd_done"], 1)
            dve.wait_ge(s["rstd_done"], 1)

            def proj_out(n):
                dve.wait_ge(s["proj_ps"], n + 1)
                t = pp[n % 2]
                if n < GB:
                    out = u_stage[:, n].rearrange("p s n -> p n s")
                    tt(out[:, 0:NCP, :], t[:, 0, :].rearrange("p (n s) -> p n s", s=T),
                       rstd_row[:, 0:SEQ].rearrange("p (n s) -> p n s", s=T), ALU.mult)
                    tt(out[:, NCP:NC, :], t[:, 1, 0:P].rearrange("p (n s) -> p n s", s=T),
                       rstd_row[:, SEQ:TOK].rearrange("p (n s) -> p n s", s=T), ALU.mult).then_inc(s["u_out"], 1)
                    dve.wait_ge(s["u_out"], n + 1)
                else:
                    out = {GB: k_t[:], 9: v_t}[n] if n in (GB, 9) else q_t[:, n - GB - 1, :]
                    tt(out[:, 0:SEQ], t[:, 0, :], rstd_row[:, 0:SEQ], ALU.mult)
                    step(tt(out[:, SEQ:TOK], t[:, 1, 0:P], rstd_row[:, SEQ:TOK], ALU.mult))
                dve.sem_inc(s["proj_out"], 1)

            proj_out(0)
            dve.wait_ge(s["prep_act"], 3)
            step(tt(pv(10), pv(10), pv(10), ALU.mult))
            step(ts(pv(11), pv(10), -2.0, 1.0, ALU.mult, ALU.add))
            a1 = (pw[:, 0, T - 1, :], pw[:, 1, T - 1, :])
            step(tt(a1[0], pv(6), pv(11), ALU.mult))
            step(tt(a1[1], pv(6), pv(9), ALU.mult))
            step(tt(pv(12), a_re, a_re, ALU.mult))
            step(tt(pv(13), a_im, a_im, ALU.mult))
            step(tt(pv(12), pv(12), pv(13), ALU.add))
            step(dve.reciprocal(pv(13), pv(12)))
            step(ts(pv(14), a1[0], -1.0, None, ALU.add))
            step(tt(pv(15), pv(14), a_re, ALU.mult))
            step(tt(pv(16), a1[1], a_im, ALU.mult))
            step(tt(pv(15), pv(15), pv(16), ALU.add))
            step(tt(pv(16), a1[1], a_re, ALU.mult))
            step(tt(pv(17), pv(14), a_im, ALU.mult))
            step(tt(pv(16), pv(16), pv(17), ALU.subtract))
            step(tt(pv(15), pv(15), pv(13), ALU.mult))
            step(tt(pv(16), pv(16), pv(13), ALU.mult))
            proj_out(1)
            power = lambda n: (pw[:, 0, T - n, :], pw[:, 1, T - n, :])
            for n, (x, y) in {2: (1, 1), 3: (2, 1), 4: (2, 2), 5: (4, 1), 6: (4, 2), 7: (4, 3), 8: (4, 4)}.items():
                cmul(power(n), power(x), power(y), (pv(12), pv(14)))
                if n == 5:
                    proj_out(2)
            f = [pv(15 + i).unsqueeze(2).to_broadcast([P, R, GC]) for i in range(2)]
            c1 = probs[:, 1, 0:256].rearrange("p (r c) -> p r c", r=R)
            c2 = probs[:, 1, 256:512].rearrange("p (r c) -> p r c", r=R)
            cmul((bbar[:, 0], bbar[:, 1]), (ssm_b[:, 0], ssm_b[:, 1]), f, (c1, c2))
            step(dve.tensor_copy(pv(18), pv(11)))
            step(dve.tensor_copy(pv(19), pv(9)))
            unit_length((pv(18), pv(19)), pv(12), pv(14))
            for n in range(3):
                src, dst = ((pv(18), pv(19)), (pv(12), pv(14)))
                cmul(dst, src, src, (pv(13), pv(17)))
                step(dve.tensor_copy(pv(18), pv(12)))
                step(dve.tensor_copy(pv(19), pv(14)))
                step(tt(pv(6), pv(6), pv(6), ALU.mult))
            unit_length((pv(18), pv(19)), pv(12), pv(14))
            dve.sem_inc(s["bbar_done"], 1)
            proj_out(3)
            step(ts(ssm_c[:, 1], ssm_c[:, 1], -1.0, None, ALU.mult))
            cr, ci = ssm_c[:, 0], ssm_c[:, 1]
            for t in range(T):
                ar, ai = [x.unsqueeze(2).to_broadcast([P, R, GC]) for x in power(t + 1)]
                tt(c1, cr, ar, ALU.mult)
                step(tt(c2, ci, ai, ALU.mult))
                step(tt(out_tab[:, :, 0, t, :], c1, c2, ALU.add))
                tt(c1, ci, ar, ALU.mult)
                step(tt(c2, cr, ai, ALU.mult))
                step(tt(out_tab[:, :, 1, t, :], c1, c2, ALU.subtract))
                if t % 2 and 4 + t // 2 < 9:
                    proj_out(4 + t // 2)
            dve.sem_inc(s["out_tab_done"], 1)
            proj_out(8)
            proj_out(9)
            dve.wait_ge(s["kv_ps"], 1)
            in_rows = pp[3][:].rearrange("p b (j n) -> p (b j) n", j=4)
            dve.tensor_copy(kv_row[:, 0:4, P:256], in_rows[:, 0:4]).then_inc(s["kv_out"], 1)
            dve.tensor_copy(kv_row[:, 4, P:256], in_rows[:, 4]).then_inc(s["kv_out"], 1)
            dve.tensor_copy(kv_row[:, 3:5, 0:P], in_rows[:, 5:7]).then_inc(s["kv_out"], 1)
            step(dve.tensor_copy(decay, pv(6).unsqueeze(2).to_broadcast([P, R, NCP])))
            dve.memset(decay[:, :, 0:1], 0.0)

            dve.wait_ge(s["rot_ready"], 1)
            dve.wait_ge(s["sum_out"], 8)
            sr, si = sums[:, 0, :, 0:NCP], sums[:, 1, :, 0:NCP]
            wr, wi = rot
            t0, t1, t2 = rot_tmp
            tt(t0, sr, wr, ALU.mult)
            step(tt(t1, si, wi, ALU.mult))
            step(tt(roll[0], t0, t1, ALU.add))
            tt(t0, si, wr, ALU.mult)
            step(tt(t1, sr, wi, ALU.mult))
            step(tt(roll[1], t0, t1, ALU.subtract))
            fl = lambda x: x.rearrange("p r n -> p (r n)")
            for i in range(2):
                dve.tensor_tensor_scan(fl(rot_tmp[i]), fl(decay), fl(roll[i]), 0.0, ALU.mult, ALU.add)\
                    .then_inc(s["decay_used"], 1)
            step(dve.memset(states[:, :, :, 0:1], 0.0))
            tt(roll[0], t0, wr, ALU.mult)
            step(tt(roll[1], t1, wi, ALU.mult))
            tt(states[:, :, 0, 1:NCP], roll[0][:, :, 0:NCP - 1], roll[1][:, :, 0:NCP - 1], ALU.subtract)
            step(tt(h_last[:, 0], roll[0][:, :, NCP - 1], roll[1][:, :, NCP - 1], ALU.subtract))
            tt(roll[0], t0, wi, ALU.mult)
            step(tt(roll[1], t1, wr, ALU.mult))
            tt(h_last[:, 1], roll[0][:, :, NCP - 1], roll[1][:, :, NCP - 1], ALU.add)
            tt(states[:, :, 1, 1:NCP], roll[0][:, :, 0:NCP - 1], roll[1][:, :, 0:NCP - 1], ALU.add)\
                .then_inc(s["states_done"], 1)

            def before_exp(n, rows, src, sink):
                mx, m, neg, es = [sm[:, n % 3, i, 0:rows] for i in (0, 1, 2, 4)]
                step(dve.tensor_reduce(mx, src, AX.X, ALU.max))
                if sink is None:
                    step(ts(m, mx, SCALE, sink_d, ALU.mult, ALU.max))
                    step(ts(es, m, -1.0, sink_d, ALU.mult, ALU.add))
                else:
                    step(stt(m, mx, SCALE, sink, ALU.mult, ALU.max))
                    step(tt(es, sink, m, ALU.subtract))
                ts(neg, m, -1.0, None, ALU.mult).then_inc(s["neg_done"], 1)

            def after_exp(n, rows, view):
                dve.wait_ge(s["exp_done"], n + 1)
                total, es, rd = [sm[:, n % 3, i, 0:rows] for i in (3, 4, 5)]
                step(tt(total, total, es, ALU.add))
                step(dve.reciprocal(rd, total))
                for h in range(rows):
                    ins = ts(view(h), view(h), rd[:, h:h + 1], None, ALU.mult)
                ins.then_inc(s["norm_done"], 1)

            def masked(n):
                m, v = n // 2, n % 2
                lo = 0 if m else P
                pr = soft[n % 3].rearrange("p (h n) -> p h n", h=QPK)[:, :, lo:256]
                sc = pp[0][:].rearrange("p b (h n) -> p (b h) n", h=2)[:, :, lo:256]
                dve.wait_ge(s["sc_ps"], n + 1)
                if n >= 3:
                    dve.wait_ge(s["pt_ps"], n - 2)
                tt(pr, sc, mask[:, lo:256].unsqueeze(1).to_broadcast([P, QPK, 256 - lo]), ALU.add)\
                    .then_inc(s["sc_read"], 1)
                dve.wait_ge(s["sc_read"], n + 1)
                before_exp(n, QPK, pr, sink_row[:, QPK * v:QPK * v + QPK])

            def unit_out(n):
                lo = 0 if n >= 2 else P
                pr = soft[n % 3].rearrange("p (h n) -> p h n", h=QPK)
                after_exp(n, QPK, lambda h: pr[:, h, lo:256])

            def attn_out(m):
                dve.wait_ge(s["av_sq"], m + 1)
                src = pp[3][:, 0, :]
                if m < NT - 1:
                    dst = attn_t[:, :, P * m:P * m + P]
                    ins = tt(dst, src.rearrange("p (h t) -> p h t", h=QPK),
                       g_attn.unsqueeze(2).to_broadcast([P, QPK, P]), ALU.mult)
                else:
                    for h in range(QPK):
                        ins = ts(attn_t[:, h, SEQ:TOK].rearrange("p (b t) -> p b t", b=NB),
                           src.rearrange("p (b h t) -> p b h t", b=NB, h=QPK)[:, :, h, :],
                           g_attn[:, h:h + 1], None, ALU.mult)
                ins.then_inc(s["attn_done"], 1)

            dve.wait_ge(s["in_small"], 48)
            masked(0)
            masked(1)
            for n in range(8):
                unit_out(n)
                if n % 2 == 0 and n >= 2:
                    attn_out(n // 2 - 1)
                if n + 2 < 8:
                    masked(n + 2)
            dve.wait_ge(s["in_attn"], 32)
            dve.tensor_copy(kd_t[:, :, WIN:NK], k_t[:, SEQ:TOK].rearrange("p (b t) -> p b t", b=NB))
            dve.wait_ge(s["attn_z"], 1)
            for v in range(NKV):
                rows = slice(HD * v, HD * v + HD)
                ins = dve.tensor_copy(q_z[rows, :, v, :, :],
                                      q_t[rows, :, SEQ:TOK].rearrange("p h (b t) -> p b h t", b=NB))
            ins.then_inc(s["streams_ready"], 1)
            attn_out(3)
            for j in range(3):
                nb = min(3, NB - 3 * j)
                n = 8 + j
                dve.wait_ge(s["sc_ps"], n + 1)
                sc = pp[0][:, j % 2, 0:nb * NK].rearrange("p (b n) -> p b n", b=nb)
                dve.wait_ge(s["pt_ps"], n - 2)
                before_exp(n, nb, sc, None)
                pr = soft[(8 + j) % 3][:, 0:3 * NK].rearrange("p (b n) -> p b n", b=3)
                after_exp(n, nb, lambda b: pr[:, b, :])
            attn_out(NT - 1)

            def group_norm(m):
                dve.wait_ge(s["ssq_ps"], NT + m)
                ts(stat[:, 1 + m, :], pp[3][:, 1, NT * m:NT * m + NT], 1.0 / W, EPS, ALU.mult, ALU.add)\
                    .then_inc(s["rs_done"], 1)
                dve.wait_ge(s["rs_act"], m + 1)
                step(dve.reciprocal(stat[:, 1 + m, :], stat[:, 1 + m, :]))

            group_norm(0)
            def weigh(n):
                dve.wait_ge(s["mixsq_done"], n + 1)
                ts(mix_t[:, n, :], mix_t[:, n, :], g_ssm[:, n:n + 1], None, ALU.mult).then_inc(s["weighed"], 1)

            for n in range(GB):
                dve.wait_ge(s["sig_done"], n + 1)
                tt(mix_t[:, n, :].rearrange("p (n t) -> p t n", t=T), y_g[:, n, :].rearrange("p (t n) -> p t n", t=T),
                   mix_sq[:, n, :].rearrange("p (t n) -> p t n", t=T), ALU.mult).then_inc(s["mix_done"], 1)
                if n >= 1:
                    weigh(n - 1)
            weigh(GB - 1)
            def ffn_norm(i):
                dve.wait_ge(s["ffn_sq"], i + 1)
                ts(stat[:, 4, i:i + 1], stat[:, 3, i:i + 1], 1.0 / D, EPS, ALU.mult, ALU.add).then_inc(s["ffn_ms"], 1)
                dve.wait_ge(s["ffn_sqrt"], i + 1)
                step(dve.reciprocal(stat[:, 4, i:i + 1], stat[:, 4, i:i + 1]))
                if i >= 2:
                    dve.wait_ge(s["parts_done"], i - 1)
                stt(ffn_in[i % 2], resid[:, i, :], stat[:, 4, i:i + 1], g_ffn[:], ALU.mult, ALU.mult)\
                    .then_inc(s["ffn_done"], 1)

            dve.wait_ge(s["in_resid"], 16)
            dve.wait_ge(s["in_rows"], 48)
            for t in range(2 * NT):
                i, m = t % NT, t // NT
                if t == 1:
                    group_norm(1)
                dve.wait_ge(s["op_ps"], t + 1)
                stt(resid[:, i, :], pp[OP_PAIR[t]][:].rearrange("p b n -> p (b n)"), stat[:, 1 + m, i:i + 1],
                    resid[:, i, :], ALU.mult, ALU.add).then_inc(s["op_out"], 1)
                if m == 1:
                    dve.wait_ge(s["op_out"], t + 1)
                    ffn_norm(i)
            dve.wait_ge(s["lg_ps"], NT)
            lg = pp[3][:, 0, 0:NT * NR].rearrange("p (i n) -> p i n", i=NT)
            step(tt(logit, lg, b_r[:].unsqueeze(1).to_broadcast([P, NT, NR]), ALU.add))

            bc = lambda x, n: x.unsqueeze(2).to_broadcast([P, NT, n])
            dve.memset(tiles_before[:, 0], 0.0)
            step(dve.tensor_copy(pad8[:, :, 0:NEG_G], logit[:, :, 0:NEG_G]))
            for i in range(NT):
                ins = dve.max(top_g[:, i, :], pad8[:, i, :])
            step(ins)
            for i in range(NT):
                ins = dve.max_index(ig[:, i, :], top_g[:, i, :], pad8[:, i, :])
            ins.then_inc(s["lg_out"], 1)
            dve.wait_ge(s["lg_out"], 1)
            tt(le_m[:, :, 0:NEG_G], logit[:, :, 0:NEG_G], bc(top_g[:, :, 0], NEG_G), ALU.subtract)\
                .then_inc(s["lg_out"], 1)
            step(dve.tensor_copy(rt[:, 0, :], ig[:, :, 0]))
            step(tt(one_g, iota_e[:, 0:NEG_G].unsqueeze(1).to_broadcast([P, NT, NEG_G]), bc(rt[:, 0, :], NEG_G),
                    ALU.is_equal))
            dve.wait_ge(s["route_act"], 1)
            step(dve.tensor_reduce(rt[:, 1, :], le_m[:, :, 0:NEG_G], AX.X, ALU.add))
            step(tt(le_m.rearrange("p i (g e) -> p i g e", g=NEG_G),
                    logit[:, :, NEG_G:NR].rearrange("p i (g e) -> p i g e", g=NEG_G),
                    one_g.unsqueeze(3).to_broadcast([P, NT, NEG_G, EPG]), ALU.mult))
            step(dve.tensor_reduce(le_g, le_m.rearrange("p i (g e) -> p i e g", g=NEG_G), AX.X, ALU.add))
            for i in range(NT):
                ins = dve.max(top_e[:, i, :], le_g[:, i, :])
            step(ins)
            for i in range(NT):
                ins = dve.max_index(ie[:, i, :], top_e[:, i, :], le_g[:, i, :])
            step(ins)
            tt(rt[:, 4, :], top_e[:, :, 1], top_e[:, :, 0], ALU.subtract).then_inc(s["lg_out"], 1)
            chosen = rt[:, 2:4, :]
            step(dve.tensor_copy(chosen, ie[:, :, 0:2].rearrange("p i k -> p k i")))
            step(stt(chosen, rt[:, 0, :].unsqueeze(1).to_broadcast([P, 2, NT]), float(EPG), chosen, ALU.mult, ALU.add))
            step(tt(pair.rearrange("p k i e -> p (k i) e"), iota_e[:].unsqueeze(1).to_broadcast([P, 2 * NT, NE]),
                    chosen.rearrange("p k i -> p (k i)").unsqueeze(2).to_broadcast([P, 2 * NT, NE]), ALU.is_equal))
            step(tt(both, pair[:, 0], pair[:, 1], ALU.add))
            for i in range(NT):
                ins = tt(tiles_before[:, i + 1], tiles_before[:, i], both[:, i], ALU.add)
                if i < NT - 1:
                    step(ins)
            ins.then_inc(s["pair_done"], 1)
            dve.wait_ge(s["place_ps"], 1)
            pl = pp[3][:, 1, 0:NT * NE].rearrange("p (i e) -> p i e", i=NT)
            step(stt(place, pl, 1.0, both, ALU.add, ALU.mult))
            step(ts(place_e.rearrange("p e i -> p i e"), place, -1.0, None, ALU.add))

            def selection(place_of):
                for i in range(NT):
                    ins = ts(sel[:, i, :], iota_t[:], place_of[:, i:i + 1], None, ALU.is_equal)
                ins.then_inc(s["sel_ready"], 1)

            selection(place_e[:, 0, :])
            step(ts(ntile[:, 0, :], pp[3][:, 1, NT * NE:NT * NE + NE], 1.0 / TT, (TT - 1) / (2.0 * TT),
                    ALU.mult, ALU.add))
            step(ts(ntile[:, 0, :], ntile[:, 0, :], MAGIC, None, ALU.add))
            step(ts(ntile[:, 0, :], ntile[:, 0, :], -MAGIC, 1.0, ALU.add, ALU.max))
            step(dve.memset(first_f[:, 0:1], 0.0))
            step(dve.tensor_tensor_scan(first_f[:, 1:NE + 1], ones[:, 0:NE], ntile[:, 0, :], 0.0, ALU.mult, ALU.add))
            dve.tensor_copy(first_i[:], first_f[0:1, :]).then_inc(s["pos_done"], 1)
            dve.wait_ge(s["pos_done"], 1)

            gu, gx, xtp = pp[0][:, 0, :], pp[2][:, 0, :], pp[2][:, 1, :]

            def keep_x(w1):
                dve.wait_ge(s["gx_ready"], w1 + 1)
                dve.tensor_copy(xrow, gx).then_inc(s["gx_copied"], 1)

            def keep_xt(w1):
                dve.wait_ge(s["xt_ready"], w1)
                dve.tensor_copy(xt_e, xtp.rearrange("p (c n) -> p c n", c=4)).then_inc(s["xt_copied"], 1)

            def select(w1):
                dve.wait_ge(s["place_ready"], w1)
                dve.wait_ge(s["gx_ready"], w1)
                selection(place_c)

            dve.sem_inc(s["gx_ready"], 1)
            step(ts(ntile[:, 1, :], first_f[:, 0:NE], float(TT), None, ALU.mult))
            step(tt(place, pl, ntile[:, 1, :].unsqueeze(1).to_broadcast([P, NT, NE]), ALU.add))
            step(tt(ptmp, pair, place.unsqueeze(1).to_broadcast([P, 2, NT, NE]), ALU.mult))
            step(dve.tensor_reduce(rt[:, 8:10, :], ptmp, AX.X, ALU.add))
            step(dve.tensor_copy(pos_u[:], rt[:, 8:10, :]))
            dve.sem_inc(s["pairs_used"], 1)
            keep_x(1)
            keep_xt(1)
            dve.wait_ge(s["route_act"], 2)
            step(ts(rt[:, 5, :], rt[:, 4, :], 1.0, None, ALU.add))
            step(tt(rt[:, 5, :], rt[:, 5, :], rt[:, 1, :], ALU.mult))
            step(dve.reciprocal(rt[:, 6, :], rt[:, 5, :]))
            step(tt(rt[:, 7, :], rt[:, 6, :], rt[:, 4, :], ALU.mult))
            with dve.Fori(0, NE) as e:
                first, end = tiles_of(dve, e)
                with dve.Fori(first, end) as w:
                    select(w + 2)
                    dve.wait_ge(s["sg_ready"], w + 1)
                    tt(hid, gu[TT:P], act_g, ALU.mult).then_inc(s["h_ready"], 1)
                    keep_x(w + 2)
                    keep_xt(w + 2)

            def add_rows(i):
                dve.wait_ge(got_in[i], 32)
                for k in range(2):
                    ins = stt(resid[:, i, :], got[i][k], rt[:, 6 + k, i:i + 1], resid[:, i, :], ALU.mult, ALU.add)
                    if k == 0:
                        step(ins)
                ins.then_inc(s["fin_sq"], 1)

            def mean_square(i):
                dve.wait_ge(s["fin_ss"], i + 1)
                ts(stat[:, 6, i:i + 1], stat[:, 5, i:i + 1], 1.0 / D, EPS, ALU.mult, ALU.add).then_inc(s["fin_ms"], 1)

            def final_norm(i):
                dve.wait_ge(s["fin_sqrt"], i + 1)
                step(dve.reciprocal(stat[:, 6, i:i + 1], stat[:, 6, i:i + 1]))
                stt(fin[i], resid[:, i, :], stat[:, 6, i:i + 1], g_fin[:], ALU.mult, ALU.mult)\
                    .then_inc(s["fin_done"], 1)

            dve.wait_ge(s["resid_back"], 16)
            for i in range(NT):
                add_rows(i)
                if i >= 1:
                    final_norm(i - 1)
                mean_square(i)
            final_norm(NT - 1)


def _layout(x):
    c = np.ascontiguousarray
    pairs = lambda v: v.reshape(R, 2, NS, *v.shape[2:]).transpose(1, 2, 0, *range(3, v.ndim + 1)).reshape(
        P, R, *v.shape[2:])
    rows = np.concatenate([x["x_prompt"].reshape(SEQ, D), x["x_sample"].reshape(NB * LS, D)], 0)
    w_in = x["w_in"][0]
    q = w_in[:, 0:W].reshape(D, NKV, QPK, HD).transpose(0, 2, 1, 3).reshape(D, W)
    w_out = x["w_out"][0]
    ssm_o = w_out[W:].reshape(GB, P, D).transpose(1, 0, 2)
    att_o = w_out[0:W].reshape(NKV, QPK, HD, D).transpose(0, 2, 1, 3).reshape(P, QPK, D)
    ck = x["cache_k"][0]
    return {
        "x_rows": c(rows),
        "x_t": c(rows.T.reshape(P, KD, TOK)),
        "w_in_u": c(w_in[:, W + 2 * P:]),
        "w_in_qkv": c(np.concatenate([q, w_in[:, W:W + 2 * P]], 1)),
        "w_out": c(np.concatenate([att_o, ssm_o], 1)),
        "w_glu": c(x["w_glu"][0]),
        "cache_k_t": c(ck.transpose(2, 3, 0, 1).reshape(P, NB, WIN)),
        "cache_k": c(ck.reshape(NB, WIN, P)),
        "cache_v": c(x["cache_v"][0].reshape(NB, WIN, P)),
        "cols": c(np.concatenate(
            [x["g_norm_mix"][0].reshape(P, KD),
             x["g_attn_out"][0].reshape(NKV, QPK, HD).transpose(0, 2, 1).reshape(P, QPK),
             x["g_ssm_out"][0].reshape(GB, P).T, x["b_glu"][0].reshape(GB, P).T,
             np.repeat(x["attn_sinks"][0], LS)[:, None]], 1)),
        "g_norm_ffn": c(x["g_norm_ffn"]),
        "g_final": c(x["g_final"][None]),
        "sinks": c(x["attn_sinks"]),
        "ssm_d": c(x["ssm_d"][0].reshape(G, GC).T),
        "w_router": c(np.concatenate([x["w_router_group"][0], x["w_router_expert"][0]], 1)),
        "b_router": c(np.concatenate([x["b_router_group"], x["b_router_expert"]], 1)),
        "tables": c(np.concatenate(
            [pairs(x[n][0]).reshape(P, -1) for n in ("ssm_a_re", "ssm_a_im", "ssm_b_re", "ssm_b_im")]
            + [pairs(x[n][0].transpose(0, 2, 1)).reshape(P, -1) for n in ("ssm_c_re", "ssm_c_im")]
            + [pairs(x[n][0].transpose(1, 2, 0)).reshape(P, -1) for n in ("state_ssm_re", "state_ssm_im")], 1)),
        "log_dt": c(x["ssm_log_dt"][0].reshape(R, 2).T),
        "w_exp_gate": c(x["w_exp_gate"][0]),
        "w_exp_up": c(x["w_exp_up"][0]),
        "w_exp_down": c(x["w_exp_down"][0]),
    }


_OUTS = {
    "y": (TOK, D), "new_k_prompt": (WIN, P), "new_v_prompt": (WIN, P),
    "new_k_sample": (NB, WIN, P), "new_v_sample": (NB, WIN, P),
    "state_prompt": (P, 2, R), "state_sample": (P, 2, R, NB),
}


def kernel(**inputs):
    import concourse.bacc as _bacc
    from concourse.bass_utils import run_bass_kernel_spmd as _run

    arrays = _layout({k: np.asarray(v) for k, v in inputs.items()})
    nc = _bacc.Bacc("TRN2", target_bir_lowering=False, num_devices=1)
    a = {n: nc.dram_tensor(f"in_{n}", v.shape, mybir.dt.from_np(v.dtype), kind="ExternalInput").ap()
         for n, v in arrays.items()}
    o = {n: nc.dram_tensor(f"out_{n}", shape, F32, kind="ExternalOutput").ap() for n, shape in _OUTS.items()}
    build(nc, a, o)
    got = _run(nc, [{f"in_{n}": v for n, v in arrays.items()}], core_ids=[0]).results[0]
    got = {n: got[f"out_{n}"] for n in _OUTS}
    y = got["y"]
    states = lambda v, i: np.ascontiguousarray(v[:, i].reshape(2, NS, R, -1).transpose(3, 2, 0, 1)).reshape(
        1, -1, G, NS)
    heads = lambda v: v.reshape(1, -1, WIN, NKV, HD)
    return (y[0:SEQ].reshape(1, SEQ, D), y[SEQ:].reshape(NB, LS, D),
            heads(got["new_k_prompt"]), heads(got["new_v_prompt"]),
            states(got["state_prompt"], 0), states(got["state_prompt"], 1),
            heads(got["new_k_sample"]), heads(got["new_v_sample"]),
            states(got["state_sample"], 0), states(got["state_sample"], 1))
```
